# Optimizing a Trainium2 kernel written in Bass

```python
import jax, jax.numpy as jnp
from jax import lax
import numpy as np

D_MODEL = 1024
BATCH = 1
SEQ = 256
DEPTH = 2
DEC_BATCH = 8
DEC_SEQ = 1
PAST_LEN = 2048
PAGE_SIZE = 128

N_AB = (DEPTH + 1) // 2
N_C = DEPTH // 2
D_A = D_MODEL // 2
A_GROUPS = 8
CONV_W = 3
HEAD_B = 64
D_B = D_MODEL // 2
H_B = D_B // HEAD_B
R_DECAY = 64
R_AAA = 64
R_GATE = 128
P_B = 3 * D_B + R_DECAY + R_AAA + R_GATE
P_AB = 3 * D_A + P_B
GN_EPS = 64e-5
D_C = D_MODEL
CHUNK = 128
C_GROUPS = 8
C_GROUP_CH = D_C // C_GROUPS
N_EXPERTS = 64
TOP_K = 8
N_GROUPS = 8
TOPK_GROUPS = 4
EXPERTS_PER_GROUP = N_EXPERTS // N_GROUPS
D_EXPERT = 256
D_SHARED = 256
ROUTE_SCALE = 2.5
EPS = 1e-6

kernel_name = 'hybrid_conv_rwkv7_gmlp_moe_adaln_step'

def rmsnorm(x, g):
    xf = x.astype(jnp.float32)
    y = xf * lax.rsqrt(jnp.mean(xf * xf, axis=-1, keepdims=True) + EPS)
    return (y * g.astype(jnp.float32)).astype(x.dtype)

def layernorm(x, g, b):
    xf = x.astype(jnp.float32)
    mu = jnp.mean(xf, axis=-1, keepdims=True)
    var = jnp.mean(jnp.square(xf - mu), axis=-1, keepdims=True)
    return ((xf - mu) * lax.rsqrt(var + EPS) * g.astype(jnp.float32) + b.astype(jnp.float32)).astype(x.dtype)

def modulation(c, w_mod, b_mod):
    m = jax.nn.silu(c) @ w_mod + b_mod
    return jnp.split(m[:, None, :], 6, axis=-1)

def short_conv_mixer(a_h, a_b, a_c, conv_prev, conv_w):
    L = a_h.shape[1]
    gated = a_c * a_h
    full = jnp.concatenate([conv_prev.astype(gated.dtype), gated], axis=1)
    conv = full[:, 0:L] * conv_w[0]
    for j in range(1, CONV_W):
        conv = conv + full[:, j:j + L] * conv_w[j]
    return a_b * conv, full[:, L:]

def _wkv_step(S, inp):
    r, w, k, v, kk, a = inp
    s_kk = jnp.einsum('bhij,bhj->bhi', S, kk)
    S = S * w[:, :, None, :] - s_kk[..., None] * (kk * a)[:, :, None, :] + v[..., None] * k[:, :, None, :]
    out = jnp.einsum('bhij,bhj->bhi', S, r)
    return S, out

def rwkv7_mixer(pb, shift_prev, wkv_prev, mu, w0, w_decay_up, a0, a_up, g_up, k_k, k_a, r_k, gn_g, gn_b):
    Bn, L, _ = pb.shape
    f32 = jnp.float32
    prev = jnp.concatenate([shift_prev[:, None, :].astype(pb.dtype), pb[:, :-1]], axis=1)
    xm = pb + (prev - pb) * mu
    r, k, v, dw, da, dg = jnp.split(xm, [D_B, 2 * D_B, 3 * D_B, 3 * D_B + R_DECAY, 3 * D_B + R_DECAY + R_AAA], axis=-1)
    w_log = -jax.nn.softplus(-(w0 + jnp.tanh(dw) @ w_decay_up).astype(f32)) - 0.5
    decay = jnp.exp(-jnp.exp(w_log))
    a = jax.nn.sigmoid((a0 + da @ a_up).astype(f32))
    g = jax.nn.sigmoid(dg) @ g_up
    heads = lambda t: t.astype(f32).reshape(Bn, L, H_B, HEAD_B)
    r_h, k_h, v_h, a_h, w_h = heads(r), heads(k), heads(v), heads(a), heads(decay)
    kk = k_h * k_k.astype(f32).reshape(H_B, HEAD_B)
    kk = kk / jnp.maximum(jnp.sqrt(jnp.sum(kk * kk, axis=-1, keepdims=True)), 1e-12)
    k_h = k_h * (1.0 + (a_h - 1.0) * k_a.astype(f32).reshape(H_B, HEAD_B))
    tm = lambda t: jnp.swapaxes(t, 0, 1)
    S_final, out = lax.scan(_wkv_step, wkv_prev.astype(f32), (tm(r_h), tm(w_h), tm(k_h), tm(v_h), tm(kk), tm(a_h)))
    out = jnp.swapaxes(out, 0, 1)
    mean = jnp.mean(out, axis=-1, keepdims=True)
    var = jnp.mean(jnp.square(out - mean), axis=-1, keepdims=True)
    out = (out - mean) * lax.rsqrt(var + GN_EPS) * gn_g.astype(f32).reshape(H_B, HEAD_B) + gn_b.astype(f32).reshape(H_B, HEAD_B)
    out = out + jnp.sum(r_h * k_h * r_k.astype(f32), axis=-1, keepdims=True) * v_h
    y = out.reshape(Bn, L, D_B).astype(pb.dtype) * g
    return y, pb[:, -1], S_final

def mixer_ab(h, conv_prev, shift_prev, wkv_prev, w, i):
    proj = h @ w['ab_w_in'][i]
    a_h, a_b, a_c, pb = jnp.split(proj, [D_A, 2 * D_A, 3 * D_A], axis=-1)
    y_a, new_conv = short_conv_mixer(a_h, a_b, a_c, conv_prev, w['ab_conv_w'][i])
    y_b, new_shift, new_wkv = rwkv7_mixer(pb, shift_prev, wkv_prev, w['ab_mu'][i], w['ab_w0'][i], w['ab_w_decay_up'][i],
                                          w['ab_a0'][i], w['ab_a_up'][i], w['ab_g_up'][i], w['ab_k_k'][i], w['ab_k_a'][i],
                                          w['ab_r_k'][i], w['ab_gn_g'][i], w['ab_gn_b'][i])
    y = jnp.concatenate([y_a, y_b], axis=-1) @ w['ab_w_out'][i]
    return y, new_conv, new_shift, new_wkv

def gmlp_mixer(h, w_in, b_in, ln_g, ln_b, w_s, b_s, w_out):
    Bn, L, _ = h.shape
    z = jax.nn.gelu(h @ w_in + b_in)
    u, v = jnp.split(z, 2, axis=-1)
    v = layernorm(v, ln_g, ln_b)
    n_chunks = -(-L // CHUNK)
    vp = jnp.pad(v, ((0, 0), (0, n_chunks * CHUNK - L), (0, 0))).reshape(Bn, n_chunks, CHUNK, C_GROUPS, C_GROUP_CH)
    mask = jnp.tril(jnp.ones((CHUNK, CHUNK), dtype=bool))
    ws = jnp.where(mask[None], w_s, jnp.zeros_like(w_s)).astype(v.dtype)
    s = jnp.einsum('gij,bnjgc->bnigc', ws, vp) + jnp.transpose(b_s)[:, :, None].astype(v.dtype)
    s = s.reshape(Bn, n_chunks * CHUNK, D_C)[:, :L]
    return (u * s) @ w_out, v

def moe(h, w_router, b_router, w_gate, w_up, w_down, ws_gate, ws_up, ws_down):
    Bn, L, D = h.shape
    x = h.reshape(-1, D)
    T = x.shape[0]
    scores = jax.nn.sigmoid((x @ w_router).astype(jnp.float32))
    sel = scores + b_router.astype(jnp.float32)
    grp_score = jnp.sum(lax.top_k(sel.reshape(T, N_GROUPS, EXPERTS_PER_GROUP), 2)[0], axis=-1)
    _, gidx = lax.top_k(grp_score, TOPK_GROUPS)
    gmask = jnp.any(gidx[:, :, None] == jnp.arange(N_GROUPS)[None, None, :], axis=1)
    emask = jnp.repeat(gmask, EXPERTS_PER_GROUP, axis=1)
    _, eidx = lax.top_k(jnp.where(emask, sel, -jnp.inf), TOP_K)
    wts = jnp.take_along_axis(scores, eidx, axis=1)
    wts = wts / jnp.sum(wts, axis=-1, keepdims=True) * ROUTE_SCALE
    combine = jnp.zeros((T, N_EXPERTS), jnp.float32).at[jnp.arange(T)[:, None], eidx].set(wts).astype(x.dtype)
    routed = jnp.zeros_like(x)
    for gi in range(N_GROUPS):
        sl = slice(gi * EXPERTS_PER_GROUP, (gi + 1) * EXPERTS_PER_GROUP)
        hg = jnp.einsum('td,edf->tef', x, w_gate[sl])
        hu = jnp.einsum('td,edf->tef', x, w_up[sl])
        hw = jax.nn.silu(hg) * hu * combine[:, sl, None]
        routed = routed + jnp.einsum('tef,efd->td', hw, w_down[sl])
    shared = (jax.nn.silu(x @ ws_gate) * (x @ ws_up)) @ ws_down
    return (routed + shared).reshape(Bn, L, D)

def trunk(x, c, conv_st, shift_st, wkv_st, w):
    new_conv, new_shift, new_wkv, chunk_v = [], [], [], []
    for layer in range(DEPTH):
        sh1, sc1, g1, sh2, sc2, g2 = modulation(c, w['w_mod'][layer], w['b_mod'][layer])
        ng = w['norm_g'][layer]
        h = rmsnorm(x, ng[0]) * (1.0 + sc1) + sh1
        if layer % 2 == 0:
            i = layer // 2
            y, nc, ns, nw = mixer_ab(h, conv_st[i], shift_st[i], wkv_st[i], w, i)
            new_conv.append(nc)
            new_shift.append(ns)
            new_wkv.append(nw)
        else:
            j = layer // 2
            y, v = gmlp_mixer(h, w['gm_w_in'][j], w['gm_b_in'][j], w['gm_ln_g'][j], w['gm_ln_b'][j],
                              w['gm_w_s'][j], w['gm_b_s'][j], w['gm_w_out'][j])
            chunk_v.append(v)
        x = x + g1 * rmsnorm(y, ng[1])
        h = rmsnorm(x, ng[2]) * (1.0 + sc2) + sh2
        f = moe(h, w['moe_w_router'][layer], w['moe_b_router'][layer], w['moe_w_gate'][layer], w['moe_w_up'][layer],
                w['moe_w_down'][layer], w['moe_ws_gate'][layer], w['moe_ws_up'][layer], w['moe_ws_down'][layer])
        x = x + g2 * rmsnorm(f, ng[3])
    return x, jnp.stack(new_conv), jnp.stack(new_shift), jnp.stack(new_wkv), jnp.stack(chunk_v)

def setup_inputs(seed: int = 0) -> dict:
    key = jax.random.key(seed)
    ks = iter(jax.random.split(key, 64))
    f32 = jnp.float32

    def nrm(shape, scale):
        return jax.random.normal(next(ks), shape, f32) * scale

    D = D_MODEL
    return {
        'x_prompt': nrm((BATCH, SEQ, D), 1.0),
        'x_sample': nrm((DEC_BATCH, DEC_SEQ, D), 1.0),
        'c_prompt': nrm((BATCH, D), 1.0),
        'c_sample': nrm((DEC_BATCH, D), 1.0),
        'state_conv': nrm((N_AB, DEC_BATCH, CONV_W - 1, D_A), 1.0),
        'state_shift': nrm((N_AB, DEC_BATCH, P_B), 1.0),
        'state_wkv': nrm((N_AB, DEC_BATCH, H_B, HEAD_B, HEAD_B), 0.5),
        'w_mod': nrm((DEPTH, D, 6 * D), 0.3 * D ** -0.5),
        'b_mod': nrm((DEPTH, 6 * D), 0.02),
        'norm_g': 1.0 + nrm((DEPTH, 4, D), 0.05),
        'ab_w_in': nrm((N_AB, D, P_AB), D ** -0.5),
        'ab_conv_w': nrm((N_AB, CONV_W, D_A), CONV_W ** -0.5),
        'ab_mu': jax.random.uniform(next(ks), (N_AB, P_B), f32),
        'ab_w0': nrm((N_AB, D_B), 0.5),
        'ab_w_decay_up': nrm((N_AB, R_DECAY, D_B), 0.3 * R_DECAY ** -0.5),
        'ab_a0': nrm((N_AB, D_B), 0.1),
        'ab_a_up': nrm((N_AB, R_AAA, D_B), 0.3 * R_AAA ** -0.5),
        'ab_g_up': nrm((N_AB, R_GATE, D_B), R_GATE ** -0.5),
        'ab_k_k': 0.85 + nrm((N_AB, D_B), 0.05),
        'ab_k_a': 1.0 + nrm((N_AB, D_B), 0.05),
        'ab_r_k': nrm((N_AB, H_B, HEAD_B), 0.1),
        'ab_gn_g': 1.0 + nrm((N_AB, D_B), 0.05),
        'ab_gn_b': nrm((N_AB, D_B), 0.02),
        'ab_w_out': nrm((N_AB, D_A + D_B, D), (D_A + D_B) ** -0.5),
        'gm_w_in': nrm((N_C, D, 2 * D_C), D ** -0.5),
        'gm_b_in': nrm((N_C, 2 * D_C), 0.02),
        'gm_ln_g': 1.0 + nrm((N_C, D_C), 0.05),
        'gm_ln_b': nrm((N_C, D_C), 0.02),
        'gm_w_s': nrm((N_C, C_GROUPS, CHUNK, CHUNK), 0.5 * CHUNK ** -0.5),
        'gm_b_s': 1.0 + nrm((N_C, C_GROUPS, CHUNK), 0.1),
        'gm_w_out': nrm((N_C, D_C, D), D_C ** -0.5),
        'moe_w_router': nrm((DEPTH, D, N_EXPERTS), D ** -0.5),
        'moe_b_router': nrm((DEPTH, N_EXPERTS), 0.01),
        'moe_w_gate': nrm((DEPTH, N_EXPERTS, D, D_EXPERT), D ** -0.5),
        'moe_w_up': nrm((DEPTH, N_EXPERTS, D, D_EXPERT), D ** -0.5),
        'moe_w_down': nrm((DEPTH, N_EXPERTS, D_EXPERT, D), D_EXPERT ** -0.5),
        'moe_ws_gate': nrm((DEPTH, D, D_SHARED), D ** -0.5),
        'moe_ws_up': nrm((DEPTH, D, D_SHARED), D ** -0.5),
        'moe_ws_down': nrm((DEPTH, D_SHARED, D), D_SHARED ** -0.5),
    }

def reference(x_prompt, x_sample, c_prompt, c_sample, state_conv, state_shift, state_wkv,
              w_mod, b_mod, norm_g, ab_w_in, ab_conv_w, ab_mu, ab_w0, ab_w_decay_up, ab_a0, ab_a_up, ab_g_up,
              ab_k_k, ab_k_a, ab_r_k, ab_gn_g, ab_gn_b, ab_w_out, gm_w_in, gm_b_in, gm_ln_g, gm_ln_b, gm_w_s,
              gm_b_s, gm_w_out, moe_w_router, moe_b_router, moe_w_gate, moe_w_up, moe_w_down, moe_ws_gate,
              moe_ws_up, moe_ws_down):
    w = dict(w_mod=w_mod, b_mod=b_mod, norm_g=norm_g, ab_w_in=ab_w_in, ab_conv_w=ab_conv_w, ab_mu=ab_mu,
             ab_w0=ab_w0, ab_w_decay_up=ab_w_decay_up, ab_a0=ab_a0, ab_a_up=ab_a_up, ab_g_up=ab_g_up,
             ab_k_k=ab_k_k, ab_k_a=ab_k_a, ab_r_k=ab_r_k, ab_gn_g=ab_gn_g, ab_gn_b=ab_gn_b, ab_w_out=ab_w_out,
             gm_w_in=gm_w_in, gm_b_in=gm_b_in, gm_ln_g=gm_ln_g, gm_ln_b=gm_ln_b, gm_w_s=gm_w_s, gm_b_s=gm_b_s,
             gm_w_out=gm_w_out, moe_w_router=moe_w_router, moe_b_router=moe_b_router, moe_w_gate=moe_w_gate,
             moe_w_up=moe_w_up, moe_w_down=moe_w_down, moe_ws_gate=moe_ws_gate, moe_ws_up=moe_ws_up,
             moe_ws_down=moe_ws_down)
    zc = jnp.zeros((N_AB, x_prompt.shape[0], CONV_W - 1, D_A), x_prompt.dtype)
    zs = jnp.zeros((N_AB, x_prompt.shape[0], P_B), x_prompt.dtype)
    zw = jnp.zeros((N_AB, x_prompt.shape[0], H_B, HEAD_B, HEAD_B), jnp.float32)
    y_prompt, conv_p, shift_p, wkv_p, _ = trunk(x_prompt, c_prompt, zc, zs, zw, w)
    y_sample, conv_s, shift_s, wkv_s, chunk_v_s = trunk(x_sample, c_sample, state_conv, state_shift, state_wkv, w)
    return (y_prompt, y_sample, conv_p, conv_s, shift_p, shift_s, wkv_p, wkv_s, chunk_v_s)


_drawn_inputs = setup_inputs


def setup_inputs(seed=0):
    import zlib

    import numpy as np

    out = dict(_drawn_inputs(seed))
    spreads = {}
    factors = {'ab_k_k': 84.534, 'ab_gn_b': 17.651, 'gm_ln_b': 3.122, 'gm_b_s': 2.682, 'ab_gn_g': 4.207}
    for name, (base, spread) in spreads.items():
        noise = np.random.default_rng([zlib.crc32(name.encode()), seed]).standard_normal(out[name].shape)
        drawn = base * np.exp(spread * noise) if base else spread * noise
        out[name] = __import__('jax').numpy.asarray(drawn.astype(out[name].dtype))
    for name, factor in factors.items():
        out[name] = (out[name] * factor).astype(out[name].dtype)
    return out
```

```python
from contextlib import ExitStack

import numpy as np

import concourse.bass as bass
from concourse import mybir

F32 = mybir.dt.float32
ALU = mybir.AluOpType
ACT = mybir.ActivationFunctionType
AX = mybir.AxisListType

P = 128
D = 1024
DT = D // P
NPR, NSA = 256, 8
T = NPR + NSA
NSEQ = 1 + NSA
DA = DB = 512
H, HD = 8, 64
QT = DB // P
PB = 3 * DB + 256
PBT = PB // P
PROJ = 3 * DA + PB
PROJT = PROJ // P
CH = 64
NCH = NPR // CH
NE, DE = 64, 256
TOPK, NG, TOPG = 8, 8, 4
TR = T // 3
EPS, GN_EPS = 1e-6, 64e-5
ROUTE_SCALE = 2.5
BIG = 1e30
EMH = float(np.exp(-0.5))
GELU_C = float(np.sqrt(2.0 / np.pi))

NSMALL = 22
UNIT = 2048
MSLOTS = 5
ESLOTS = 12
CAP = 64
MAXR = -(-T // CAP)
MOD_FIRST = 4
MOD_PROJ = [[MOD_FIRST + u] for u in range(13)]
MOD_LATE = MOD_FIRST + sum(len(x) for x in MOD_PROJ)
NPAIR = NE // 2
EBODY = 4
NTURN = NPAIR // EBODY
PU = 6
RU = NPAIR * PU

C_ID, C_ONE, C_BLK, C_UPS, C_UPI, C_LOS, C_LV0T, C_LV, C_S4 = 0, 128, 256, 384, 512, 640, 768, 896, 896 + 6 * 128
C_TRI = C_S4 + NSEQ
C_IOTA = C_TRI + 64
C_TOK = C_IOTA + T
C_UPT = C_TOK + 3
C_UPF = C_UPT + P
NCONST = C_UPF + P


def shape_constants():
    c = np.zeros((P, NCONST), np.float32)
    i = np.arange(P)
    same = (i[:, None] // CH) == (i[None, :] // CH)
    c[:, C_ID:C_ID + P] = np.eye(P)
    c[:, C_ONE:C_ONE + P] = 1.0
    c[:, C_BLK:C_BLK + P] = same
    c[:, C_UPS:C_UPS + P] = same & (i[:, None] < i[None, :])
    c[:, C_UPI:C_UPI + P] = same & (i[:, None] <= i[None, :])
    c[:, C_LOS:C_LOS + P] = same & (i[:, None] > i[None, :])
    for k in range(6):
        b = 1 << k
        m = ((i[:, None] // (2 * b)) == (i[None, :] // (2 * b))) & (i[:, None] // b % 2 == 0) & (i[None, :] // b % 2 == 1)
        c[:, C_LV + k * P:C_LV + (k + 1) * P] = m
        if k == 0:
            c[:, C_LV0T:C_LV0T + P] = m.T
    for j in range(4):
        for s in range(NSEQ):
            c[32 * j + s, C_S4 + s] = 1.0
    g = np.arange(8)
    c[:, C_TRI:C_TRI + 64] = (g[None, :] < g[:, None]).reshape(1, 64)
    c[:, C_IOTA:C_IOTA + T] = np.arange(T)
    c[:, C_TOK:C_TOK + 3] = i[:, None] + TR * np.arange(3)[None, :]
    c[:, C_UPF:C_UPF + P] = i[:, None] <= i[None, :]
    c[:, C_UPT:C_UPT + P] = i[:, None] < i[None, :]
    return c


def build(nc, ins, outs):
    (x_prompt, x_sample, c_prompt, c_sample, state_conv, state_shift, state_wkv, w_mod, b_mod, norm_g,
     ab_w_in, ab_conv_w, ab_mu, ab_w0, ab_w_decay_up, ab_a0, ab_a_up, ab_g_up, ab_k_k, ab_k_a, ab_r_k,
     ab_gn_g, ab_gn_b, ab_w_out, gm_w_in, gm_b_in, gm_ln_g, gm_ln_b, gm_w_s, gm_b_s, gm_w_out,
     moe_w_router, moe_b_router, moe_w_gate, moe_w_up, moe_w_down, moe_ws_gate, moe_ws_up, moe_ws_down,
     constants) = ins
    (y_prompt, y_sample, conv_p, conv_s, shift_p, shift_s, wkv_p, wkv_s, chunk_v_s) = outs
    vec_scratch = nc.dram_tensor("vec_scratch", (NSA, 6, DB), F32).ap()
    out_scratch = nc.dram_tensor("out_scratch", (NSA * H, HD), F32).ap()

    with ExitStack() as ctx:
        def sb(name, shape):
            return ctx.enter_context(nc.sbuf_tensor(name, shape, F32))

        def sem(name):
            return ctx.enter_context(nc.semaphore(name))

        ring = sb("ring", [P, ESLOTS, UNIT])
        arena = sb("arena", [P, 17600])
        xT = sb("xT", [P, DT, T])
        hT = sb("hT", [P, DT, T])
        K = sb("K", [P, NCONST])
        mod = sb("mod", [P, 2, 6, DT, NSEQ])
        b_modT = sb("b_modT", [P, 2, 6, DT])
        ngT = sb("ngT", [P, 2, 4, DT])
        lora = sb("lora", [P, DB])
        gup = sb("gup", [P, DB])
        router = sb("router", [P, 2, DT, NE])
        brout = sb("brout", [TR, 2, NE])
        vecs = sb("vecs", [P, 64])
        gvec = sb("gvec", [P, 16 + 8 + 8 + 8])
        rstd = sb("rstd", [P, T])
        psum = ctx.enter_context(nc.psum_tensor("psum", [P, 8, 512], F32))

        ident = K[:, C_ID:C_ID + P]
        ones = K[:, C_ONE:C_ONE + P]
        blk = K[:, C_BLK:C_BLK + P]
        conv_w, mu = vecs[:, 0:12].rearrange("p (w q) -> p w q", w=3), vecs[:, 12:26]
        w0, a0, k_k, k_a = vecs[:, 26:30], vecs[:, 30:34], vecs[:, 34:38], vecs[:, 38:42]
        r_k, gn_g, gn_b = vecs[:, 42:46], vecs[:, 46:50], vecs[:, 50:54]
        gb_in, ln_g, ln_b, ws00 = gvec[:, 0:16], gvec[:, 16:24], gvec[:, 24:32], gvec[:, 32:40]

        class Arena:
            def __init__(self, base, size):
                self.base, self.at, self.size = base, 0, size

            def take(self, *shape):
                n = int(np.prod(shape))
                v = self.base[:, self.at:self.at + n]
                self.at += n
                assert self.at <= self.size, self.at
                if len(shape) == 2:
                    v = v.rearrange("p (a b) -> p a b", a=shape[0])
                if len(shape) == 3:
                    v = v.rearrange("p (a b c) -> p a b c", a=shape[0], b=shape[1])
                return v

        st = Arena(arena, 17600)
        xtok = st.take(3, D)
        ctok = st.take(D)
        ctok2 = st.take(D)
        cT = ring[:, 5, 0:DT * 32].rearrange("p (c s) -> p c s", c=DT)
        mrow = ring[:, 5, 512:512 + D]

        m0 = Arena(arena, 17600)
        proj = m0.take(PROJT, T)
        xm = m0.take(PBT, T)
        kh, bb, bonus, tmp = (m0.take(QT, T) for _ in range(4))
        Uz = m0.take(2, 512)
        rhs_s = m0.take(512)
        S0T = m0.take(QT, HD)
        s_tmp = m0.take(16, HD)
        side_mem = sb("side_mem", [P, 16 + 2 * HD + 6 * HD])
        PC = side_mem[:, 0:16].rearrange("p (c q) -> p c q", c=NCH)
        s_u, s_o = side_mem[:, 16:80], side_mem[:, 80:144]
        svec = side_mem[:, 144:528].rearrange("p (v j) -> p v j", v=6)
        a_sig = proj[:, 0:4, :]
        kk = proj[:, 4:8, :]
        g_t = proj[:, 8:12, :]
        pb = proj[:, 12:26, :]
        ld = proj[:, 12:16, :]
        cs = proj[:, 16:20, :]
        px = proj[:, 20:24, :]
        r_, k_, v_ = xm[:, 0:4, :], xm[:, 4:8, :], xm[:, 8:12, :]
        flat = lambda a, b: arena[:, a * T:b * T]
        Lmat = flat(12, 26)[:, 0:3072].rearrange("p (m h t) -> p m h t", m=3, h=H)
        L1, L1T, L2T = Lmat[:, 0], Lmat[:, 1], Lmat[:, 2]
        Rmat = flat(0, 8)[:, 0:2048].rearrange("p (m h t) -> p m h t", m=2, h=H)
        R1T, R2T = Rmat[:, 0], Rmat[:, 1]
        XY = flat(26, 34)[:, 0:2048].rearrange("p (m h t) -> p m h t", m=2, h=H)
        X, Y = XY[:, 0], XY[:, 1]
        Z = flat(34, 38)[:, 0:1024].rearrange("p (h t) -> p h t", h=H)
        conv_t = tmp
        hi = Arena(ring[:, 8:12, :].rearrange("p s n -> p (s n)"), 8192)
        Az, Rz = hi.take(H, NPR), hi.take(H, NPR)
        Vz = hi.take(2, 2, 512)
        Btok, Ktok = hi.take(2, 512), hi.take(2, 512)
        sh_in = ring[0:NSA, 8, 0:PB]
        cv_in = ring[0:NSA, 9, 0:2 * DA].rearrange("p (w n) -> p w n", w=2)
        sh_out = ring[0:NSEQ, 10, 0:PB]
        cv_out = ring[0:10, 11, 0:DA]
        stT = sb("stT", [P, 176])
        st_shift = stT[:, 0:112].rearrange("p (q s) -> p q s", q=PBT)
        st_conv = stT[:, 112:176].rearrange("p (w q s) -> p w q s", w=2, q=QT)
        upi_full = K[:, C_UPF:C_UPF + P]
        wkv_o = flat(34, 38)[:, 0:512].rearrange("p (h j) -> p h j", h=H)
        S_s = ring[0:64, 6:8, :].rearrange("p s (i j) -> p (s i) j", j=HD)
        outT = hT[:, 4:8, :]
        y_a = hT[:, 0:4, :]

        m1 = Arena(arena, 17600)
        z = m1.take(16, T)
        gt1, gt2 = m1.take(8, T), m1.take(8, T)
        vtok = m1.take(2, D)
        wsn = m1.take(8, P)
        wsT = m1.take(8, P)
        bsb = m1.take(8, P)
        vs_out = m1.take(D)
        mu_b = m1.take(T)

        me = Arena(arena, 17600)
        yacc = me.take(DT, T)
        xg = [me.take(DT, P) for _ in range(2)]
        xgT = [me.take(DT, P) for _ in range(2)]
        slotsel = me.take(3, 2, CAP)
        selT = [me.take(T) for _ in range(4)]
        wt = me.take(4)
        idxf = me.take(4)
        gsil, ghid = me.take(DE), me.take(DE)
        ghT = me.take(2, P)
        gout = me.take(D)
        posm = me.take(3, NE + 4)
        comb = me.take(3, NE + 4)
        me_keep = me.at
        htok = me.take(3, D)
        score, sel, selm, rep, mask = (me.take(3, NE) for _ in range(5))
        gt8 = me.take(3, NG, 8)
        grp, rank, gm = me.take(3, NG), me.take(3, NG), me.take(3, NG)
        cmp1, cmp2 = me.take(3, 64), me.take(3, 64)
        top8 = me.take(3, 8)
        csum, cmax, cthr = me.take(3), me.take(1), me.take(4)
        ssil, shid = me.take(2, T), me.take(2, T)
        mx = Arena(arena, 17600)
        mx.take(DT, T)
        xo = mx.take(3, D)

        S = {}

        def signals(*names):
            for n in names:
                S[n] = sem(n)

        signals("const_in", "x_in", "c_in", "small_in", "state_in", "swkv_in", "gmisc_in", "store", "vec", "act", "pool_step", "x_tr", "x_sb", "silu_c", "c_tr", "c_sb", "mod_mm", "mod_row", "mod_tr", "mod_set",
                "sq_ready", "ss_mm", "var_ready", "sd_ready", "h_ready", "proj_mm", "proj_sb", "st_tr",
                "tail_ready", "tail_tr", "tail_sb", "mixed", "lora_in", "lora_mm", "lora_sb", "cs_ready",
                "exp_ready", "kksq_ready", "kkss_mm", "kknorm", "rk_ready", "rk_mm", "pad_ready", "tok_tr", "tok_sb",
                "gram_mm", "gram_sb", "xy0", "z_mm", "z_sb", "d_mm", "xy", "rhs_mm", "rhs_sb", "u_mm", "u_sb",
                "o_mm", "o_sb", "s_mm", "s_sb", "svec_tr", "svec_sb", "svec_out", "svec_in", "samp_out", "samp_in",
                "samp_tr", "samp_sb", "wkv_tr", "wkv_sb", "gn_mm", "gn_c", "gn_v", "gn_sd", "yab_ready",
                "out_mm", "out_sb", "y_done", "rwkv_free", "z_mm1", "z_sb1", "vmu_mm", "vc_ready", "vvar_mm",
                "v_ready", "ln_var", "ln_sd", "ws_tr", "ws_sb", "vt_tr", "vt_sb", "vs_sb", "sg_mm", "sg_ready",
                "logit_mm", "score_ready", "mask_ready", "rank_mm", "htr_mm", "htr_sb", "htok_out",
                "sh_mm", "sh_act", "sh_hid", "shd_mm", "shd_sb", "vs_stored", "gather_go", "fin_tr", "fin_sb")
        signals("round_set", "sel", "slot_mm", "idx", "gat_a", "gat_b", "xt_mm", "xt_sb", "gsil", "ghid",
                "ht_mm", "ht_sb", "os_a", "os_b", "cb_mm", "cb_add", "unit_used", "idxf", "next")
        mload = [sem(f"mload{i}") for i in range(MSLOTS)]
        eload = [sem(f"eload{i}") for i in range(ESLOTS)]
        h_rows = [nc.dram_tensor(f"h_rows{l}", (T, D), F32).ap() for l in range(2)]
        nrounds = ctx.enter_context(nc.sbuf_tensor("nrounds", [P, 2], mybir.dt.int32))
        rounds = sb("rounds", [P, 2])
        slot_idx = ctx.enter_context(nc.sbuf_tensor("slot_idx", [P, 4], mybir.dt.uint32))
        so_tok = tmp[0:NSA].rearrange("p q t -> p (q t)")[:, 0:DB]
        svec_tok = ring[0:NSA, 10:12, :].rearrange("p s n -> p (s n)")[:, 0:6 * DB].rearrange("p (v n) -> p v n", v=6)

        mix_units, mod_unit, proj_unit = [], [], []
        wm = w_mod.rearrange("l (p c) n -> l p c n", c=DT)
        wi = ab_w_in[0].rearrange("(p c) n -> p c n", c=DT)

        def half_units(k):
            for u in (2 * k, 2 * k + 1):
                mod_unit.append(len(mix_units))
                mix_units.append(("mod", wm[u // 24, :, :, u % 24 * 256:(u % 24 + 1) * 256], DT))

        for k in range(MOD_FIRST):
            half_units(k)
        for u in range(PROJT // 2):
            proj_unit.append(len(mix_units))
            mix_units.append(("proj", wi[:, :, u * 256:(u + 1) * 256], DT))
            for k in MOD_PROJ[u]:
                half_units(k)
        for k in range(MOD_LATE, 24):
            half_units(k)
        U_ABO = len(mix_units)
        wo = ab_w_out[0].rearrange("(q p) n -> p q n", p=P)
        for u in range(4):
            mix_units.append(("abo", wo[:, 2 * u:2 * u + 2, :], 2))

        def shared_units(l):
            mix_units.append(("shg", moe_ws_gate[l].rearrange("(p c) f -> p c f", c=DT), DT))
            mix_units.append(("shu", moe_ws_up[l].rearrange("(p c) f -> p c f", c=DT), DT))
            mix_units.append(("shd", moe_ws_down[l].rearrange("(p j) n -> p j n", j=2), 2))

        shared_units(0)
        N0 = len(mix_units)
        gi = gm_w_in[0].rearrange("(p c) n -> p c n", c=DT)
        for u in range(8):
            mix_units.append(("gmi", gi[:, :, u * 256:(u + 1) * 256], DT))
        go = gm_w_out[0].rearrange("(q p) n -> p q n", p=P)
        for u in range(4):
            mix_units.append(("gmo", go[:, 2 * u:2 * u + 2, :], 2))
        shared_units(1)
        N1 = len(mix_units)
        U_GMI, U_GMO = N0, N0 + 8
        U_SH = (N0 - 3, N1 - 3)

        def mix_view(n):
            kind, src, a = mix_units[n]
            return ring[:, n % MSLOTS, :].rearrange("p (a n) -> p a n", a=a)

        def eslot(j):
            return (j + PU) % ESLOTS

        block = ctx.enter_context(nc.Block())

        @block.sync
        def _(sp):
            def load(dst, src, s):
                sp.dma_start(dst, src).then_inc(S[s], 16)

            load(ctok[0:1, :], c_prompt, "c_in")
            load(ctok[1:NSEQ, :], c_sample, "c_in")
            load(K[:, :], constants, "const_in")

            def wait_used(n):
                kind, l = mix_units[n][0], int(n >= N0)
                if kind == "mod":
                    sp.wait_ge(S["mod_mm"], mod_unit.index(n) + 1)
                elif kind == "proj":
                    sp.wait_ge(S["proj_mm"], 2 * (proj_unit.index(n) + 1))
                elif kind == "gmi":
                    sp.wait_ge(S["z_mm1"], 2 * (n - U_GMI + 1))
                elif kind in ("abo", "gmo"):
                    sp.wait_ge(S["out_mm"], 8 * (l + 1))
                elif kind in ("shg", "shu"):
                    sp.wait_ge(S["sh_mm"], 2 * l + (1 if kind == "shg" else 2))
                else:
                    sp.wait_ge(S["shd_mm"], 8 * (l + 1))

            def mix_load(n):
                if n >= MSLOTS:
                    wait_used(n - MSLOTS)
                sp.dma_start(mix_view(n), mix_units[n][1]).then_inc(mload[n % MSLOTS], 16)

            for n in range(2):
                mix_load(n)
            load(xtok[:, 0:2, :], x_prompt[0].rearrange("(t p) d -> p t d", p=P), "x_in")
            load(xtok[0:NSA, 2, :], x_sample[:, 0, :], "x_in")
            for n in range(2, 12):
                mix_load(n)
            load(sh_in, state_shift[0], "state_in")
            load(cv_in, state_conv[0], "state_in")
            load(S_s, state_wkv[0].rearrange("b h i j -> (b h) i j"), "swkv_in")
            for n in range(12, N0):
                mix_load(n)

            def expert_load(l, pair2, j):
                sp.dma_start(ring[:, eslot(j), :], expert_src(l, pair2 + (j // PU * 2 + j % 2), j % PU // 2)).then_inc(eload[eslot(j)], 16)

            def first_pair(l):
                for j in range(PU):
                    expert_load(l, 0, j)

            def experts(l, last):
                if l == 0:
                    sp.wait_ge(S["rwkv_free"], 1)
                    sp.wait_ge(S["wkv_sb"], 1)
                    first_pair(0)
                for n, j in sorted((last - 1 - ((last - 1 - j) % MSLOTS), j) for j in range(MSLOTS)):
                    wait_used(n)
                    expert_load(l, 0, PU + j)
                expert_load(l, 0, PU + MSLOTS)
                sp.wait_ge(S["round_set"], l + 1)
                first = sp.value_load(nrounds[0:1, 0:1], min_val=1, max_val=MAXR) if l else 0
                end = sp.value_load(nrounds[0:1, l:l + 1], min_val=1, max_val=(l + 1) * MAXR)
                with sp.Fori(first, end) as r:
                    with sp.Fori(0, RU // ESLOTS - 1) as i:
                        for j in range(ESLOTS):
                            sp.wait_ge(S["unit_used"], r * RU + i * ESLOTS + (j + 1))
                            expert_load(l, (i + 1) * 4, j)
                    with sp.If(r + 1 < end):
                        for j in range(ESLOTS):
                            sp.wait_ge(S["unit_used"], r * RU + (RU - ESLOTS) + (j + 1))
                            expert_load(l, 0, j)

                if l == 0:
                    sp.wait_ge(S["unit_used"], end * RU)

            def expert_src(l, e, kind):
                w = (moe_w_gate, moe_w_up, moe_w_down)[kind]
                src = w[l, e] if isinstance(e, int) else w[l, bass.ds(e, 1)].rearrange("o a b -> (o a) b")
                return src.rearrange("(p c) n -> p (c n)", p=P)

            experts(0, N0)
            for n in range(N0, N1):
                if n == N0 + MSLOTS:
                    first_pair(1)
                mix_load(n)
            experts(1, N1)

        @block.gpsimd
        def _(pool):
            def load(dst, src, s):
                pool.dma_start(dst, src).then_inc(S[s], 16)

            with nc.allow_non_contiguous_dma(reason="small vectors"):
                load(b_modT[:, :, :, :].rearrange("p l a c -> p (l a) c"), b_mod.rearrange("l (a p c) -> p (l a) c", a=6, c=DT), "small_in")
                load(ngT[:, :, :, :].rearrange("p l a c -> p (l a) c"), norm_g.rearrange("l a (p c) -> p (l a) c", c=DT), "small_in")
                load(conv_w, ab_conv_w[0].rearrange("w (q p) -> p w q", p=P), "small_in")
                load(mu, ab_mu[0].rearrange("(q p) -> p q", p=P), "small_in")
                for dst, src in ((w0, ab_w0), (a0, ab_a0), (k_k, ab_k_k), (k_a, ab_k_a), (gn_g, ab_gn_g), (gn_b, ab_gn_b)):
                    load(dst, src[0].rearrange("(q p) -> p q", p=P), "small_in")
                load(r_k, ab_r_k[0].rearrange("(q a) j -> (a j) q", a=2), "small_in")
                load(lora[0:64, :], ab_w_decay_up[0], "small_in")
                load(lora[64:128, :], ab_a_up[0], "small_in")
                load(gup[:, :], ab_g_up[0], "small_in")
                for l in range(2):
                    load(router[:, l], moe_w_router[l].rearrange("(p c) n -> p c n", c=DT), "small_in")
                    load(brout[:, l], moe_b_router[l].partition_broadcast(TR), "small_in")
                load(gb_in, gm_b_in[0].rearrange("(q p) -> p q", p=P), "small_in")
                load(ln_g, gm_ln_g[0].rearrange("(q p) -> p q", p=P), "small_in")
                load(ln_b, gm_ln_b[0].rearrange("(q p) -> p q", p=P), "small_in")
                load(ws00, gm_w_s[0, :, 0, 0].partition_broadcast(P), "small_in")

                pool.wait_ge(S["state_in"], 32)
                pool.dma_start(conv_s[0, :, 0, :], cv_in[:, 1, :]).then_inc(S["store"], 16)
                pool.wait_ge(S["tail_sb"], 2)
                pool.dma_start(shift_p[0], sh_out[0:1, :]).then_inc(S["store"], 16)
                pool.dma_start(shift_s[0], sh_out[1:NSEQ, :]).then_inc(S["store"], 16)
                pool.dma_start(conv_p[0, 0], cv_out[0:2, :]).then_inc(S["store"], 16)
                pool.dma_start(conv_s[0, :, 1, :], cv_out[2:10, :]).then_inc(S["store"], 16)
                pool.wait_ge(S["store"], 80)

                pool.wait_ge(S["svec_sb"], 1)
                pool.dma_start(vec_scratch, svec_tok).then_inc(S["svec_out"], 16)
                pool.wait_ge(S["svec_out"], 16)
                for b in range(NSA):
                    pool.dma_start(svec[8 * b:8 * b + 8], vec_scratch[b].rearrange("v (h j) -> h v j", j=HD)).then_inc(S["svec_in"], 16)
            pool.wait_ge(S["svec_in"], 16 * NSA)
            pool.wait_ge(S["swkv_in"], 16)

            n = [0]

            def step(i):
                n[0] += 1
                i.then_inc(S["pool_step"], 1)
                pool.wait_ge(S["pool_step"], n[0])

            r_v, w_v, k_v, v_v, kk_v, b_v = (svec[0:64, i, :] for i in range(6))
            rows = lambda v, i0: v.unsqueeze(1).broadcast_to([64, 16, HD])
            cols = lambda v, i0: v[:, i0:i0 + 16].unsqueeze(2).broadcast_to([64, 16, HD])
            t = s_tmp[0:64]

            def row_sums(out):
                for n in (32, 16, 8, 4, 2):
                    step(nc.gpsimd.tensor_tensor(t[:, :, 0:n], t[:, :, 0:n], t[:, :, n:2 * n], ALU.add))
                step(nc.gpsimd.tensor_tensor(out, t[:, :, 0], t[:, :, 1], ALU.add))

            for i0 in range(0, HD, 16):
                Sp = S_s[:, i0:i0 + 16, :]
                step(nc.gpsimd.tensor_tensor(t, Sp, rows(kk_v, i0), ALU.mult))
                row_sums(s_u[0:64, i0:i0 + 16])
                step(nc.gpsimd.tensor_tensor(Sp, Sp, rows(w_v, i0), ALU.mult))
                step(nc.gpsimd.tensor_tensor(t, cols(s_u[0:64], i0), rows(b_v, i0), ALU.mult))
                step(nc.gpsimd.tensor_tensor(Sp, Sp, t, ALU.subtract))
                step(nc.gpsimd.tensor_tensor(t, cols(v_v, i0), rows(k_v, i0), ALU.mult))
                step(nc.gpsimd.tensor_tensor(Sp, Sp, t, ALU.add))
                step(nc.gpsimd.tensor_tensor(t, Sp, rows(r_v, i0), ALU.mult))
                row_sums(s_o[0:64, i0:i0 + 16])
            pool.dma_start(wkv_s[0].rearrange("b h i j -> (b h) i j"), S_s).then_inc(S["store"], 16)
            pool.dma_start(out_scratch, s_o[0:64, :]).then_inc(S["samp_out"], 16)
            pool.wait_ge(S["samp_out"], 16)
            pool.dma_start(so_tok, out_scratch.rearrange("(b h) i -> b (h i)", h=H)).then_inc(S["samp_in"], 16)
            pool.wait_ge(S["store"], 96)
            pool.wait_ge(S["wkv_sb"], 1)
            pool.dma_start(wkv_p[0, 0].rearrange("h i j -> i h j"), wkv_o[0:64]).then_inc(S["store"], 16)
            pool.wait_ge(S["store"], 112)
            pool.wait_ge(S["s_sb"], NCH)
            pool.sem_inc(S["rwkv_free"], 1)

            def moe(l):
                pool.wait_ge(S["htr_sb"], 6 * l + 6)
                pool.dma_start(h_rows[l].rearrange("(t p) d -> p t d", p=TR), htok[0:TR]).then_inc(S["htok_out"], 16)
                pool.wait_ge(S["htok_out"], 16 * (l + 1))
                pool.wait_ge(S["round_set"], l + 1)
                first = pool.value_load(nrounds[0:1, 0:1], min_val=1, max_val=MAXR) if l else 0
                end = pool.value_load(nrounds[0:1, l:l + 1], min_val=1, max_val=(l + 1) * MAXR)

                def gather(jj, count):
                    pool.wait_ge(S["idx"], count)
                    pool.sem_inc(S["gather_go"], 1)
                    pool.indirect_dma_start(xg[jj % 2].rearrange("p c d -> p (c d)"), None, h_rows[l],
                                            bass.IndirectOffsetOnAxis(slot_idx[:, jj:jj + 1], 0)).then_inc(S["gat_" + "ab"[jj % 2]], 16)

                with pool.Fori(first, end) as r:
                    for j in range(2):
                        pool.wait_ge(S["xt_mm"], r * 66)
                        gather(j, r * 34 + (j + 1))
                    with pool.Fori(0, NTURN) as i:
                        for b in range(EBODY):
                            pool.wait_ge(S["xt_mm"], r * 66 + i * 8 + (2 * b + 2))
                            gather((b + 2) % 4, r * 34 + i * EBODY + (b + 3))

            moe(0)
            pool.wait_ge(S["y_done"], 2)
            pool.dma_start(wsn, gm_w_s[0].rearrange("g i j -> i g j")).then_inc(S["gmisc_in"], 16)
            pool.dma_start(bsb, gm_b_s[0].partition_broadcast(P)).then_inc(S["gmisc_in"], 16)
            pool.wait_ge(S["vs_sb"], 1)
            pool.dma_start(chunk_v_s[0, :, 0, :], vs_out[0:NSA, :]).then_inc(S["store"], 16)
            pool.wait_ge(S["store"], 128)
            pool.sem_inc(S["vs_stored"], 1)
            moe(1)
            pool.wait_ge(S["fin_sb"], 6)
            pool.dma_start(y_prompt[0, 0:2 * TR, :].rearrange("(t p) d -> p t d", p=TR), xo[0:TR, 0:2, :]).then_inc(S["store"], 16)
            pool.dma_start(y_prompt[0, 2 * TR:NPR, :], xo[0:NPR - 2 * TR, 2, :]).then_inc(S["store"], 16)
            pool.dma_start(y_sample[:, 0, :], xo[NPR - 2 * TR:TR, 2, :]).then_inc(S["store"], 16)
            pool.wait_ge(S["store"], 176)

        @block.tensor
        def _(pe):
            def mm(out, lhsT, rhs, start=True, stop=True):
                return nc.tensor.matmul(out, lhsT, rhs, start=start, stop=stop)

            def tr(out, in_):
                return nc.tensor.transpose(out, in_, ident[0:in_.shape[0], 0:in_.shape[0]])

            def arrived(n):
                pe.wait_ge(mload[n % MSLOTS], 16 * (n // MSLOTS + 1))

            def sum_squares(k):
                pe.wait_ge(S["sq_ready"], k + 1)
                for c in range(DT):
                    last = mm(psum[:, 7, 0:T], ones, hT[:, c, :], c == 0, c == DT - 1)
                last.then_inc(S["ss_mm"], 1)

            pe.wait_ge(S["const_in"], 16)
            pe.wait_ge(S["silu_c"], 1)
            for c in range(DT):
                last = tr(psum[:, 5, c * NSEQ:(c + 1) * NSEQ], ctok2[0:NSEQ, c::DT])
            last.then_inc(S["c_tr"], 1)
            def mod_turn(g):
                pe.wait_ge(S["mod_row"], 2 * (g + 1))
                if g >= 1:
                    pe.wait_ge(S["mod_set"], g)
                for c in range(DT):
                    last = mm(psum[:, 7, c * NSEQ:(c + 1) * NSEQ], mrow[:, c::DT], K[:, C_S4:C_S4 + NSEQ])
                last.then_inc(S["mod_tr"], 1)

            def mod_half(k):
                if k >= 1:
                    pe.wait_ge(S["mod_row"], k)
                if k % 2 == 0 and k not in (0, MOD_FIRST):
                    mod_turn(k // 2 - 1)
                for u in (2 * k, 2 * k + 1):
                    arrived(mod_unit[u])
                    w = mix_view(mod_unit[u])
                    for k2 in range(2):
                        for j in range(4):
                            last = mm(psum[32 * j:32 * j + 32, 6, (u % 2) * 256:(u % 2 + 1) * 256], cT[:, 4 * k2 + j, :],
                                      w[:, 4 * k2 + j, :], k2 == 0, k2 == 1)
                    last.then_inc(S["mod_mm"], 1)

            pe.wait_ge(S["c_sb"], 1)
            mod_half(0)
            pe.wait_ge(S["x_in"], 32)
            for t in range(2):
                for c in range(DT):
                    last = tr(psum[:, 2 * t + c // 4, (c % 4) * P:(c % 4 + 1) * P], xtok[:, t, c::DT])
                last.then_inc(S["x_tr"], 1)
            for c in range(DT):
                last = tr(psum[:, 4, c * NSA:(c + 1) * NSA], xtok[0:NSA, 2, c::DT])
            last.then_inc(S["x_tr"], 1)
            mod_half(1)
            sum_squares(0)
            pe.wait_ge(S["var_ready"], 1)
            mod_half(2)
            mod_half(3)
            mod_turn(1)

            pe.wait_ge(S["x_sb"], 3)
            pe.wait_ge(S["state_in"], 32)
            for q in range(PBT):
                tr(psum[:, 4, q * NSA:(q + 1) * NSA], sh_in[:, q * P:(q + 1) * P])
            for w in range(2):
                for q in range(QT):
                    last = tr(psum[:, 4, (PBT + w * QT + q) * NSA:(PBT + w * QT + q + 1) * NSA], cv_in[:, w, q * P:(q + 1) * P])
            last.then_inc(S["st_tr"], 1)
            pe.wait_ge(S["h_ready"], 1)
            for m in range(PROJT):
                n = proj_unit[m // 2]
                if m % 2 == 0:
                    arrived(n)
                if m >= 4:
                    pe.wait_ge(S["proj_sb"], m - 3)
                w = mix_view(n)
                for c in range(DT):
                    last = mm(psum[:, m % 4, 0:T], w[:, c, (m % 2) * P:(m % 2 + 1) * P], hT[:, c, :], c == 0, c == DT - 1)
                last.then_inc(S["proj_mm"], 1)
                if m % 2:
                    for k in MOD_PROJ[m // 2]:
                        mod_half(k)

            pe.wait_ge(S["proj_sb"], PROJT)
            pe.wait_ge(S["tail_ready"], 1)
            for q in range(PBT):
                last = tr(psum[0:NSEQ, q // 4, (q % 4) * P:(q % 4 + 1) * P], pb[:, q, NPR - 1:T])
            last.then_inc(S["tail_tr"], 1)
            for q in range(QT):
                last = tr(psum[0:10, 4, q * P:(q + 1) * P], proj[:, 8 + q, NPR - 2:T])
            last.then_inc(S["tail_tr"], 1)

            mod_half(17)
            pe.wait_ge(S["small_in"], 16 * NSMALL)
            pe.wait_ge(S["lora_in"], 2)
            pe.wait_ge(S["tail_sb"], 2)
            for q in range(QT):
                last = mm(psum[:, q, 0:T], lora[0:64, q * P:(q + 1) * P], xm[0:64, 12, :])
            last.then_inc(S["lora_mm"], 1)
            pe.wait_ge(S["mod_row"], 18)
            pe.wait_ge(S["mod_set"], 8)
            for q in range(QT):
                last = mm(psum[:, 4 + q, 0:T], lora[64:128, q * P:(q + 1) * P], xm[64:128, 12, :])
            last.then_inc(S["lora_mm"], 1)
            pe.wait_ge(S["lora_sb"], 1)
            for q in range(QT):
                last = mm(psum[:, q, 0:T], gup[:, q * P:(q + 1) * P], xm[:, 13, :])
            last.then_inc(S["lora_mm"], 1)

            pe.wait_ge(S["lora_sb"], 3)
            pe.wait_ge(S["kksq_ready"], 1)
            for q in range(QT):
                last = mm(psum[:, q, 0:T], blk, tmp[:, q, :])
            last.then_inc(S["kkss_mm"], 1)
            pe.wait_ge(S["rk_ready"], 1)
            for q in range(QT):
                last = mm(psum[:, 4 + q, 0:T], blk, bonus[:, q, :])
            last.then_inc(S["rk_mm"], 1)

            pe.wait_ge(S["pad_ready"], 1)
            pe.wait_ge(S["exp_ready"], 1)
            for v, src in enumerate((r_, cs, kh, v_, kk, bb)):
                for q in range(QT):
                    last = tr(psum[0:NSA, v, q * P:(q + 1) * P], src[:, q, NPR:T])
            last.then_inc(S["svec_tr"], 1)
            pe.wait_ge(S["svec_sb"], 1)
            pe.wait_ge(S["pad_ready"], 2)
            for t in range(2):
                for v, src in enumerate((v_, bb, kh)):
                    for q in range(QT):
                        last = tr(psum[:, 3 * t + v, q * P:(q + 1) * P], src[:, q, t * P:(t + 1) * P])
            last.then_inc(S["tok_tr"], 1)
            mod_half(18)
            pe.wait_ge(S["tok_sb"], 2)

            pairs = ((Az, bb), (bb, Az), (kh, Az), (bb, Rz), (kh, Rz))

            def side(a, h, t):
                return a[:, h if a.shape[1] == H else h // 2, t * P:(t + 1) * P]

            for t in range(2):
                for m in range(5):
                    for hh in range(2):
                        g = t * 10 + m * 2 + hh
                        if g >= 4:
                            pe.wait_ge(S["gram_sb"], g - 3)
                        for h in range(4 * hh, 4 * hh + 4):
                            last = mm(psum[:, g % 4, (h % 4) * P:(h % 4 + 1) * P], side(pairs[m][0], h, t), side(pairs[m][1], h, t))
                        last.then_inc(S["gram_mm"], 1)
                pe.wait_ge(S["xy0"], 2 * t + 2)
                for k in range(1, 6):
                    if t == 0:
                        mod_half(18 + k)
                    elif k == 1:
                        mod_turn(11)
                    for hh in range(2):
                        n = t * 10 + (k - 1) * 2 + hh
                        if n >= 2:
                            pe.wait_ge(S["xy"], n - 1)
                        for h in range(4 * hh, 4 * hh + 4):
                            last = mm(psum[:, 4 + hh, (h % 4) * P:(h % 4 + 1) * P], L1[:, h, :], Y[:, h, :])
                        last.then_inc(S["z_mm"], 1)
                    for hh in range(2):
                        n = t * 10 + (k - 1) * 2 + hh
                        pe.wait_ge(S["z_sb"], n + 1)
                        for h in range(4 * hh, 4 * hh + 4):
                            mm(psum[:, 2 * hh, (h % 4) * P:(h % 4 + 1) * P], X[:, h, :], Z[:, h, :])
                        for h in range(4 * hh, 4 * hh + 4):
                            last = mm(psum[:, 2 * hh + 1, (h % 4) * P:(h % 4 + 1) * P], Z[:, h, :], X[:, h, :])
                        last.then_inc(S["d_mm"], 1)
                pe.wait_ge(S["xy"], t * 10 + 10)
                for c in (2 * t, 2 * t + 1):
                    p0, par = 64 * (c % 2), c % 2
                    tok = slice(c * CH, (c + 1) * CH)
                    if c >= 1:
                        pe.wait_ge(S["s_sb"], c)
                    pe.wait_ge(S["mod_row"], 24)
                    pe.wait_ge(S["mod_set"], 11 + t)
                    for h in range(H):
                        o = psum[p0:p0 + 64, 6, h * 64:(h + 1) * 64]
                        if c >= 1:
                            mm(o, Az[:, h, tok], S0T[:, h // 2, :], True, False)
                        last = mm(o, L2T[:, h, p0:p0 + 64], Vz[:, par, t, h * 64:(h + 1) * 64], c == 0, True)
                    last.then_inc(S["rhs_mm"], 1)
                    pe.wait_ge(S["rhs_sb"], c + 1)
                    for h in range(H):
                        last = mm(psum[p0:p0 + 64, 7, h * 64:(h + 1) * 64], Y[:, h, p0:p0 + 64], rhs_s[:, h * 64:(h + 1) * 64])
                    last.then_inc(S["u_mm"], 1)
                    pe.wait_ge(S["u_sb"], c + 1)
                    for h in range(H):
                        ps = slice(64 * (h % 2), 64 * (h % 2) + 64)
                        o = psum[ps, 4, (h // 2) * 64:(h // 2 + 1) * 64]
                        if c >= 1:
                            mm(o, S0T[:, h // 2, :], Rz[:, h, tok], True, False)
                        mm(o, Uz[:, par, h * 64:(h + 1) * 64], R1T[:, h, p0:p0 + 64], c == 0, False)
                        last = mm(o, Vz[:, par, t, h * 64:(h + 1) * 64], R2T[:, h, p0:p0 + 64], False, True)
                    last.then_inc(S["o_mm"], 1)
                    for h in range(H):
                        ps = slice(64 * (h % 2), 64 * (h % 2) + 64)
                        o = psum[ps, 5, (h // 2) * 64:(h // 2 + 1) * 64]
                        mm(o, Btok[:, t, h * 64:(h + 1) * 64], Uz[:, par, h * 64:(h + 1) * 64], True, False)
                        last = mm(o, Ktok[:, t, h * 64:(h + 1) * 64], Vz[:, par, t, h * 64:(h + 1) * 64], False, True)
                    last.then_inc(S["s_mm"], 1)
            pe.wait_ge(S["s_sb"], NCH)
            for q in range(QT):
                last = tr(psum[0:64, 0, q * P:(q + 1) * P], S0T[:, q, :])
            last.then_inc(S["wkv_tr"], 1)
            pe.wait_ge(S["samp_in"], 16)
            for q in range(QT):
                last = tr(psum[:, 1, q * NSA:(q + 1) * NSA], so_tok[:, q * P:(q + 1) * P])
            last.then_inc(S["samp_tr"], 1)
            pe.wait_ge(S["wkv_sb"], 1)
            pe.wait_ge(S["samp_sb"], 1)
            for q in range(QT):
                last = mm(psum[:, q, 0:T], blk, outT[:, q, :])
            last.then_inc(S["gn_mm"], 1)
            pe.wait_ge(S["gn_c"], 1)
            for q in range(QT):
                last = mm(psum[:, 4 + q, 0:T], blk, tmp[:, q, :])
            last.then_inc(S["gn_mm"], 1)

            def output_product(l, u0, rhs):
                for u in range(4):
                    arrived(u0 + u)
                for m in range(DT):
                    if m >= 4:
                        pe.wait_ge(S["out_sb"], 8 * l + m - 3)
                    for q in range(8):
                        last = mm(psum[:, m % 4, 0:T], mix_view(u0 + q // 2)[:, q % 2, m::DT], rhs[:, q, :], q == 0, q == 7)
                    last.then_inc(S["out_mm"], 1)

            def moe(l):
                pe.wait_ge(S["h_ready"], 2 * l + 2)
                for t in range(3):
                    for c in range(DT):
                        last = mm(psum[0:TR, 0, t * NE:(t + 1) * NE], hT[:, c, t * TR:(t + 1) * TR], router[:, l, c, :], c == 0, c == DT - 1)
                last.then_inc(S["logit_mm"], 1)
                for n in range(6):
                    if n >= 2:
                        pe.wait_ge(S["htr_sb"], 6 * l + n - 1)
                    for c in range(4):
                        last = tr(psum[0:TR, 2 + n % 2, c * P:(c + 1) * P], hT[:, (n % 2) * 4 + c, (n // 2) * TR:(n // 2 + 1) * TR])
                    last.then_inc(S["htr_mm"], 1)
                u0 = U_SH[l]
                for b, n in ((4, u0), (6, u0 + 1)):
                    arrived(n)
                    for j in range(2):
                        for c in range(DT):
                            last = mm(psum[:, b + j, 0:T], mix_view(n)[:, c, j::2], hT[:, c, :], c == 0, c == DT - 1)
                    last.then_inc(S["sh_mm"], 1)
                pe.wait_ge(S["mask_ready"], l + 1)
                for t in range(3):
                    for s in range(t + 1):
                        last = mm(psum[0:TR, 1, t * NE:(t + 1) * NE], (K[0:TR, C_UPT:C_UPT + TR] if s == t else ones[0:TR, 0:TR]), mask[0:TR, s, :], s == 0, s == t)
                for s in range(3):
                    last = mm(psum[0:TR, 1, 3 * NE:4 * NE], ones[0:TR, 0:TR], mask[0:TR, s, :], s == 0, s == 2)
                last.then_inc(S["rank_mm"], 1)
                pe.wait_ge(S["htr_sb"], 6 * l + 6)
                pe.wait_ge(S["sh_hid"], l + 1)
                arrived(u0 + 2)
                for m in range(DT):
                    if m >= 2:
                        pe.wait_ge(S["shd_sb"], 8 * l + m - 1)
                    for j in range(2):
                        last = mm(psum[:, 2 + m % 2, 0:T], mix_view(u0 + 2)[:, j, m::DT], shid[:, j, :], j == 0, j == 1)
                    last.then_inc(S["shd_mm"], 1)

                pe.wait_ge(S["round_set"], l + 1)
                pe.wait_ge(S["shd_sb"], 8 * l + 8)
                first = pe.value_load(nrounds[0:1, 0:1], min_val=1, max_val=MAXR) if l else 0
                end = pe.value_load(nrounds[0:1, l:l + 1], min_val=1, max_val=(l + 1) * MAXR)

                def slots(r, j, jj):
                    pe.wait_ge(S["sel"], r * 34 + (j + 1))
                    for t in range(3):
                        mm(psum[:, 4, 0:1], slotsel[0:TR, t].rearrange("p a s -> p (a s)"), K[0:TR, C_TOK + t:C_TOK + t + 1], t == 0, t == 2)
                    for t in range(3):
                        last = mm(psum[:, 4, 2:4], slotsel[0:TR, t].rearrange("p a s -> p (a s)"), comb[0:TR, t, 2 * j:2 * j + 2], t == 0, t == 2)
                    last.then_inc(S["slot_mm"], 1)

                with pe.Fori(first, end) as r:
                    for j in range(2):
                        slots(r, j, j)
                    pe.wait_ge(S["gat_a"], r * 272 + 16)
                    pe.wait_ge(S["ht_sb"], r * NPAIR)
                    for half in range(2):
                        if half:
                            pe.wait_ge(S["xt_sb"], r * 66 + 1)
                        for c in range(4):
                            last = tr(psum[:, 5, c * P:(c + 1) * P], xg[0][:, half * 4 + c, :])
                        last.then_inc(S["xt_mm"], 1)
                    with pe.Fori(0, NTURN) as i:
                        for b in range(EBODY):
                            m1_ = r * NPAIR + i * EBODY + (b + 1)
                            nb = (b + 1) % 2
                            pe.wait_ge(S["gat_" + "ab"[nb]], r * 272 + i * 32 + 16 * ((b + 1) // 2 + 1))
                            pe.wait_ge(S["ht_sb"], m1_ - 1)
                            pe.wait_ge(S["xt_sb"], r * 66 + i * 8 + (2 * b + 2))
                            for c in range(4):
                                last = tr(psum[:, 5, c * P:(c + 1) * P], xg[nb][:, c, :])
                            last.then_inc(S["xt_mm"], 1)
                            s0 = eslot((b % 2) * PU)

                            def product(kind, bank, inp):
                                for e in range(2):
                                    pe.wait_ge(eload[s0 + 2 * kind + e], r * (RU // ESLOTS * 16) + i * 32 + 16 * (b // 2 + 1))
                                for c in range(DT):
                                    for e in range(2):
                                        x = mm(psum[64 * e:64 * e + 64, bank, 0:DE], inp[:, c, 64 * e:64 * e + 64],
                                               ring[:, s0 + 2 * kind + e, c * DE:(c + 1) * DE], c == 0, c == DT - 1)
                                        if c == DT - 1:
                                            x.then_inc(S["unit_used"], 1)

                            pe.wait_ge(S["gsil"], m1_ - 1)
                            product(0, 0, xgT[b % 2])
                            pe.wait_ge(S["sel"], r * 34 + i * EBODY + (b + 3))
                            for t in range(3):
                                mm(psum[:, 4, 0:1], slotsel[0:TR, t].rearrange("p a s -> p (a s)"), K[0:TR, C_TOK + t:C_TOK + t + 1], t == 0, t == 2)
                            for t in range(3):
                                last = mm(psum[:, 4, 2:4], slotsel[0:TR, t].rearrange("p a s -> p (a s)"),
                                          comb[0:TR, t, bass.ds(i * 8 + (2 * b + 4), 2)], t == 0, t == 2)
                            last.then_inc(S["slot_mm"], 1)
                            pe.wait_ge(S["xt_sb"], r * 66 + i * 8 + (2 * b + 3))
                            for c in range(4):
                                last = tr(psum[:, 5, c * P:(c + 1) * P], xg[nb][:, 4 + c, :])
                            last.then_inc(S["xt_mm"], 1)
                            pe.wait_ge(S["ghid"], m1_ - 1)
                            product(1, 1, xgT[b % 2])
                            pe.wait_ge(S["os_a"], m1_ - 1)
                            pe.wait_ge(S["os_b"], m1_ - 1)
                            for c in range(DT):
                                q = r * 264 + i * 32 + (8 * b + c)
                                if b or c >= 2:
                                    pe.wait_ge(S["cb_add"], q - 1)
                                else:
                                    pe.wait_ge(S["cb_add"], r * 264 + i * 32)
                                mm(psum[:, 6 + c % 2, 0:T], gout[:, c::DT], selT[(b + 3) % 4]).then_inc(S["cb_mm"], 1)
                            pe.wait_ge(S["ghid"], m1_)
                            pe.wait_ge(S["xt_sb"], r * 66 + i * 8 + (2 * b + 4))
                            for j in range(2):
                                last = tr(psum[:, 5, j * P:(j + 1) * P], ghid[:, j::2])
                            last.then_inc(S["ht_mm"], 1)
                            pe.wait_ge(S["ht_sb"], m1_)
                            for e in range(2):
                                pe.wait_ge(eload[s0 + 4 + e], r * (RU // ESLOTS * 16) + i * 32 + 16 * (b // 2 + 1))
                            for n in range(2):
                                for j in range(2):
                                    for e in range(2):
                                        x = mm(psum[64 * e:64 * e + 64, 2 + n, :], ghT[:, j, 64 * e:64 * e + 64],
                                               ring[:, s0 + 4 + e, j * D + n * 512:j * D + n * 512 + 512], j == 0, j == 1)
                                        if n == 1 and j == 1:
                                            x.then_inc(S["unit_used"], 1)
                    pe.wait_ge(S["gat_b"], (r + 1) * 272)
                    pe.wait_ge(S["os_a"], (r + 1) * NPAIR)
                    pe.wait_ge(S["os_b"], (r + 1) * NPAIR)
                    for c in range(DT):
                        pe.wait_ge(S["cb_add"], r * 264 + (256 + c - (1 if c >= 2 else 0) if c >= 2 else 256))
                        mm(psum[:, 6 + c % 2, 0:T], gout[:, c::DT], selT[3]).then_inc(S["cb_mm"], 1)

            pe.wait_ge(S["yab_ready"], 1)
            output_product(0, U_ABO, hT)
            sum_squares(1)
            sum_squares(2)
            moe(0)
            sum_squares(3)
            sum_squares(4)

            pe.wait_ge(S["h_ready"], 3)
            for m in range(16):
                n = U_GMI + m // 2
                if m % 2 == 0:
                    arrived(n)
                if m >= 4:
                    pe.wait_ge(S["z_sb1"], m - 3)
                for c in range(DT):
                    last = mm(psum[:, m % 4, 0:T], mix_view(n)[:, c, (m % 2) * P:(m % 2 + 1) * P], hT[:, c, :], c == 0, c == DT - 1)
                last.then_inc(S["z_mm1"], 1)
            pe.wait_ge(S["gmisc_in"], 32)
            for g in range(8):
                last = tr(psum[:, 4 + g // 4, (g % 4) * P:(g % 4 + 1) * P], wsn[:, g, :])
            last.then_inc(S["ws_tr"], 1)
            pe.wait_ge(S["z_sb1"], 16)
            for g in range(8):
                last = mm(psum[:, 6, 0:T], ones, z[:, 8 + g, :], g == 0, g == 7)
            last.then_inc(S["vmu_mm"], 1)
            pe.wait_ge(S["vc_ready"], 1)
            for g in range(8):
                last = mm(psum[:, 7, 0:T], ones, gt1[:, g, :], g == 0, g == 7)
            last.then_inc(S["vvar_mm"], 1)
            pe.wait_ge(S["v_ready"], 1)
            for t in range(2):
                for g in range(8):
                    last = tr(psum[:, 2 * t + g // 4, (g % 4) * P:(g % 4 + 1) * P], z[:, 8 + g, t * P:(t + 1) * P])
                last.then_inc(S["vt_tr"], 1)
            pe.wait_ge(S["ws_sb"], 1)
            for g in range(8):
                last = tr(psum[0:NSA, 4 + g // 4, (g % 4) * P:(g % 4 + 1) * P], z[:, 8 + g, NPR:T])
            last.then_inc(S["vt_tr"], 1)
            pe.wait_ge(S["vt_sb"], 2)
            for t in range(2):
                for g in range(8):
                    last = mm(psum[:, 2 * t + g // 4, (g % 4) * P:(g % 4 + 1) * P], vtok[:, t, g * P:(g + 1) * P], wsT[:, g, :])
                last.then_inc(S["sg_mm"], 1)
            pe.wait_ge(S["sg_ready"], 1)
            output_product(1, U_GMO, z)
            sum_squares(5)
            sum_squares(6)
            moe(1)
            sum_squares(7)
            pe.wait_ge(S["y_done"], 4)
            for n in range(6):
                if n >= 2:
                    pe.wait_ge(S["fin_sb"], n - 1)
                for c in range(4):
                    last = tr(psum[0:TR, n % 2, c * P:(c + 1) * P], xT[:, (n % 2) * 4 + c, (n // 2) * TR:(n // 2 + 1) * TR])
                last.then_inc(S["fin_tr"], 1)

        @block.scalar
        def _(act):
            def f(out, in_, func, **kw):
                return nc.scalar.activation(out, in_, func, **kw)

            def root(k, a, b, n=1):
                act.wait_ge(S[a], k)
                f(rstd[:, :], rstd[:, :], ACT.Sqrt).then_inc(S[b], 1)

            act.wait_ge(S["c_in"], 32)
            f(ctok2[0:NSEQ, :], ctok[0:NSEQ, :], ACT.Silu).then_inc(S["silu_c"], 1)

            def mod_rows(k):
                act.wait_ge(S["mod_mm"], 2 * (k + 1))
                if k >= 2:
                    act.wait_ge(S["mod_tr"], k // 2)
                f(mrow[:, k % 2 * 512:(k % 2 + 1) * 512], psum[:, 6, :], ACT.Copy).then_inc(S["mod_row"], 1)

            mod_rows(0)
            mod_rows(1)
            root(1, "var_ready", "sd_ready")
            mod_rows(2)
            mod_rows(3)
            for m in range(PROJT):
                act.wait_ge(S["proj_mm"], m + 1)
                f(proj[:, m, :], psum[:, m % 4, 0:T], ACT.Copy).then_inc(S["proj_sb"], 1)
                if m % 2:
                    for k in MOD_PROJ[m // 2]:
                        mod_rows(k)
            mod_rows(17)
            act.wait_ge(S["small_in"], 16 * NSMALL)
            act.wait_ge(S["mixed"], 1)
            f(xm[0:64, 12, :], xm[0:64, 12, :], ACT.Tanh).then_inc(S["lora_in"], 1)
            f(xm[:, 13, :], xm[:, 13, :], ACT.Sigmoid).then_inc(S["lora_in"], 1)
            act.wait_ge(S["mixed"], 2)
            act.wait_ge(S["lora_mm"], 1)
            for q in range(QT):
                last = f(ld[:, q, :], psum[:, q, 0:T], ACT.Sigmoid, bias=w0[:, q:q + 1])
            last.then_inc(S["lora_sb"], 1)
            act.wait_ge(S["lora_mm"], 2)
            for q in range(QT):
                last = f(a_sig[:, q, :], psum[:, 4 + q, 0:T], ACT.Sigmoid, bias=a0[:, q:q + 1])
            last.then_inc(S["lora_sb"], 1)
            act.wait_ge(S["lora_mm"], 3)
            f(g_t, psum[:, 0:4, 0:T], ACT.Copy).then_inc(S["lora_sb"], 1)
            act.wait_ge(S["kkss_mm"], 1)
            f(tmp, psum[:, 0:4, 0:T], ACT.Sqrt).then_inc(S["kknorm"], 1)
            act.wait_ge(S["cs_ready"], 1)
            f(px, px, ACT.Exp).then_inc(S["act"], 1)
            f(ld, cs, ACT.Exp, scale=-1.0).then_inc(S["act"], 1)
            act.wait_ge(S["act"], 2)
            f(cs, cs, ACT.Exp).then_inc(S["exp_ready"], 1)
            act.wait_ge(S["svec_tr"], 1)
            act.wait_ge(S["store"], 80)
            f(svec_tok, psum[0:NSA, 0:6, :], ACT.Copy).then_inc(S["svec_sb"], 1)
            act.wait_ge(S["svec_out"], 16)
            act.wait_ge(S["tok_tr"], 1)
            for t in range(2):
                f(Btok[:, t, :], psum[:, 3 * t + 1, :], ACT.Copy)
                last = f(Ktok[:, t, :], psum[:, 3 * t + 2, :], ACT.Copy)
            last.then_inc(S["tok_sb"], 1)
            for k in range(18, 24):
                mod_rows(k)
            act.wait_ge(S["wkv_tr"], 1)
            f(wkv_o[0:64], psum[0:64, 0, :].rearrange("p (h j) -> p h j", h=H), ACT.Copy).then_inc(S["wkv_sb"], 1)
            act.wait_ge(S["gn_v"], 1)
            f(tmp, tmp, ACT.Sqrt).then_inc(S["gn_sd"], 1)

            def outputs(l, y):
                for m in range(DT):
                    act.wait_ge(S["out_mm"], 8 * l + m + 1)
                    f(y[:, m, :], psum[:, m % 4, 0:T], ACT.Copy).then_inc(S["out_sb"], 1)

            def moe(l):
                act.wait_ge(S["logit_mm"], l + 1)
                if l == 0:
                    act.wait_ge(S["rwkv_free"], 1)
                else:
                    act.wait_ge(S["vs_stored"], 1)
                act.wait_ge(S["y_done"], 2 * l + 1)
                f(score[0:TR], psum[0:TR, 0, 0:3 * NE].rearrange("p (t e) -> p t e", t=3), ACT.Sigmoid).then_inc(S["score_ready"], 1)
                for n in range(6):
                    act.wait_ge(S["htr_mm"], 6 * l + n + 1)
                    f(htok[0:TR, n // 2, (n % 2) * 512:(n % 2 + 1) * 512], psum[0:TR, 2 + n % 2, :], ACT.Copy).then_inc(S["htr_sb"], 1)
                act.wait_ge(S["sh_mm"], 2 * l + 1)
                f(ssil, psum[:, 4:6, 0:T], ACT.Silu).then_inc(S["sh_act"], 1)
                for m in range(DT):
                    act.wait_ge(S["shd_mm"], 8 * l + m + 1)
                    f(yacc[:, m, :], psum[:, 2 + m % 2, 0:T], ACT.Copy).then_inc(S["shd_sb"], 1)
                act.wait_ge(S["round_set"], l + 1)
                first = act.value_load(nrounds[0:1, 0:1], min_val=1, max_val=MAXR) if l else 0
                end = act.value_load(nrounds[0:1, l:l + 1], min_val=1, max_val=(l + 1) * MAXR)
                with act.Fori(first, end) as r:
                    for half in range(2):
                        act.wait_ge(S["xt_mm"], r * 66 + (half + 1))
                        if half == 0:
                            act.wait_ge(S["unit_used"], r * RU)
                        f(xgT[0][:, half * 4:half * 4 + 4, :], psum[:, 5, :].rearrange("p (c s) -> p c s", c=4), ACT.Copy).then_inc(S["xt_sb"], 1)
                    with act.Fori(0, NTURN) as i:
                        for b in range(EBODY):
                            m1_ = r * NPAIR + i * EBODY + (b + 1)
                            u0_ = r * RU + i * (EBODY * PU) + b * PU
                            nb = (b + 1) % 2
                            for half in range(2):
                                act.wait_ge(S["xt_mm"], r * 66 + i * 8 + (2 * b + 3 + half))
                                if half == 0:
                                    act.wait_ge(S["unit_used"], u0_)
                                f(xgT[nb][:, half * 4:half * 4 + 4, :], psum[:, 5, :].rearrange("p (c s) -> p c s", c=4), ACT.Copy).then_inc(S["xt_sb"], 1)
                                if half == 0:
                                    act.wait_ge(S["unit_used"], u0_ + 2)
                                    act.wait_ge(S["ghid"], m1_ - 1)
                                    f(gsil, psum[:, 0, 0:DE], ACT.Silu).then_inc(S["gsil"], 1)
                            act.wait_ge(S["ht_mm"], m1_)
                            act.wait_ge(S["unit_used"], u0_)
                            f(ghT, psum[:, 5, 0:2 * P].rearrange("p (j s) -> p j s", j=2), ACT.Copy).then_inc(S["ht_sb"], 1)
                            act.wait_ge(S["unit_used"], u0_ + 6)
                            f(gout[:, 0:512], psum[:, 2, :], ACT.Copy).then_inc(S["os_a"], 1)

            outputs(0, yacc)
            root(2, "var_ready", "sd_ready")
            root(3, "var_ready", "sd_ready")
            moe(0)
            root(4, "var_ready", "sd_ready")
            root(5, "var_ready", "sd_ready")
            for m in range(16):
                act.wait_ge(S["z_mm1"], m + 1)
                if m == 0:
                    act.wait_ge(S["y_done"], 2)
                f(z[:, m, :], psum[:, m % 4, 0:T], ACT.Gelu_apprx_tanh, bias=gb_in[:, m:m + 1]).then_inc(S["z_sb1"], 1)
            root(1, "ln_var", "ln_sd")
            act.wait_ge(S["vt_tr"], 1)
            f(vtok[:, 0, :].rearrange("p (a n) -> p a n", a=2), psum[:, 0:2, :], ACT.Copy).then_inc(S["vt_sb"], 1)
            act.wait_ge(S["vt_tr"], 2)
            f(vtok[:, 1, :].rearrange("p (a n) -> p a n", a=2), psum[:, 2:4, :], ACT.Copy).then_inc(S["vt_sb"], 1)
            act.wait_ge(S["vt_tr"], 3)
            f(vs_out[0:NSA, :].rearrange("p (a n) -> p a n", a=2), psum[0:NSA, 4:6, :], ACT.Copy).then_inc(S["vs_sb"], 1)
            outputs(1, gt1)
            root(6, "var_ready", "sd_ready")
            root(7, "var_ready", "sd_ready")
            moe(1)
            root(8, "var_ready", "sd_ready")
            act.wait_ge(S["y_done"], 4)
            for n in range(6):
                act.wait_ge(S["fin_tr"], n + 1)
                out = xo[0:TR, n // 2, :].rearrange("p (d c) -> p c d", c=DT)[:, (n % 2) * 4:(n % 2) * 4 + 4, :]
                f(out, psum[0:TR, n % 2, :].rearrange("p (c d) -> p c d", c=4), ACT.Copy).then_inc(S["fin_sb"], 1)

        @block.vector
        def _(dve):
            V = nc.vector
            done = [0]

            def v(i):
                done[0] += 1
                i.then_inc(S["vec"], 1)
                dve.wait_ge(S["vec"], done[0])

            def over(col, n):
                return col.unsqueeze(len(col.shape)).broadcast_to([*col.shape, n])

            def rms(k, src):
                V.tensor_tensor(hT[:, :, :], src, src, ALU.mult).then_inc(S["sq_ready"], 1)
                dve.wait_ge(S["ss_mm"], k + 1)
                V.tensor_scalar(rstd[:, :], psum[:, 7, 0:T], 1.0 / D, EPS, ALU.mult, ALU.add).then_inc(S["var_ready"], 1)
                dve.wait_ge(S["sd_ready"], k + 1)
                v(V.reciprocal(rstd[:, :], rstd[:, :]))

            wide = lambda: rstd[:, :].unsqueeze(1).broadcast_to([P, DT, T])

            def pre(k, l, half):
                normalise(k)
                modulate(l, half)

            def normalise(k):
                rms(k, xT[:, :, :])
                v(V.tensor_tensor(hT[:, :, :], xT[:, :, :], wide(), ALU.mult))

            def modulate(l, half):
                sh, sc = mod[:, l, 3 * half], mod[:, l, 3 * half + 1]
                v(V.tensor_tensor(hT[:, :, NPR:T], hT[:, :, NPR:T], sc[:, :, 1:NSEQ], ALU.mult))
                V.tensor_tensor(hT[:, :, NPR:T], hT[:, :, NPR:T], sh[:, :, 1:NSEQ], ALU.add)
                for c in range(DT):
                    last = V.tensor_scalar(hT[:, c, 0:NPR], hT[:, c, 0:NPR], sc[:, c, 0:1], sh[:, c, 0:1], ALU.mult, ALU.add)
                last.then_inc(S["h_ready"], 1)

            def post(k, l, half, y):
                rms(k, y)
                v(V.tensor_tensor(y, y, wide(), ALU.mult))
                g = mod[:, l, 3 * half + 2]
                v(V.tensor_tensor(y[:, :, NPR:T], y[:, :, NPR:T], g[:, :, 1:NSEQ], ALU.mult))
                V.tensor_tensor(xT[:, :, NPR:T], xT[:, :, NPR:T], y[:, :, NPR:T], ALU.add)
                for c in range(DT):
                    last = V.scalar_tensor_tensor(xT[:, c, 0:NPR], y[:, c, 0:NPR], g[:, c, 0:1], xT[:, c, 0:NPR], ALU.mult, ALU.add)
                last.then_inc(S["y_done"], 1)
                dve.wait_ge(S["y_done"], 2 * l + half + 1)

            v(V.memset(cT[:, :, :], 0.0))
            dve.wait_ge(S["c_tr"], 1)
            V.tensor_copy(cT[:, :, 0:NSEQ], psum[:, 5, 0:DT * NSEQ].rearrange("p (c s) -> p c s", c=DT)).then_inc(S["c_sb"], 1)
            for t in range(2):
                dve.wait_ge(S["x_tr"], t + 1)
                V.tensor_copy(xT[:, :, t * P:(t + 1) * P].rearrange("p (a c) n -> p a c n", a=2),
                              psum[:, 2 * t:2 * t + 2, :].rearrange("p a (c n) -> p a c n", c=4)).then_inc(S["x_sb"], 1)
            dve.wait_ge(S["x_tr"], 3)
            V.tensor_copy(xT[:, :, NPR:T], psum[:, 4, 0:DT * NSA].rearrange("p (c s) -> p c s", c=DT)).then_inc(S["x_sb"], 1)
            dve.wait_ge(S["x_sb"], 3)
            normalise(0)

            def mod_part(g):
                l, part = g // 6, g % 6
                dve.wait_ge(S["mod_tr"], g + 1)
                m = mod[:, l, part]
                V.tensor_tensor(m, psum[:, 7, 0:DT * NSEQ].rearrange("p (c s) -> p c s", c=DT),
                                over(b_modT[:, l, part], NSEQ), ALU.add).then_inc(S["mod_set"], 1)
                dve.wait_ge(S["mod_set"], g + 1)
                if part in (1, 4):
                    v(V.tensor_scalar(m, m, 1.0, None, ALU.add))
                    v(V.tensor_tensor(m, m, over(ngT[:, l, part // 3 * 2], NSEQ), ALU.mult))
                if part in (2, 5):
                    v(V.tensor_tensor(m, m, over(ngT[:, l, part // 3 * 2 + 1], NSEQ), ALU.mult))

            dve.wait_ge(S["small_in"], 16 * NSMALL)
            mod_part(0)
            mod_part(1)
            modulate(0, 0)
            dve.wait_ge(S["st_tr"], 1)
            v(V.tensor_copy(st_shift, psum[:, 4, 0:PBT * NSA].rearrange("p (q s) -> p q s", q=PBT)))
            v(V.tensor_copy(st_conv, psum[:, 4, PBT * NSA:PBT * NSA + 64].rearrange("p (w q s) -> p w q s", w=2, q=QT)))
            for g in range(2, 8):
                mod_part(g)
            dve.wait_ge(S["proj_sb"], PROJT)
            V.tensor_tensor(xm[:, :, 1:NPR], pb[:, :, 0:NPR - 1], pb[:, :, 1:NPR], ALU.subtract)
            V.tensor_scalar(xm[:, :, 0:1], pb[:, :, 0:1], -1.0, None, ALU.mult)
            v(V.tensor_tensor(xm[:, :, NPR:T], st_shift, pb[:, :, NPR:T], ALU.subtract))
            for q in reversed(range(PBT)):
                last = V.scalar_tensor_tensor(xm[:, q, :], xm[:, q, :], mu[:, q:q + 1], pb[:, q, :], ALU.mult, ALU.add)
            last.then_inc(S["mixed"], 1)
            gated = proj[:, 8:12, :]
            V.tensor_tensor(gated, gated, proj[:, 0:4, :], ALU.mult).then_inc(S["tail_ready"], 1)
            dve.wait_ge(S["tail_ready"], 1)
            for q in range(QT):
                y, gq = conv_t[:, q, :], gated[:, q, :]
                wq = [conv_w[:, w, q:q + 1] for w in range(3)]
                v(V.tensor_scalar(y, gq, wq[2], None, ALU.mult))
                v(V.scalar_tensor_tensor(y[:, 1:NPR], gq[:, 0:NPR - 1], wq[1], y[:, 1:NPR], ALU.mult, ALU.add))
                v(V.scalar_tensor_tensor(y[:, 2:NPR], gq[:, 0:NPR - 2], wq[0], y[:, 2:NPR], ALU.mult, ALU.add))
                v(V.scalar_tensor_tensor(y[:, NPR:T], st_conv[:, 1, q], wq[1], y[:, NPR:T], ALU.mult, ALU.add))
                v(V.scalar_tensor_tensor(y[:, NPR:T], st_conv[:, 0, q], wq[0], y[:, NPR:T], ALU.mult, ALU.add))
            v(V.tensor_tensor(y_a, conv_t, proj[:, 4:8, :], ALU.mult))
            dve.wait_ge(S["state_in"], 32)
            dve.wait_ge(S["tail_tr"], 1)
            V.tensor_copy(sh_out, psum[0:NSEQ, 0:4, :].rearrange("p a b -> p (a b)")[:, 0:PB]).then_inc(S["tail_sb"], 1)
            dve.wait_ge(S["tail_tr"], 2)
            V.tensor_copy(cv_out, psum[0:10, 4, :]).then_inc(S["tail_sb"], 1)
            dve.wait_ge(S["tail_sb"], 2)
            V.memset(Uz, 0.0)
            V.memset(rhs_s, 0.0).then_inc(S["mixed"], 1)

            dve.wait_ge(S["lora_sb"], 1)
            v(V.tensor_scalar(ld, ld, -EMH, None, ALU.mult))
            for q in range(QT):
                for c in range(NCH):
                    s = slice(c * CH, (c + 1) * CH)
                    V.tensor_tensor_scan(cs[:, q, s], ones[:, 0:CH], ld[:, q, s], 0.0, ALU.mult, ALU.add)
            v(V.tensor_copy(cs[:, :, NPR:T], ld[:, :, NPR:T]))
            V.tensor_tensor(px, cs, ld, ALU.subtract).then_inc(S["cs_ready"], 1)
            dve.wait_ge(S["lora_sb"], 3)
            v(V.tensor_tensor(kk, k_, over(k_k, T), ALU.mult))
            V.tensor_tensor(tmp, kk, kk, ALU.mult).then_inc(S["kksq_ready"], 1)
            v(V.tensor_scalar(kh, a_sig, -1.0, None, ALU.add))
            v(V.tensor_tensor(kh, kh, over(k_a, T), ALU.mult))
            v(V.scalar_tensor_tensor(kh, kh, 1.0, k_, ALU.add, ALU.mult))
            v(V.tensor_tensor(bonus, r_, over(r_k, T), ALU.mult))
            V.tensor_tensor(bonus, bonus, kh, ALU.mult).then_inc(S["rk_ready"], 1)
            dve.wait_ge(S["kknorm"], 1)
            v(V.tensor_scalar(tmp, tmp, 1e-12, None, ALU.max))
            v(V.reciprocal(tmp, tmp))
            v(V.tensor_tensor(kk, kk, tmp, ALU.mult))
            v(V.tensor_tensor(bb, kk, a_sig, ALU.mult))
            dve.wait_ge(S["rk_mm"], 1)
            V.tensor_tensor(bonus, psum[:, 4:8, 0:T], v_, ALU.mult).then_inc(S["pad_ready"], 1)
            dve.wait_ge(S["pad_ready"], 1)
            dve.wait_ge(S["exp_ready"], 1)
            dve.wait_ge(S["store"], 80)
            pr = slice(0, NPR)
            for o in range(2):
                own, other = slice(64 * o, 64 * o + 64), slice(64 - 64 * o, 128 - 64 * o)
                V.memset(Az[other, o::2, :], 0.0)
                V.memset(Rz[other, o::2, :], 0.0)
                V.tensor_tensor(Az[own, o::2, :], px[own, :, pr], kk[own, :, pr], ALU.mult)
                V.tensor_tensor(Rz[own, o::2, :], cs[own, :, pr], r_[own, :, pr], ALU.mult)
            V.tensor_tensor(bb[:, :, pr], bb[:, :, pr], ld[:, :, pr], ALU.mult)
            v(V.tensor_tensor(kh[:, :, pr], kh[:, :, pr], ld[:, :, pr], ALU.mult))
            for c in range(NCH):
                last = V.tensor_copy(PC[:, c, :], cs[:, :, c * CH + CH - 1])
            last.then_inc(S["pad_ready"], 1)
            dve.wait_ge(S["pad_ready"], 2)
            dve.wait_ge(S["svec_out"], 16)
            dve.wait_ge(S["tok_tr"], 1)
            V.memset(Vz[64:128, 0], 0.0)
            V.memset(Vz[0:64, 1], 0.0)
            for t in range(2):
                V.tensor_copy(Vz[0:64, 0, t, :], psum[0:64, 3 * t, :])
                last = V.tensor_copy(Vz[64:128, 1, t, :], psum[64:128, 3 * t, :])
            last.then_inc(S["tok_sb"], 1)

            mod_part(8)

            def wide4(col):
                return K[:, col:col + P].unsqueeze(1).broadcast_to([P, 4, P])

            quad = lambda b: psum[:, b, :].rearrange("p (h t) -> p h t", h=4)
            gram = ((L1, C_LOS), (L1T, C_UPS), (L2T, C_UPS), (R1T, C_UPI), (R2T, C_UPI))
            for t in range(2):
                for m, (dst, mask_) in enumerate(gram):
                    for hh in range(2):
                        g = t * 10 + m * 2 + hh
                        dve.wait_ge(S["gram_mm"], g + 1)
                        V.tensor_tensor(dst[:, 4 * hh:4 * hh + 4, :], quad(g % 4), wide4(mask_), ALU.mult).then_inc(S["gram_sb"], 1)
                dve.wait_ge(S["gram_sb"], t * 10 + 10)
                for hh in range(2):
                    hs = slice(4 * hh, 4 * hh + 4)
                    v(V.tensor_tensor(X[:, hs], L1[:, hs], wide4(C_LV0T), ALU.mult))
                    v(V.tensor_tensor(X[:, hs], wide4(C_ID), X[:, hs], ALU.subtract))
                    v(V.tensor_tensor(Y[:, hs], L1T[:, hs], wide4(C_LV), ALU.mult))
                    V.tensor_tensor(Y[:, hs], wide4(C_ID), Y[:, hs], ALU.subtract).then_inc(S["xy0"], 1)
                    dve.wait_ge(S["xy0"], 2 * t + hh + 1)
                for k in range(1, 6):
                    for hh in range(2):
                        hs = slice(4 * hh, 4 * hh + 4)
                        n = t * 10 + (k - 1) * 2 + hh
                        dve.wait_ge(S["z_mm"], n + 1)
                        V.tensor_tensor(Z[:, hs], quad(4 + hh), wide4(C_LV + k * P), ALU.mult).then_inc(S["z_sb"], 1)
                    for hh in range(2):
                        hs = slice(4 * hh, 4 * hh + 4)
                        n = t * 10 + (k - 1) * 2 + hh
                        dve.wait_ge(S["d_mm"], n + 1)
                        V.tensor_tensor(Y[:, hs], Y[:, hs], quad(2 * hh), ALU.subtract)
                        V.tensor_tensor(X[:, hs], X[:, hs], quad(2 * hh + 1), ALU.subtract).then_inc(S["xy"], 1)
                        dve.wait_ge(S["xy"], n + 1)
                    if (t, k) in ((0, 2), (0, 4), (1, 1)):
                        mod_part({(0, 2): 9, (0, 4): 10, (1, 1): 11}[t, k])
                for c in (2 * t, 2 * t + 1):
                    ps = slice(64 * (c % 2), 64 * (c % 2) + 64)
                    dve.wait_ge(S["rhs_mm"], c + 1)
                    V.tensor_copy(rhs_s[ps, :], psum[ps, 6, :]).then_inc(S["rhs_sb"], 1)
                    dve.wait_ge(S["u_mm"], c + 1)
                    V.tensor_scalar(Uz[ps, c % 2, :], psum[ps, 7, :], -1.0, None, ALU.mult).then_inc(S["u_sb"], 1)
                    dve.wait_ge(S["o_mm"], c + 1)
                    V.tensor_copy(outT[:, :, c * CH:(c + 1) * CH], psum[:, 4, 0:256].rearrange("p (q t) -> p q t", q=QT)).then_inc(S["o_sb"], 1)
                    dve.wait_ge(S["s_mm"], c + 1)
                    s_ps = psum[:, 5, 0:256].rearrange("p (q i) -> p q i", q=QT)
                    if c == 0:
                        v(V.tensor_copy(S0T, s_ps))
                    else:
                        v(V.tensor_tensor(S0T, S0T, s_ps, ALU.add))
                    V.tensor_tensor(S0T, S0T, over(PC[:, c, :], HD), ALU.mult).then_inc(S["s_sb"], 1)
                    dve.wait_ge(S["s_sb"], c + 1)
            dve.wait_ge(S["samp_tr"], 1)
            V.tensor_copy(outT[:, :, NPR:T], psum[:, 1, 0:QT * NSA].rearrange("p (q s) -> p q s", q=QT)).then_inc(S["samp_sb"], 1)
            dve.wait_ge(S["samp_sb"], 1)
            dve.wait_ge(S["o_sb"], NCH)
            dve.wait_ge(S["gn_mm"], 1)
            v(V.scalar_tensor_tensor(outT, psum[:, 0:4, 0:T], -1.0 / HD, outT, ALU.mult, ALU.add))
            V.tensor_tensor(tmp, outT, outT, ALU.mult).then_inc(S["gn_c"], 1)
            dve.wait_ge(S["gn_mm"], 2)
            V.tensor_scalar(tmp, psum[:, 4:8, 0:T], 1.0 / HD, GN_EPS, ALU.mult, ALU.add).then_inc(S["gn_v"], 1)
            dve.wait_ge(S["gn_sd"], 1)
            v(V.reciprocal(tmp, tmp))
            v(V.tensor_tensor(outT, outT, tmp, ALU.mult))
            for q in range(QT):
                last = V.tensor_scalar(outT[:, q], outT[:, q], gn_g[:, q:q + 1], gn_b[:, q:q + 1], ALU.mult, ALU.add)
            v(last)
            v(V.tensor_tensor(outT, outT, bonus, ALU.add))
            V.tensor_tensor(outT, outT, g_t, ALU.mult).then_inc(S["yab_ready"], 1)

            def moe(l):
                if l == 0:
                    dve.wait_ge(S["rwkv_free"], 1)
                g3 = lambda a: a[0:TR]
                dve.wait_ge(S["score_ready"], l + 1)
                v(V.tensor_tensor(g3(sel), g3(score), brout[:, l].unsqueeze(1).broadcast_to([TR, 3, NE]), ALU.add))
                for t in range(3):
                    for g in range(NG):
                        last = V.max(out=gt8[0:TR, t, g, :], in_=sel[0:TR, t, g * 8:(g + 1) * 8])
                v(last)
                v(V.tensor_tensor(g3(grp), gt8[0:TR, :, :, 0], gt8[0:TR, :, :, 1], ALU.add))
                for t in range(3):
                    a = grp[0:TR, t].unsqueeze(1).broadcast_to([TR, NG, NG])
                    b = grp[0:TR, t].unsqueeze(2).broadcast_to([TR, NG, NG])
                    c1, c2 = (c[0:TR, t].rearrange("p (g h) -> p g h", g=NG) for c in (cmp1, cmp2))
                    V.tensor_tensor(c1, a, b, ALU.is_gt)
                    v(V.tensor_tensor(c2, a, b, ALU.is_equal))
                v(V.tensor_tensor(g3(cmp2), g3(cmp2), K[0:TR, C_TRI:C_TRI + 64].unsqueeze(1).broadcast_to([TR, 3, 64]), ALU.mult))
                v(V.tensor_tensor(g3(cmp1), g3(cmp1), g3(cmp2), ALU.add))
                v(V.tensor_reduce(g3(rank), g3(cmp1).rearrange("p t (g h) -> p t g h", g=NG), AX.X, ALU.add))
                v(V.tensor_scalar(g3(gm), g3(rank), float(TOPG), None, ALU.is_lt))
                eg = lambda a: a[0:TR].rearrange("p t (g e) -> p t g e", g=NG)
                v(V.tensor_tensor(eg(selm), eg(sel), over(g3(gm), 8), ALU.mult))
                v(V.tensor_scalar(g3(gm), g3(gm), -1.0, BIG, ALU.add, ALU.mult))
                v(V.tensor_tensor(eg(selm), eg(selm), over(g3(gm), 8), ALU.add))
                for t in range(3):
                    v(V.max(out=top8[0:TR, t, :], in_=selm[0:TR, t, :]))
                    v(V.match_replace(out=rep[0:TR, t, :], in_to_replace=top8[0:TR, t, :], in_values=selm[0:TR, t, :], imm_value=-2 * BIG))
                V.tensor_tensor(g3(mask), g3(rep), g3(selm), ALU.is_lt).then_inc(S["mask_ready"], 1)
                dve.wait_ge(S["mask_ready"], l + 1)
                v(V.tensor_tensor(g3(score), g3(score), g3(mask), ALU.mult))
                v(V.tensor_reduce(csum[0:TR], g3(score), AX.X, ALU.add))
                v(V.reciprocal(csum[0:TR], csum[0:TR]))
                v(V.tensor_scalar(csum[0:TR], csum[0:TR], ROUTE_SCALE, None, ALU.mult))
                V.memset(comb[0:TR, :, NE:NE + 4], 0.0)
                V.memset(posm[0:TR, :, NE:NE + 4], -1.0)
                v(V.tensor_tensor(comb[0:TR, :, 0:NE], g3(score), over(csum[0:TR], NE), ALU.mult))
                dve.wait_ge(S["sh_act"], l + 1)
                dve.wait_ge(S["sh_mm"], 2 * l + 2)
                V.tensor_tensor(shid, ssil, psum[:, 6:8, 0:T], ALU.mult).then_inc(S["sh_hid"], 1)
                dve.wait_ge(S["rank_mm"], l + 1)
                pm = posm[0:TR, :, 0:NE]
                v(V.scalar_tensor_tensor(pm, psum[0:TR, 1, 0:3 * NE].rearrange("p (t e) -> p t e", t=3), 1.0, g3(mask), ALU.add, ALU.mult))
                v(V.tensor_scalar(pm, pm, -1.0, None, ALU.add))
                v(V.tensor_reduce(cmax[0:TR], psum[0:TR, 1, 3 * NE:4 * NE], AX.X, ALU.max))
                for n in range(1, MAXR):
                    v(V.tensor_scalar(cthr[0:TR, n - 1:n], cmax[0:TR], float(CAP * n), None, ALU.is_gt))
                v(V.tensor_reduce(cmax[0:TR], cthr[0:TR, 0:MAXR - 1], AX.X, ALU.add))
                v(V.tensor_scalar(rounds[0:TR, l:l + 1], cmax[0:TR], 1.0, None, ALU.add))
                if l:
                    v(V.tensor_tensor(rounds[0:TR, 1:2], rounds[0:TR, 0:1], rounds[0:TR, 1:2], ALU.add))
                V.memset(gout, 0.0)
                V.memset(selT[3], 0.0)
                V.tensor_copy(nrounds[0:TR, l:l + 1], rounds[0:TR, l:l + 1]).then_inc(S["round_set"], 1)
                dve.wait_ge(S["shd_sb"], 8 * l + 8)
                dve.wait_ge(S["round_set"], l + 1)
                first = dve.value_load(nrounds[0:1, 0:1], min_val=1, max_val=MAXR) if l else 0
                end = dve.value_load(nrounds[0:1, l:l + 1], min_val=1, max_val=(l + 1) * MAXR)
                vl = S["idxf"]

                def choose(j2):
                    iota = K[0:TR, C_IOTA:C_IOTA + CAP].unsqueeze(1).broadcast_to([TR, 2, CAP])
                    for t in range(3):
                        p = posm[0:TR, t, bass.ds(j2, 2)] if not isinstance(j2, int) else posm[0:TR, t, j2:j2 + 2]
                        last = V.tensor_tensor(slotsel[0:TR, t], iota, over(p, CAP), ALU.is_equal)
                    last.then_inc(S["sel"], 1)

                def take_slots(jj, count):
                    dve.wait_ge(S["slot_mm"], count)
                    V.tensor_copy(idxf[:, jj:jj + 1], psum[:, 4, 0:1])
                    V.tensor_copy(wt[0:64, jj:jj + 1], psum[0:64, 4, 2:3])
                    V.tensor_copy(wt[64:128, jj:jj + 1], psum[64:128, 4, 3:4]).then_inc(vl, 1)
                    dve.wait_ge(vl, count)
                    V.tensor_copy(slot_idx[:, jj:jj + 1], idxf[:, jj:jj + 1])
                    V.tensor_scalar(selT[jj], K[:, C_IOTA:C_IOTA + T], idxf[:, jj:jj + 1], None, ALU.is_equal).then_inc(S["idx"], 1)

                def add_back(base):
                    for c in range(DT):
                        dve.wait_ge(S["cb_mm"], base + (c + 1))
                        V.tensor_tensor(yacc[:, c, :], yacc[:, c, :], psum[:, 6 + c % 2, 0:T], ALU.add).then_inc(S["cb_add"], 1)

                with dve.Fori(first, end) as r:
                    for j in range(2):
                        choose(2 * j)
                        take_slots(j, r * 34 + (j + 1))
                    with dve.Fori(0, NTURN) as i:
                        for b in range(EBODY):
                            m1_ = r * NPAIR + i * EBODY + (b + 1)
                            u0_ = r * RU + i * (EBODY * PU) + b * PU
                            choose(i * 8 + (2 * b + 4))
                            take_slots((b + 2) % 4, r * 34 + i * EBODY + (b + 3))
                            dve.wait_ge(S["gsil"], m1_)
                            dve.wait_ge(S["unit_used"], u0_ + 4)
                            dve.wait_ge(S["ht_mm"], m1_ - 1)
                            V.scalar_tensor_tensor(ghid, gsil, wt[:, b:b + 1], psum[:, 1, 0:DE], ALU.mult, ALU.mult).then_inc(S["ghid"], 1)
                            dve.wait_ge(S["cb_add"], r * 264 + i * 32 + 8 * b)
                            add_back(r * 264 + i * 32 + 8 * b)
                            dve.wait_ge(S["unit_used"], u0_ + 6)
                            V.tensor_copy(gout[:, 512:D], psum[:, 3, :]).then_inc(S["os_b"], 1)
                    dve.wait_ge(S["cb_add"], r * 264 + 256)
                    add_back(r * 264 + 256)
                    dve.wait_ge(S["cb_add"], r * 264 + 264)
                    V.memset(selT[3], 0.0)
                    V.tensor_scalar(posm[0:TR, :, :], posm[0:TR, :, :], -float(CAP), None, ALU.add).then_inc(S["next"], 1)
                    dve.wait_ge(S["next"], r + 1)

            def wait_outputs(l):
                dve.wait_ge(S["out_sb"], 8 * (l + 1))

            wait_outputs(0)
            post(1, 0, 0, yacc)
            pre(2, 0, 1)
            moe(0)
            post(3, 0, 1, yacc)
            pre(4, 1, 0)
            vz, uz = z[:, 8:16, :], z[:, 0:8, :]
            dve.wait_ge(S["ws_tr"], 1)
            V.tensor_tensor(wsT.rearrange("p (a g) n -> p a g n", a=2), psum[:, 4:6, :].rearrange("p a (g n) -> p a g n", g=4),
                            upi_full.unsqueeze(1).unsqueeze(1).broadcast_to([P, 2, 4, P]), ALU.mult).then_inc(S["ws_sb"], 1)
            dve.wait_ge(S["z_sb1"], 16)
            dve.wait_ge(S["vmu_mm"], 1)
            v(V.tensor_scalar(mu_b, psum[:, 6, 0:T], 1.0 / D, None, ALU.mult))
            v(V.tensor_tensor(vz, vz, mu_b.unsqueeze(1).broadcast_to([P, 8, T]), ALU.subtract))
            V.tensor_tensor(gt1, vz, vz, ALU.mult).then_inc(S["vc_ready"], 1)
            dve.wait_ge(S["vvar_mm"], 1)
            V.tensor_scalar(rstd[:, :], psum[:, 7, 0:T], 1.0 / D, EPS, ALU.mult, ALU.add).then_inc(S["ln_var"], 1)
            dve.wait_ge(S["ln_sd"], 1)
            v(V.reciprocal(rstd[:, :], rstd[:, :]))
            v(V.tensor_tensor(vz, vz, wide(), ALU.mult))
            for g in range(8):
                last = V.tensor_scalar(vz[:, g], vz[:, g], ln_g[:, g:g + 1], ln_b[:, g:g + 1], ALU.mult, ALU.add)
            last.then_inc(S["v_ready"], 1)
            dve.wait_ge(S["v_ready"], 1)
            dve.wait_ge(S["gmisc_in"], 32)
            for g in range(8):
                last = V.tensor_scalar(gt2[:, g, NPR:T], vz[:, g, NPR:T], ws00[:, g:g + 1], bsb[:, g, 0:1], ALU.mult, ALU.add)
            v(last)
            for t in range(2):
                dve.wait_ge(S["sg_mm"], t + 1)
                for a in range(2):
                    v(V.tensor_tensor(gt2[:, 4 * a:4 * a + 4, t * P:(t + 1) * P], psum[:, 2 * t + a, :].rearrange("p (g n) -> p g n", g=4), bsb[:, 4 * a:4 * a + 4, :], ALU.add))
            V.tensor_tensor(uz, uz, gt2, ALU.mult).then_inc(S["sg_ready"], 1)
            wait_outputs(1)
            post(5, 1, 0, gt1)
            pre(6, 1, 1)
            moe(1)
            post(7, 1, 1, yacc)


_INS = ['x_prompt', 'x_sample', 'c_prompt', 'c_sample', 'state_conv', 'state_shift', 'state_wkv', 'w_mod', 'b_mod', 'norm_g',
        'ab_w_in', 'ab_conv_w', 'ab_mu', 'ab_w0', 'ab_w_decay_up', 'ab_a0', 'ab_a_up', 'ab_g_up', 'ab_k_k', 'ab_k_a', 'ab_r_k',
        'ab_gn_g', 'ab_gn_b', 'ab_w_out', 'gm_w_in', 'gm_b_in', 'gm_ln_g', 'gm_ln_b', 'gm_w_s', 'gm_b_s', 'gm_w_out',
        'moe_w_router', 'moe_b_router', 'moe_w_gate', 'moe_w_up', 'moe_w_down', 'moe_ws_gate', 'moe_ws_up', 'moe_ws_down']
_OUTS = [(1, NPR, D), (NSA, 1, D), (1, 1, 2, DA), (1, NSA, 2, DA), (1, 1, PB), (1, NSA, PB), (1, 1, H, HD, HD), (1, NSA, H, HD, HD), (1, NSA, 1, D)]


def kernel(**inputs):
    import concourse.bacc as _bacc
    from concourse.bass_utils import run_bass_kernel_spmd as _run

    nc = _bacc.Bacc("TRN2", target_bir_lowering=False, num_devices=1)
    arrays, ins, outs = {}, [], []
    for name in _INS:
        a = np.ascontiguousarray(inputs[name])
        arrays[f"in_{name}"] = a
        ins.append(nc.dram_tensor(f"in_{name}", a.shape, F32, kind="ExternalInput").ap())
    arrays["shape_constants"] = shape_constants()
    ins.append(nc.dram_tensor("shape_constants", (P, NCONST), F32, kind="ExternalInput").ap())
    for i, shape in enumerate(_OUTS):
        outs.append(nc.dram_tensor(f"out_{i}_dram", shape, F32, kind="ExternalOutput").ap())
    build(nc, ins, outs)
    r = _run(nc, [arrays], core_ids=[0])
    return tuple(r.results[0][f"out_{i}_dram"] for i in range(len(_OUTS)))
```

```python
from contextlib import ExitStack

import numpy as np

import concourse.bass as bass
from concourse import mybir

F32 = mybir.dt.float32
ALU = mybir.AluOpType
ACT = mybir.ActivationFunctionType
AX = mybir.AxisListType

P = 128
D = 1024
DT = D // P
NPR, NSA = 256, 8
T = NPR + NSA
NSEQ = 1 + NSA
DA = DB = 512
H, HD = 8, 64
QT = DB // P
PB = 3 * DB + 256
PBT = PB // P
PROJ = 3 * DA + PB
PROJT = PROJ // P
CH = 64
NCH = NPR // CH
NE, DE = 64, 256
TOPK, NG, TOPG = 8, 8, 4
TR = T // 3
EPS, GN_EPS = 1e-6, 64e-5
ROUTE_SCALE = 2.5
BIG = 1e30
EMH = float(np.exp(-0.5))
GELU_C = float(np.sqrt(2.0 / np.pi))

NSMALL = 20
UNIT = 2048
MSLOTS = 5
ESLOTS = 12
CAP = 64
MAXR = -(-T // CAP)
MOD_FIRST = 4
PROJ_ORDER = [12, 6, 7, 8, 9, 10, 11, 0, 1, 4, 5, 2, 3]
PROJ_TILE = [2 * u + i for u in PROJ_ORDER for i in range(2)]
MOD_PROJ = [[MOD_FIRST + u] for u in range(13)]
MOD_LATE = MOD_FIRST + sum(len(x) for x in MOD_PROJ)
NPAIR = NE // 2
EBODY = 4
NTURN = NPAIR // EBODY
PU = 6
RU = NPAIR * PU

C_ID, C_ONE, C_BLK, C_UPS, C_UPI, C_LOS, C_LV0T, C_LV, C_S4 = 0, 128, 256, 384, 512, 640, 768, 896, 896 + 6 * 128
C_TRI = C_S4 + NSEQ
C_IOTA = C_TRI + 64
C_TOK = C_IOTA + T
C_UPT = C_TOK + 3
C_UPF = C_UPT + P
NCONST = C_UPF + P


def shape_constants():
    c = np.zeros((P, NCONST), np.float32)
    i = np.arange(P)
    same = (i[:, None] // CH) == (i[None, :] // CH)
    c[:, C_ID:C_ID + P] = np.eye(P)
    c[:, C_ONE:C_ONE + P] = 1.0
    c[:, C_BLK:C_BLK + P] = same
    c[:, C_UPS:C_UPS + P] = same & (i[:, None] < i[None, :])
    c[:, C_UPI:C_UPI + P] = same & (i[:, None] <= i[None, :])
    c[:, C_LOS:C_LOS + P] = same & (i[:, None] > i[None, :])
    for k in range(6):
        b = 1 << k
        m = ((i[:, None] // (2 * b)) == (i[None, :] // (2 * b))) & (i[:, None] // b % 2 == 0) & (i[None, :] // b % 2 == 1)
        c[:, C_LV + k * P:C_LV + (k + 1) * P] = m
        if k == 0:
            c[:, C_LV0T:C_LV0T + P] = m.T
    for j in range(4):
        for s in range(NSEQ):
            c[32 * j + s, C_S4 + s] = 1.0
    g = np.arange(8)
    c[:, C_TRI:C_TRI + 64] = (g[None, :] < g[:, None]).reshape(1, 64)
    c[:, C_IOTA:C_IOTA + T] = np.arange(T)
    c[:, C_TOK:C_TOK + 3] = i[:, None] + TR * np.arange(3)[None, :]
    c[:, C_UPF:C_UPF + P] = i[:, None] <= i[None, :]
    c[:, C_UPT:C_UPT + P] = i[:, None] < i[None, :]
    return c


def build(nc, ins, outs):
    (x_prompt, x_sample, c_prompt, c_sample, state_conv, state_shift, state_wkv, w_mod, b_mod, norm_g,
     ab_w_in, ab_conv_w, ab_mu, ab_w0, ab_w_decay_up, ab_a0, ab_a_up, ab_g_up, ab_k_k, ab_k_a, ab_r_k,
     ab_gn_g, ab_gn_b, ab_w_out, gm_w_in, gm_b_in, gm_ln_g, gm_ln_b, gm_w_s, gm_b_s, gm_w_out,
     moe_w_router, moe_b_router, moe_w_gate, moe_w_up, moe_w_down, moe_ws_gate, moe_ws_up, moe_ws_down,
     constants) = ins
    (y_prompt, y_sample, conv_p, conv_s, shift_p, shift_s, wkv_p, wkv_s, chunk_v_s) = outs
    vec_scratch = nc.dram_tensor("vec_scratch", (NSA, 6, DB), F32).ap()
    out_scratch = nc.dram_tensor("out_scratch", (NSA * H, HD), F32).ap()

    with ExitStack() as ctx:
        def sb(name, shape):
            return ctx.enter_context(nc.sbuf_tensor(name, shape, F32))

        def sem(name):
            return ctx.enter_context(nc.semaphore(name))

        ring = sb("ring", [P, ESLOTS, UNIT])
        arena = sb("arena", [P, 17600])
        xT = sb("xT", [P, DT, T])
        hT = sb("hT", [P, DT, T])
        K = sb("K", [P, NCONST])
        mod = sb("mod", [P, 2, 6, DT, NSEQ])
        b_modT = sb("b_modT", [P, 2, 6, DT])
        ngT = sb("ngT", [P, 2, 4, DT])
        lora = sb("lora", [P, DB])
        gup = sb("gup", [P, DB])
        router = sb("router", [P, 2, DT, NE])
        brout = sb("brout", [TR, 2, NE])
        vecs = sb("vecs", [P, 64])
        gvec = sb("gvec", [P, 16 + 8 + 8 + 8])
        rstd = sb("rstd", [P, T])
        eps = sb("eps", [P, 2])
        psum = ctx.enter_context(nc.psum_tensor("psum", [P, 8, 512], F32))

        ident = K[:, C_ID:C_ID + P]
        ones = K[:, C_ONE:C_ONE + P]
        blk = K[:, C_BLK:C_BLK + P]
        conv_w, mu = vecs[:, 0:12].rearrange("p (w q) -> p w q", w=3), vecs[:, 12:26]
        w0, a0, k_k, k_a = vecs[:, 26:30], vecs[:, 30:34], vecs[:, 34:38], vecs[:, 38:42]
        r_k, gn_g, gn_b = vecs[:, 42:46], vecs[:, 46:50], vecs[:, 50:54]
        gb_in, ln_g, ln_b, ws00 = gvec[:, 0:16], gvec[:, 16:24], gvec[:, 24:32], gvec[:, 32:40]

        class Arena:
            def __init__(self, base, size):
                self.base, self.at, self.size = base, 0, size

            def take(self, *shape):
                n = int(np.prod(shape))
                v = self.base[:, self.at:self.at + n]
                self.at += n
                assert self.at <= self.size, self.at
                if len(shape) == 2:
                    v = v.rearrange("p (a b) -> p a b", a=shape[0])
                if len(shape) == 3:
                    v = v.rearrange("p (a b c) -> p a b c", a=shape[0], b=shape[1])
                return v

        st = Arena(arena, 17600)
        xtok = st.take(3, D)
        ctok = st.take(D)
        ctok2 = st.take(D)
        cT = ring[:, 5, 0:DT * 32].rearrange("p (c s) -> p c s", c=DT)
        mrow = ring[:, 5, 512:512 + D]

        m0 = Arena(arena, 17600)
        proj = m0.take(PROJT, T)
        xm = m0.take(PBT, T)
        kh, bb, bonus, tmp = (m0.take(QT, T) for _ in range(4))
        Uz = m0.take(2, 512)
        rhs_s = m0.take(512)
        S0T = m0.take(QT, HD)
        s_tmp = m0.take(16, HD)
        side_mem = sb("side_mem", [P, 16 + 2 * HD + 6 * HD])
        PC = side_mem[:, 0:16].rearrange("p (c q) -> p c q", c=NCH)
        s_u, s_o = side_mem[:, 16:80], side_mem[:, 80:144]
        svec = side_mem[:, 144:528].rearrange("p (v j) -> p v j", v=6)
        a_sig = proj[:, 0:4, :]
        kk = proj[:, 4:8, :]
        g_t = proj[:, 8:12, :]
        pb = proj[:, 12:26, :]
        ld = proj[:, 12:16, :]
        cs = proj[:, 16:20, :]
        px = proj[:, 20:24, :]
        r_, k_, v_ = xm[:, 0:4, :], xm[:, 4:8, :], xm[:, 8:12, :]
        flat = lambda a, b: arena[:, a * T:b * T]
        Lmat = flat(12, 26)[:, 0:3072].rearrange("p (m h t) -> p m h t", m=3, h=H)
        L1, L1T, L2T = Lmat[:, 0], Lmat[:, 1], Lmat[:, 2]
        Rmat = flat(0, 8)[:, 0:2048].rearrange("p (m h t) -> p m h t", m=2, h=H)
        R1T, R2T = Rmat[:, 0], Rmat[:, 1]
        XY = flat(26, 34)[:, 0:2048].rearrange("p (m h t) -> p m h t", m=2, h=H)
        X = XY[:, 0]
        Y = (XY[:, 1], flat(52, 56)[:, 0:1024].rearrange("p (h t) -> p h t", h=H))
        Z = flat(34, 38)[:, 0:1024].rearrange("p (h t) -> p h t", h=H)
        hi = Arena(ring[:, 8:12, :].rearrange("p s n -> p (s n)"), 8192)
        Az, Rz = hi.take(H, NPR), hi.take(H, NPR)
        Vz = hi.take(2, 2, 512)
        Btok, Ktok = hi.take(2, 512), hi.take(2, 512)
        sh_in = ring[0:NSA, 8, 0:PB]
        cv_in = ring[0:NSA, 9, 0:2 * DA].rearrange("p (w n) -> p w n", w=2)
        hi2 = Arena(ring[:, 8:12, :].rearrange("p s n -> p (s n)"), 8192)
        conv_in, conv_t = hi2.take(12, T), hi2.take(QT, T)
        sh_out = ring[0:NSEQ, 10, 256:256 + PB]
        cv_out = s_tmp[0:10].rearrange("p i j -> p (i j)")[:, 0:DA]
        stT = sb("stT", [P, 176])
        st_shift = stT[:, 0:112].rearrange("p (q s) -> p q s", q=PBT)
        st_conv = stT[:, 112:176].rearrange("p (w q s) -> p w q s", w=2, q=QT)
        upi_full = K[:, C_UPF:C_UPF + P]
        wkv_o = flat(34, 38)[:, 0:512].rearrange("p (h j) -> p h j", h=H)
        S_s = ring[0:64, 6:8, :].rearrange("p s (i j) -> p (s i) j", j=HD)
        outT = hT[:, 4:8, :]

        def squares(k):
            return arena[:, 12 * T:20 * T].rearrange("p (c t) -> p c t", c=DT) if k == 1 else hT

        y_a = hT[:, 0:4, :]

        m1 = Arena(arena, 17600)
        z = m1.take(16, T)
        gt1, gt2 = m1.take(8, T), m1.take(8, T)
        vtok = m1.take(2, D)
        wsn = m1.take(8, P)
        wsT = m1.take(8, P)
        bsb = m1.take(8, P)
        vs_out = m1.take(D)
        mu_b = m1.take(T)

        me = Arena(arena, 17600)
        yacc = me.take(DT, T)
        xg = [me.take(DT, P) for _ in range(2)]
        xgT = [me.take(DT, P) for _ in range(2)]
        slotsel = me.take(3, 2, CAP)
        selT = [me.take(T) for _ in range(4)]
        wt = me.take(4)
        idxf = me.take(4)
        gsil, ghid = me.take(DE), me.take(DE)
        ghT = me.take(2, P)
        gout = me.take(D)
        posm = me.take(3, NE + 4)
        comb = me.take(3, NE + 4)
        me_keep = me.at
        htok = me.take(3, D)
        score, sel, selm, rep, mask = (me.take(3, NE) for _ in range(5))
        gt8 = me.take(3, NG, 8)
        grp, rank, gm = me.take(3, NG), me.take(3, NG), me.take(3, NG)
        cmp1, cmp2 = me.take(3, 64), me.take(3, 64)
        top8 = me.take(3, 8)
        csum, cmax, cthr = me.take(3), me.take(1), me.take(4)
        ssil, shid = me.take(2, T), me.take(2, T)
        mx = Arena(arena, 17600)
        mx.take(DT, T)
        xo = mx.take(3, D)

        S = {}

        def signals(*names):
            for n in names:
                S[n] = sem(n)

        signals("const_in", "const2_in", "h_act", "sq_act", "norm_half", "x_in", "c_in", "small_in", "state_in", "swkv_in", "gmisc_in", "store", "vec", "act", "st_sb", "conv_out", "conv_done", "zeros", "shift_out", "modp_in", "pool_step", "x_tr", "x_sb", "silu_c", "c_tr", "c_sb", "mod_mm", "mod_row", "mod_tr", "mod_set",
                "sq_ready", "ss_mm", "sd_ready", "h_ready", "proj_mm", "proj_sb", "st_tr",
                "tail_ready", "tail_tr", "tail_sb", "mixed", "lora_in", "lora_mm", "lora_sb", "cs_ready",
                "exp_ready", "kksq_ready", "kkss_mm", "kknorm", "rk_ready", "rk_mm", "pad_ready", "tok_tr", "tok_sb",
                "gram_mm", "gram_sb", "xy0", "z_mm", "z_sb", "d_mm", "xy", "rhs_mm", "rhs_sb", "u_mm", "u_sb",
                "o_mm", "o_sb", "s_mm", "s_sb", "svec_tr", "svec_sb", "svec_out", "svec_in", "samp_out", "samp_in",
                "samp_tr", "samp_sb", "wkv_tr", "wkv_sb", "gn_mm", "gn_c", "gn_sd", "yab_ready",
                "out_mm", "out_sb", "y_done", "rwkv_free", "z_mm1", "z_sb1", "vmu_mm", "vc_ready", "vvar_mm",
                "v_ready", "ln_sd", "ws_tr", "ws_sb", "vt_tr", "vt_sb", "vs_sb", "sg_mm", "sg_ready",
                "logit_mm", "score_ready", "mask_ready", "rank_mm", "htr_mm", "htr_sb", "htok_out",
                "sh_mm", "sh_act", "sh_hid", "shd_mm", "shd_sb", "vs_stored", "gather_go", "fin_tr", "fin_sb")
        signals("round_set", "sel", "slot_mm", "idx", "gat_a", "gat_b", "xt_mm", "xt_sb", "gsil", "ghid",
                "ht_mm", "ht_sb", "os_a", "os_b", "cb_mm", "cb_add", "unit_used", "idxf", "next")
        mload = [sem(f"mload{i}") for i in range(MSLOTS)]
        eload = [sem(f"eload{i}") for i in range(ESLOTS)]
        h_rows = [nc.dram_tensor(f"h_rows{l}", (T, D), F32).ap() for l in range(2)]
        nrounds = ctx.enter_context(nc.sbuf_tensor("nrounds", [P, 2], mybir.dt.int32))
        rounds = sb("rounds", [P, 2])
        slot_idx = ctx.enter_context(nc.sbuf_tensor("slot_idx", [P, 4], mybir.dt.uint32))
        so_tok = s_tmp[0:NSA].rearrange("p i j -> p (i j)")[:, 0:DB]

        def gram_bank(g):
            return g % 4 if g < 4 or 10 <= g < 14 else 4 + g % 2 if g < 10 else 4 + g % 4

        svec_tok = ring[0:NSA, 10:12, :].rearrange("p s n -> p (s n)")[:, 256:256 + 6 * DB].rearrange("p (v n) -> p v n", v=6)

        mix_units, mod_unit, proj_unit = [], [], []
        wm = w_mod.rearrange("l (p c) n -> l p c n", c=DT)
        wi = ab_w_in[0].rearrange("(p c) n -> p c n", c=DT)

        def half_units(k):
            for u in (2 * k, 2 * k + 1):
                mod_unit.append(len(mix_units))
                mix_units.append(("mod", wm[u // 24, :, :, u % 24 * 256:(u % 24 + 1) * 256], DT))

        for k in range(MOD_FIRST):
            half_units(k)
        for u in range(PROJT // 2):
            proj_unit.append(len(mix_units))
            mix_units.append(("proj", wi[:, :, PROJ_ORDER[u] * 256:(PROJ_ORDER[u] + 1) * 256], DT))
            for k in MOD_PROJ[u]:
                half_units(k)
        for k in range(MOD_LATE, 24):
            half_units(k)
        U_ABO = len(mix_units)
        wo = ab_w_out[0].rearrange("(q p) n -> p q n", p=P)
        for u in range(4):
            mix_units.append(("abo", wo[:, 2 * u:2 * u + 2, :], 2))

        def shared_units(l):
            mix_units.append(("shg", moe_ws_gate[l].rearrange("(p c) f -> p c f", c=DT), DT))
            mix_units.append(("shu", moe_ws_up[l].rearrange("(p c) f -> p c f", c=DT), DT))
            mix_units.append(("shd", moe_ws_down[l].rearrange("(p j) n -> p j n", j=2), 2))

        shared_units(0)
        N0 = len(mix_units)
        gi = gm_w_in[0].rearrange("(p c) n -> p c n", c=DT)
        for u in (4, 5, 6, 7, 0, 1, 2, 3):
            mix_units.append(("gmi", gi[:, :, u * 256:(u + 1) * 256], DT))
        go = gm_w_out[0].rearrange("(q p) n -> p q n", p=P)
        for u in range(4):
            mix_units.append(("gmo", go[:, 2 * u:2 * u + 2, :], 2))
        shared_units(1)
        N1 = len(mix_units)
        U_GMI, U_GMO = N0, N0 + 8
        U_SH = (N0 - 3, N1 - 3)

        def mix_view(n):
            kind, src, a = mix_units[n]
            return ring[:, n % MSLOTS, :].rearrange("p (a n) -> p a n", a=a)

        def eslot(j):
            return (j + PU) % ESLOTS

        block = ctx.enter_context(nc.Block())

        @block.sync
        def _(sp):
            def load(dst, src, s):
                sp.dma_start(dst, src).then_inc(S[s], 16)

            load(ctok[0:1, :], c_prompt, "c_in")
            load(ctok[1:NSEQ, :], c_sample, "c_in")
            load(K[:, 0:C_BLK], constants[:, 0:C_BLK], "const_in")
            load(K[:, C_S4:C_TRI], constants[:, C_S4:C_TRI], "const_in")

            def wait_used(n):
                kind, l = mix_units[n][0], int(n >= N0)
                if kind == "mod":
                    sp.wait_ge(S["mod_mm"], mod_unit.index(n) + 1)
                elif kind == "proj":
                    sp.wait_ge(S["proj_mm"], 2 * (proj_unit.index(n) + 1))
                elif kind == "gmi":
                    sp.wait_ge(S["z_mm1"], 2 * (n - U_GMI + 1))
                elif kind in ("abo", "gmo"):
                    sp.wait_ge(S["out_mm"], 8 * (l + 1))
                elif kind in ("shg", "shu"):
                    sp.wait_ge(S["sh_mm"], 2 * l + (1 if kind == "shg" else 2))
                else:
                    sp.wait_ge(S["shd_mm"], 8 * (l + 1))

            def mix_load(n):
                if n >= MSLOTS:
                    wait_used(n - MSLOTS)
                sp.dma_start(mix_view(n), mix_units[n][1]).then_inc(mload[n % MSLOTS], 16)

            for n in range(2):
                mix_load(n)
            load(xtok[:, 0:2, :], x_prompt[0].rearrange("(t p) d -> p t d", p=P), "x_in")
            load(xtok[0:NSA, 2, :], x_sample[:, 0, :], "x_in")
            for n in range(2, 12):
                mix_load(n)
            load(K[:, C_BLK:C_S4], constants[:, C_BLK:C_S4], "const2_in")
            load(K[:, C_TRI:NCONST], constants[:, C_TRI:NCONST], "const2_in")
            load(sh_in, state_shift[0], "state_in")
            load(cv_in, state_conv[0], "state_in")
            load(S_s, state_wkv[0].rearrange("b h i j -> (b h) i j"), "swkv_in")
            for n in range(12, N0):
                mix_load(n)

            def expert_load(l, pair2, j):
                sp.dma_start(ring[:, eslot(j), :], expert_src(l, pair2 + (j // PU * 2 + j % 2), j % PU // 2)).then_inc(eload[eslot(j)], 16)

            def first_pair(l):
                for j in range(PU):
                    expert_load(l, 0, j)

            def experts(l, last):
                if l == 0:
                    sp.wait_ge(S["rwkv_free"], 1)
                    sp.wait_ge(S["wkv_sb"], 1)
                    first_pair(0)
                for n, j in sorted((last - 1 - ((last - 1 - j) % MSLOTS), j) for j in range(MSLOTS)):
                    wait_used(n)
                    expert_load(l, 0, PU + j)
                expert_load(l, 0, PU + MSLOTS)
                sp.wait_ge(S["round_set"], l + 1)
                first = sp.value_load(nrounds[0:1, 0:1], min_val=1, max_val=MAXR) if l else 0
                end = sp.value_load(nrounds[0:1, l:l + 1], min_val=1, max_val=(l + 1) * MAXR)
                with sp.Fori(first, end) as r:
                    with sp.Fori(0, RU // ESLOTS - 1) as i:
                        for j in range(ESLOTS):
                            sp.wait_ge(S["unit_used"], r * RU + i * ESLOTS + (j + 1))
                            expert_load(l, (i + 1) * 4, j)
                    with sp.If(r + 1 < end):
                        for j in range(ESLOTS):
                            sp.wait_ge(S["unit_used"], r * RU + (RU - ESLOTS) + (j + 1))
                            expert_load(l, 0, j)

                if l == 0:
                    sp.wait_ge(S["unit_used"], end * RU)

            def expert_src(l, e, kind):
                w = (moe_w_gate, moe_w_up, moe_w_down)[kind]
                src = w[l, e] if isinstance(e, int) else w[l, bass.ds(e, 1)].rearrange("o a b -> (o a) b")
                return src.rearrange("(p c) n -> p (c n)", p=P)

            experts(0, N0)
            for n in range(N0, N1):
                if n == N0 + MSLOTS:
                    first_pair(1)
                mix_load(n)
            experts(1, N1)

        @block.gpsimd
        def _(pool):
            def load(dst, src, s):
                pool.dma_start(dst, src).then_inc(S[s], 16)

            with nc.allow_non_contiguous_dma(reason="small vectors"):
                load(b_modT[:, :, :, :].rearrange("p l a c -> p (l a) c"), b_mod.rearrange("l (a p c) -> p (l a) c", a=6, c=DT), "modp_in")
                load(ngT[:, :, :, :].rearrange("p l a c -> p (l a) c"), norm_g.rearrange("l a (p c) -> p (l a) c", c=DT), "modp_in")
                pool.wait_ge(S["mod_mm"], 2 * MOD_FIRST)
                load(conv_w, ab_conv_w[0].rearrange("w (q p) -> p w q", p=P), "small_in")
                load(mu, ab_mu[0].rearrange("(q p) -> p q", p=P), "small_in")
                for dst, src in ((w0, ab_w0), (a0, ab_a0), (k_k, ab_k_k), (k_a, ab_k_a), (gn_g, ab_gn_g), (gn_b, ab_gn_b)):
                    load(dst, src[0].rearrange("(q p) -> p q", p=P), "small_in")
                load(r_k, ab_r_k[0].rearrange("(q a) j -> (a j) q", a=2), "small_in")
                load(lora[0:64, :], ab_w_decay_up[0], "small_in")
                load(lora[64:128, :], ab_a_up[0], "small_in")
                load(gup[:, :], ab_g_up[0], "small_in")
                for l in range(2):
                    load(router[:, l], moe_w_router[l].rearrange("(p c) n -> p c n", c=DT), "small_in")
                    load(brout[:, l], moe_b_router[l].partition_broadcast(TR), "small_in")
                load(gb_in, gm_b_in[0].rearrange("(q p) -> p q", p=P), "small_in")
                load(ln_g, gm_ln_g[0].rearrange("(q p) -> p q", p=P), "small_in")
                load(ln_b, gm_ln_b[0].rearrange("(q p) -> p q", p=P), "small_in")
                load(ws00, gm_w_s[0, :, 0, 0].partition_broadcast(P), "small_in")

                pool.wait_ge(S["state_in"], 32)
                pool.dma_start(conv_s[0, :, 0, :], cv_in[:, 1, :]).then_inc(S["conv_out"], 16)
                pool.wait_ge(S["tail_sb"], 1)
                pool.dma_start(shift_p[0], sh_out[0:1, :]).then_inc(S["shift_out"], 16)
                pool.dma_start(shift_s[0], sh_out[1:NSEQ, :]).then_inc(S["shift_out"], 16)

                pool.wait_ge(S["conv_done"], 1)
                pool.wait_ge(S["tail_tr"], 2)
                for o in range(2):
                    other = slice(64 - 64 * o, 128 - 64 * o)
                    nc.gpsimd.memset(Az[other, o::2, :], 0.0).then_inc(S["zeros"], 1)
                    nc.gpsimd.memset(Rz[other, o::2, :], 0.0).then_inc(S["zeros"], 1)

                pool.wait_ge(S["svec_sb"], 1)
                pool.dma_start(vec_scratch, svec_tok).then_inc(S["svec_out"], 16)
                pool.wait_ge(S["svec_out"], 16)
                nc.gpsimd.memset(Vz[64:128, 0], 0.0).then_inc(S["zeros"], 1)
                nc.gpsimd.memset(Vz[0:64, 1], 0.0).then_inc(S["zeros"], 1)
                for b in range(NSA):
                    pool.dma_start(svec[8 * b:8 * b + 8], vec_scratch[b].rearrange("v (h j) -> h v j", j=HD)).then_inc(S["svec_in"], 16)
                pool.wait_ge(S["tail_sb"], 2)
                pool.dma_start(conv_p[0, 0], cv_out[0:2, :]).then_inc(S["store"], 16)
                pool.dma_start(conv_s[0, :, 1, :], cv_out[2:10, :]).then_inc(S["store"], 16)
            pool.wait_ge(S["store"], 32)
            pool.wait_ge(S["svec_in"], 16 * NSA)
            pool.wait_ge(S["swkv_in"], 16)

            n = [0]

            def step(i):
                n[0] += 1
                i.then_inc(S["pool_step"], 1)
                pool.wait_ge(S["pool_step"], n[0])

            r_v, w_v, k_v, v_v, kk_v, b_v = (svec[0:64, i, :] for i in range(6))
            rows = lambda v, i0: v.unsqueeze(1).broadcast_to([64, 16, HD])
            cols = lambda v, i0: v[:, i0:i0 + 16].unsqueeze(2).broadcast_to([64, 16, HD])
            t = s_tmp[0:64]

            def row_sums(out):
                for n in (32, 16, 8, 4, 2):
                    step(nc.gpsimd.tensor_tensor(t[:, :, 0:n], t[:, :, 0:n], t[:, :, n:2 * n], ALU.add))
                step(nc.gpsimd.tensor_tensor(out, t[:, :, 0], t[:, :, 1], ALU.add))

            for i0 in range(0, HD, 16):
                Sp = S_s[:, i0:i0 + 16, :]
                step(nc.gpsimd.tensor_tensor(t, Sp, rows(kk_v, i0), ALU.mult))
                row_sums(s_u[0:64, i0:i0 + 16])
                step(nc.gpsimd.tensor_tensor(Sp, Sp, rows(w_v, i0), ALU.mult))
                step(nc.gpsimd.tensor_tensor(t, cols(s_u[0:64], i0), rows(b_v, i0), ALU.mult))
                step(nc.gpsimd.tensor_tensor(Sp, Sp, t, ALU.subtract))
                step(nc.gpsimd.tensor_tensor(t, cols(v_v, i0), rows(k_v, i0), ALU.mult))
                step(nc.gpsimd.tensor_tensor(Sp, Sp, t, ALU.add))
                step(nc.gpsimd.tensor_tensor(t, Sp, rows(r_v, i0), ALU.mult))
                row_sums(s_o[0:64, i0:i0 + 16])
            pool.dma_start(wkv_s[0].rearrange("b h i j -> (b h) i j"), S_s).then_inc(S["store"], 16)
            pool.dma_start(out_scratch, s_o[0:64, :]).then_inc(S["samp_out"], 16)
            pool.wait_ge(S["samp_out"], 16)
            pool.dma_start(so_tok, out_scratch.rearrange("(b h) i -> b (h i)", h=H)).then_inc(S["samp_in"], 16)
            pool.wait_ge(S["store"], 48)
            pool.wait_ge(S["wkv_sb"], 1)
            pool.dma_start(wkv_p[0, 0].rearrange("h i j -> i h j"), wkv_o[0:64]).then_inc(S["store"], 16)
            pool.wait_ge(S["store"], 64)
            pool.wait_ge(S["s_sb"], NCH)
            pool.sem_inc(S["rwkv_free"], 1)

            def moe(l):
                pool.wait_ge(S["htr_sb"], 6 * l + 6)
                pool.dma_start(h_rows[l].rearrange("(t p) d -> p t d", p=TR), htok[0:TR]).then_inc(S["htok_out"], 16)
                pool.wait_ge(S["htok_out"], 16 * (l + 1))
                pool.wait_ge(S["round_set"], l + 1)
                first = pool.value_load(nrounds[0:1, 0:1], min_val=1, max_val=MAXR) if l else 0
                end = pool.value_load(nrounds[0:1, l:l + 1], min_val=1, max_val=(l + 1) * MAXR)

                def gather(jj, count):
                    pool.wait_ge(S["idx"], count)
                    pool.sem_inc(S["gather_go"], 1)
                    pool.indirect_dma_start(xg[jj % 2].rearrange("p c d -> p (c d)"), None, h_rows[l],
                                            bass.IndirectOffsetOnAxis(slot_idx[:, jj:jj + 1], 0)).then_inc(S["gat_" + "ab"[jj % 2]], 16)

                def first_pairs(r):
                    for j in range(2):
                        if not isinstance(r, int):
                            pool.wait_ge(S["xt_mm"], r * 66)
                        gather(j, r * 34 + (j + 1))

                first_pairs(first)
                with pool.Fori(first, end) as r:
                    with pool.Fori(0, NTURN) as i:
                        for b in range(EBODY):
                            pool.wait_ge(S["xt_mm"], r * 66 + i * 8 + (2 * b + 2))
                            gather((b + 2) % 4, r * 34 + i * EBODY + (b + 3))
                    with pool.If(r + 1 < end):
                        first_pairs(r + 1)

            moe(0)
            pool.wait_ge(S["y_done"], 2)
            pool.dma_start(wsn, gm_w_s[0].rearrange("g i j -> i g j")).then_inc(S["gmisc_in"], 16)
            pool.dma_start(bsb, gm_b_s[0].partition_broadcast(P)).then_inc(S["gmisc_in"], 16)
            pool.wait_ge(S["vs_sb"], 1)
            pool.dma_start(chunk_v_s[0, :, 0, :], vs_out[0:NSA, :]).then_inc(S["store"], 16)
            pool.wait_ge(S["store"], 80)
            pool.sem_inc(S["vs_stored"], 1)
            moe(1)
            pool.wait_ge(S["fin_sb"], 6)
            pool.dma_start(y_prompt[0, 0:2 * TR, :].rearrange("(t p) d -> p t d", p=TR), xo[0:TR, 0:2, :]).then_inc(S["store"], 16)
            pool.dma_start(y_prompt[0, 2 * TR:NPR, :], xo[0:NPR - 2 * TR, 2, :]).then_inc(S["store"], 16)
            pool.dma_start(y_sample[:, 0, :], xo[NPR - 2 * TR:TR, 2, :]).then_inc(S["store"], 16)
            pool.wait_ge(S["store"], 128)
            pool.wait_ge(S["conv_out"], 16)
            pool.wait_ge(S["shift_out"], 32)

        @block.tensor
        def _(pe):
            def mm(out, lhsT, rhs, start=True, stop=True):
                return nc.tensor.matmul(out, lhsT, rhs, start=start, stop=stop)

            def tr(out, in_):
                return nc.tensor.transpose(out, in_, ident[0:in_.shape[0], 0:in_.shape[0]])

            def arrived(n):
                pe.wait_ge(mload[n % MSLOTS], 16 * (n // MSLOTS + 1))

            def sum_squares(k):
                for c in range(DT):
                    pe.wait_ge(S["sq_ready"], DT * k + c + 1)
                    last = mm(psum[:, 7, 0:T], ones, squares(k)[:, c, :], c == 0, c == DT - 1)
                last.then_inc(S["ss_mm"], 1)

            pe.wait_ge(S["const_in"], 32)
            pe.wait_ge(S["silu_c"], 1)
            for c in range(DT):
                last = tr(psum[:, 5, c * NSEQ:(c + 1) * NSEQ], ctok2[0:NSEQ, c::DT])
            last.then_inc(S["c_tr"], 1)
            def mod_turn(g):
                pe.wait_ge(S["mod_row"], 2 * (g + 1))
                if g >= 1:
                    pe.wait_ge(S["mod_set"], g)
                for c in range(DT):
                    last = mm(psum[:, 7, c * NSEQ:(c + 1) * NSEQ], mrow[:, c::DT], K[:, C_S4:C_S4 + NSEQ])
                last.then_inc(S["mod_tr"], 1)

            def mod_half(k):
                if k >= 1:
                    pe.wait_ge(S["mod_row"], k)
                if k % 2 == 0 and k not in (0, MOD_FIRST):
                    mod_turn(k // 2 - 1)
                for u in (2 * k, 2 * k + 1):
                    arrived(mod_unit[u])
                    w = mix_view(mod_unit[u])
                    for k2 in range(2):
                        for j in range(4):
                            last = mm(psum[32 * j:32 * j + 32, 6, (u % 2) * 256:(u % 2 + 1) * 256], cT[:, 4 * k2 + j, :],
                                      w[:, 4 * k2 + j, :], k2 == 0, k2 == 1)
                    last.then_inc(S["mod_mm"], 1)

            pe.wait_ge(S["c_sb"], 1)
            mod_half(0)
            pe.wait_ge(S["x_in"], 32)
            for t in range(2):
                for c in range(DT):
                    last = tr(psum[:, 2 * t + c // 4, (c % 4) * P:(c % 4 + 1) * P], xtok[:, t, c::DT])
                last.then_inc(S["x_tr"], 1)
            for c in range(DT):
                last = tr(psum[:, 4, c * NSA:(c + 1) * NSA], xtok[0:NSA, 2, c::DT])
            last.then_inc(S["x_tr"], 1)
            mod_half(1)
            sum_squares(0)
            pe.wait_ge(S["sd_ready"], 1)
            mod_half(2)
            mod_half(3)
            mod_turn(1)

            pe.wait_ge(S["x_sb"], 3)
            pe.wait_ge(S["h_ready"], 1)

            def beside_projection(pos):
                if pos == 5:
                    pe.wait_ge(S["const2_in"], 32)
                    pe.wait_ge(S["state_in"], 32)
                    for q in range(PBT):
                        tr(psum[:, 4, q * NSA:(q + 1) * NSA], sh_in[:, q * P:(q + 1) * P])
                    for w in range(2):
                        for q in range(QT):
                            last = tr(psum[:, 4, (PBT + w * QT + q) * NSA:(PBT + w * QT + q + 1) * NSA], cv_in[:, w, q * P:(q + 1) * P])
                    last.then_inc(S["st_tr"], 1)
                elif pos == 14:
                    pe.wait_ge(S["proj_sb"], 14)
                    pe.wait_ge(S["st_sb"], 2)
                    for q in range(PBT):
                        last = tr(psum[0:NSEQ, 2 + q // 4, (q % 4) * P:(q % 4 + 1) * P], pb[:, q, NPR - 1:T])
                    last.then_inc(S["tail_tr"], 1)
                elif pos == 16:
                    pe.wait_ge(S["small_in"], 16 * NSMALL)
                    pe.wait_ge(S["lora_in"], 2)
                    pe.wait_ge(S["tail_sb"], 1)
                    for q in range(QT):
                        last = mm(psum[:, 2 + q, 0:T], lora[0:64, q * P:(q + 1) * P], xm[0:64, 12, :])
                    last.then_inc(S["lora_mm"], 1)
                elif pos == 17:
                    pe.wait_ge(S["lora_sb"], 1)
                    for q in range(QT):
                        last = mm(psum[:, 2 + q, 0:T], lora[64:128, q * P:(q + 1) * P], xm[64:128, 12, :])
                    last.then_inc(S["lora_mm"], 1)
                elif pos == 18:
                    pe.wait_ge(S["lora_sb"], 2)
                    for q in range(QT):
                        last = mm(psum[:, 2 + q, 0:T], gup[:, q * P:(q + 1) * P], xm[:, 13, :])
                    last.then_inc(S["lora_mm"], 1)
                elif pos == 20:
                    pe.wait_ge(S["lora_sb"], 3)
                    pe.wait_ge(S["kksq_ready"], 1)
                    for q in range(QT):
                        last = mm(psum[:, 2 + q, 0:T], blk, tmp[:, q, :])
                    last.then_inc(S["kkss_mm"], 1)
                elif pos == 22:
                    pe.wait_ge(S["kknorm"], 1)
                    pe.wait_ge(S["rk_ready"], 1)
                    for q in range(QT):
                        last = mm(psum[:, 2 + q, 0:T], blk, bonus[:, q, :])
                    last.then_inc(S["rk_mm"], 1)

            for pos in range(PROJT):
                m, n = PROJ_TILE[pos], proj_unit[pos // 2]
                if pos % 2 == 0:
                    arrived(n)
                if pos >= 2:
                    pe.wait_ge(S["proj_sb"], pos - 1)
                w = mix_view(n)
                for c in range(DT):
                    last = mm(psum[:, pos % 2, 0:T], w[:, c, (m % 2) * P:(m % 2 + 1) * P], hT[:, c, :], c == 0, c == DT - 1)
                last.then_inc(S["proj_mm"], 1)
                if pos % 2:
                    for k in MOD_PROJ[pos // 2]:
                        mod_half(k)
                beside_projection(pos)

            pe.wait_ge(S["proj_sb"], PROJT)
            pe.wait_ge(S["pad_ready"], 1)
            pe.wait_ge(S["exp_ready"], 1)
            for v, src in enumerate((r_, cs, kh, v_, kk, bb)):
                for q in range(QT):
                    last = tr(psum[0:NSA, v, q * P:(q + 1) * P], src[:, q, NPR:T])
            last.then_inc(S["svec_tr"], 1)
            mod_half(17)
            pe.wait_ge(S["mod_set"], 8)
            pe.wait_ge(S["tail_ready"], 1)
            for q in range(QT):
                last = tr(psum[0:10, 7, q * P:(q + 1) * P], conv_in[:, 8 + q, NPR - 2:T])
            last.then_inc(S["tail_tr"], 1)
            pe.wait_ge(S["tail_sb"], 2)
            mod_half(18)
            mod_half(19)
            pe.wait_ge(S["svec_sb"], 1)
            pe.wait_ge(S["pad_ready"], 2)
            for t in range(2):
                for v, src in enumerate((v_, bb, kh)):
                    for q in range(QT):
                        last = tr(psum[:, 3 * t + v, q * P:(q + 1) * P], src[:, q, t * P:(t + 1) * P])
            last.then_inc(S["tok_tr"], 1)
            pe.wait_ge(S["tok_sb"], 2)

            pairs = ((Az, bb), (bb, Az), (kh, Az), (bb, Rz), (kh, Rz))

            def side(a, h, t):
                return a[:, h if a.shape[1] == H else h // 2, t * P:(t + 1) * P]

            def gram_products(t, m):
                for hh in range(2):
                    g = t * 10 + m * 2 + hh
                    if 6 <= g < 10:
                        pe.wait_ge(S["gram_sb"], g - 1)
                    elif g >= 18:
                        pe.wait_ge(S["gram_sb"], g - 3)
                    for h in range(4 * hh, 4 * hh + 4):
                        last = mm(psum[:, gram_bank(g), (h % 4) * P:(h % 4 + 1) * P], side(pairs[m][0], h, t), side(pairs[m][1], h, t))
                    last.then_inc(S["gram_mm"], 1)

            def level_z(t, k):
                for hh in range(2):
                    n = t * 10 + (k - 1) * 2 + hh
                    if n >= 2:
                        pe.wait_ge(S["xy"], n - 1)
                    for h in range(4 * hh, 4 * hh + 4):
                        last = mm(psum[:, 2 * hh, (h % 4) * P:(h % 4 + 1) * P], L1[:, h, :], Y[t][:, h, :])
                    last.then_inc(S["z_mm"], 1)

            def level_d(t, k):
                for hh in range(2):
                    pe.wait_ge(S["z_sb"], t * 10 + (k - 1) * 2 + hh + 1)
                    for h in range(4 * hh, 4 * hh + 4):
                        last = mm(psum[:, 2 * hh, (h % 4) * P:(h % 4 + 1) * P], X[:, h, :], Z[:, h, :])
                    for h in range(4 * hh, 4 * hh + 4):
                        if k == 5:
                            break
                        last = mm(psum[:, 2 * hh + 1, (h % 4) * P:(h % 4 + 1) * P], Z[:, h, :], X[:, h, :])
                    last.then_inc(S["d_mm"], 1)

            def chunk_rhs(c):
                t, p0, par = c // 2, 64 * (c % 2), c % 2
                if c >= 1:
                    pe.wait_ge(S["s_sb"], c)
                for h in range(H):
                    o = psum[p0:p0 + 64, 6, h * 64:(h + 1) * 64]
                    if c >= 1:
                        mm(o, Az[:, h, c * CH:(c + 1) * CH], S0T[:, h // 2, :], True, False)
                    last = mm(o, L2T[:, h, p0:p0 + 64], Vz[:, par, t, h * 64:(h + 1) * 64], c == 0, True)
                last.then_inc(S["rhs_mm"], 1)

            def chunk_u(c):
                pe.wait_ge(S["rhs_sb"], c + 1)
                p0 = 64 * (c % 2)
                for h in range(H):
                    last = mm(psum[p0:p0 + 64, 7, h * 64:(h + 1) * 64], Y[c // 2][:, h, p0:p0 + 64], rhs_s[:, h * 64:(h + 1) * 64])
                last.then_inc(S["u_mm"], 1)

            def chunk_out(c):
                pe.wait_ge(S["u_sb"], c + 1)
                t, p0, par = c // 2, 64 * (c % 2), c % 2
                for h in range(H):
                    ps = slice(64 * (h % 2), 64 * (h % 2) + 64)
                    o = psum[ps, 4, (h // 2) * 64:(h // 2 + 1) * 64]
                    if c >= 1:
                        mm(o, S0T[:, h // 2, :], Rz[:, h, c * CH:(c + 1) * CH], True, False)
                    mm(o, Uz[:, par, h * 64:(h + 1) * 64], R1T[:, h, p0:p0 + 64], c == 0, False)
                    last = mm(o, Vz[:, par, t, h * 64:(h + 1) * 64], R2T[:, h, p0:p0 + 64], False, True)
                last.then_inc(S["o_mm"], 1)
                for h in range(H):
                    ps = slice(64 * (h % 2), 64 * (h % 2) + 64)
                    o = psum[ps, 5, (h // 2) * 64:(h // 2 + 1) * 64]
                    mm(o, Btok[:, t, h * 64:(h + 1) * 64], Uz[:, par, h * 64:(h + 1) * 64], True, False)
                    last = mm(o, Ktok[:, t, h * 64:(h + 1) * 64], Vz[:, par, t, h * 64:(h + 1) * 64], False, True)
                last.then_inc(S["s_mm"], 1)

            pe.wait_ge(S["zeros"], 6)
            gram_products(0, 0)
            gram_products(0, 1)
            pe.wait_ge(S["xy0"], 2)
            for k in range(1, 6):
                level_z(0, k)
                if k <= 3:
                    gram_products(0, k + 1)
                if k < 5:
                    mod_half(19 + k)
                level_d(0, k)
            mod_turn(11)
            pe.wait_ge(S["xy"], 10)
            gram_products(1, 0)
            gram_products(1, 1)
            pe.wait_ge(S["xy0"], 4)
            pe.wait_ge(S["gram_sb"], 10)
            pe.wait_ge(S["mod_row"], 24)
            pe.wait_ge(S["mod_set"], 12)
            level_z(1, 1)
            chunk_rhs(0)
            level_d(1, 1)
            chunk_u(0)
            level_z(1, 2)
            chunk_out(0)
            level_d(1, 2)
            chunk_rhs(1)
            level_z(1, 3)
            chunk_u(1)
            level_d(1, 3)
            chunk_out(1)
            level_z(1, 4)
            pe.wait_ge(S["s_sb"], 2)
            gram_products(1, 2)
            level_d(1, 4)
            gram_products(1, 3)
            level_z(1, 5)
            gram_products(1, 4)
            level_d(1, 5)
            pe.wait_ge(S["gram_sb"], 20)
            pe.wait_ge(S["xy"], 20)
            for c in (2, 3):
                chunk_rhs(c)
                chunk_u(c)
                chunk_out(c)
            pe.wait_ge(S["s_sb"], NCH)
            for q in range(QT):
                last = tr(psum[0:64, 0, q * P:(q + 1) * P], S0T[:, q, :])
            last.then_inc(S["wkv_tr"], 1)
            pe.wait_ge(S["samp_in"], 16)
            for q in range(QT):
                last = tr(psum[:, 1, q * NSA:(q + 1) * NSA], so_tok[:, q * P:(q + 1) * P])
            last.then_inc(S["samp_tr"], 1)
            pe.wait_ge(S["wkv_sb"], 1)
            pe.wait_ge(S["samp_sb"], 1)
            for q in range(QT):
                last = mm(psum[:, q, 0:T], blk, outT[:, q, :])
            last.then_inc(S["gn_mm"], 1)
            arrived(U_ABO)
            arrived(U_ABO + 1)
            for m in range(4):
                for q in range(QT):
                    mm(psum[:, 4 + m, 0:T], mix_view(U_ABO + q // 2)[:, q % 2, m::DT], y_a[:, q, :], q == 0, False)
            pe.wait_ge(S["gn_c"], 1)
            for q in range(QT):
                last = mm(psum[:, q, 0:T], blk, tmp[:, q, :])
            last.then_inc(S["gn_mm"], 1)

            def output_product(l, u0, rhs):
                for u in range(4):
                    arrived(u0 + u)
                for m in range(DT):
                    first = 4 if l == 0 and m < 4 else 0
                    for q in range(first, 8):
                        last = mm(psum[:, (m + 4) % 8, 0:T], mix_view(u0 + q // 2)[:, q % 2, m::DT], rhs[:, q, :], q == 0, q == 7)
                    last.then_inc(S["out_mm"], 1)

            def moe(l):
                pe.wait_ge(S["h_ready"], 2 * l + 2)
                for t in range(3):
                    for c in range(DT):
                        last = mm(psum[0:TR, 0, t * NE:(t + 1) * NE], hT[:, c, t * TR:(t + 1) * TR], router[:, l, c, :], c == 0, c == DT - 1)
                last.then_inc(S["logit_mm"], 1)
                for n in range(6):
                    if n >= 2:
                        pe.wait_ge(S["htr_sb"], 6 * l + n - 1)
                    for c in range(4):
                        last = tr(psum[0:TR, 2 + n % 2, c * P:(c + 1) * P], hT[:, (n % 2) * 4 + c, (n // 2) * TR:(n // 2 + 1) * TR])
                    last.then_inc(S["htr_mm"], 1)
                u0 = U_SH[l]
                def shared_in(b, n):
                    arrived(n)
                    for j in range(2):
                        for c in range(DT):
                            last = mm(psum[:, b + j, 0:T], mix_view(n)[:, c, j::2], hT[:, c, :], c == 0, c == DT - 1)
                    last.then_inc(S["sh_mm"], 1)

                shared_in(4, u0)
                pe.wait_ge(S["mask_ready"], l + 1)
                for t in range(3):
                    for s in range(t + 1):
                        last = mm(psum[0:TR, 1, t * NE:(t + 1) * NE], (K[0:TR, C_UPT:C_UPT + TR] if s == t else ones[0:TR, 0:TR]), mask[0:TR, s, :], s == 0, s == t)
                for s in range(3):
                    last = mm(psum[0:TR, 1, 3 * NE:4 * NE], ones[0:TR, 0:TR], mask[0:TR, s, :], s == 0, s == 2)
                last.then_inc(S["rank_mm"], 1)
                shared_in(6, u0 + 1)
                pe.wait_ge(S["round_set"], l + 1)
                first = pe.value_load(nrounds[0:1, 0:1], min_val=1, max_val=MAXR) if l else 0
                end = pe.value_load(nrounds[0:1, l:l + 1], min_val=1, max_val=(l + 1) * MAXR)

                def slots(r, j):
                    pe.wait_ge(S["sel"], r * 34 + (j + 1))
                    for t in range(3):
                        mm(psum[:, 4, 0:1], slotsel[0:TR, t].rearrange("p a s -> p (a s)"), K[0:TR, C_TOK + t:C_TOK + t + 1], t == 0, t == 2)
                    for t in range(3):
                        last = mm(psum[:, 4, 2:4], slotsel[0:TR, t].rearrange("p a s -> p (a s)"), comb[0:TR, t, 2 * j:2 * j + 2], t == 0, t == 2)
                    last.then_inc(S["slot_mm"], 1)

                pe.wait_ge(S["sh_act"], l + 1)
                slots(first, 0)
                pe.wait_ge(S["htr_sb"], 6 * l + 6)
                pe.wait_ge(S["sh_hid"], l + 1)
                arrived(u0 + 2)
                for m in range(DT):
                    if m >= 2:
                        pe.wait_ge(S["shd_sb"], 8 * l + m - 1)
                    for j in range(2):
                        last = mm(psum[:, 2 + m % 2, 0:T], mix_view(u0 + 2)[:, j, m::DT], shid[:, j, :], j == 0, j == 1)
                    last.then_inc(S["shd_mm"], 1)
                    if m == 2:
                        slots(first, 1)
                pe.wait_ge(S["shd_sb"], 8 * l + 8)
                with pe.Fori(first, end) as r:
                    pe.wait_ge(S["gat_a"], r * 272 + 16)
                    pe.wait_ge(S["ht_sb"], r * NPAIR)
                    for half in range(2):
                        if half:
                            pe.wait_ge(S["xt_sb"], r * 66 + 1)
                        for c in range(4):
                            last = tr(psum[:, 5, c * P:(c + 1) * P], xg[0][:, half * 4 + c, :])
                        last.then_inc(S["xt_mm"], 1)
                    with pe.Fori(0, NTURN) as i:
                        for b in range(EBODY):
                            m1_ = r * NPAIR + i * EBODY + (b + 1)
                            nb = (b + 1) % 2
                            pe.wait_ge(S["gat_" + "ab"[nb]], r * 272 + i * 32 + 16 * ((b + 1) // 2 + 1))
                            pe.wait_ge(S["ht_sb"], m1_ - 1)
                            pe.wait_ge(S["xt_sb"], r * 66 + i * 8 + (2 * b + 2))
                            for c in range(4):
                                last = tr(psum[:, 5, c * P:(c + 1) * P], xg[nb][:, c, :])
                            last.then_inc(S["xt_mm"], 1)
                            s0 = eslot((b % 2) * PU)

                            def put_back(c):
                                if b or c >= 2:
                                    pe.wait_ge(S["cb_add"], r * 264 + i * 32 + (8 * b + c) - 1)
                                else:
                                    pe.wait_ge(S["cb_add"], r * 264 + i * 32)
                                mm(psum[:, 6 + c % 2, 0:T], gout[:, c::DT], selT[(b + 3) % 4]).then_inc(S["cb_mm"], 1)

                            def product(kind, bank, inp):
                                for e in range(2):
                                    pe.wait_ge(eload[s0 + 2 * kind + e], r * (RU // ESLOTS * 16) + i * 32 + 16 * (b // 2 + 1))
                                for c in range(DT):
                                    for e in range(2):
                                        x = mm(psum[64 * e:64 * e + 64, bank, 0:DE], inp[:, c, 64 * e:64 * e + 64],
                                               ring[:, s0 + 2 * kind + e, c * DE:(c + 1) * DE], c == 0, c == DT - 1)
                                        if c == DT - 1:
                                            x.then_inc(S["unit_used"], 1)
                                    if kind == 1 and c in (1, 3, 5):
                                        put_back(c // 2)

                            pe.wait_ge(S["gsil"], m1_ - 1)
                            product(0, 0, xgT[b % 2])
                            pe.wait_ge(S["sel"], r * 34 + i * EBODY + (b + 3))
                            for t in range(3):
                                mm(psum[:, 4, 0:1], slotsel[0:TR, t].rearrange("p a s -> p (a s)"), K[0:TR, C_TOK + t:C_TOK + t + 1], t == 0, t == 2)
                            for t in range(3):
                                last = mm(psum[:, 4, 2:4], slotsel[0:TR, t].rearrange("p a s -> p (a s)"),
                                          comb[0:TR, t, bass.ds(i * 8 + (2 * b + 4), 2)], t == 0, t == 2)
                            last.then_inc(S["slot_mm"], 1)
                            pe.wait_ge(S["xt_sb"], r * 66 + i * 8 + (2 * b + 3))
                            for c in range(4):
                                last = tr(psum[:, 5, c * P:(c + 1) * P], xg[nb][:, 4 + c, :])
                            last.then_inc(S["xt_mm"], 1)
                            pe.wait_ge(S["ghid"], m1_ - 1)
                            pe.wait_ge(S["os_a"], m1_ - 1)
                            pe.wait_ge(S["os_b"], m1_ - 1)
                            product(1, 1, xgT[b % 2])
                            for c in (3, 4, 5):
                                put_back(c)
                            pe.wait_ge(S["ghid"], m1_)
                            pe.wait_ge(S["xt_sb"], r * 66 + i * 8 + (2 * b + 4))
                            for j in range(2):
                                last = tr(psum[:, 5, j * P:(j + 1) * P], ghid[:, j::2])
                            last.then_inc(S["ht_mm"], 1)
                            for c in (6, 7):
                                put_back(c)
                            pe.wait_ge(S["ht_sb"], m1_)
                            for e in range(2):
                                pe.wait_ge(eload[s0 + 4 + e], r * (RU // ESLOTS * 16) + i * 32 + 16 * (b // 2 + 1))
                            for n in range(2):
                                for j in range(2):
                                    for e in range(2):
                                        x = mm(psum[64 * e:64 * e + 64, 2 + n, :], ghT[:, j, 64 * e:64 * e + 64],
                                               ring[:, s0 + 4 + e, j * D + n * 512:j * D + n * 512 + 512], j == 0, j == 1)
                                        if n == 1 and j == 1:
                                            x.then_inc(S["unit_used"], 1)
                    pe.wait_ge(S["gat_b"], (r + 1) * 272)
                    pe.wait_ge(S["os_a"], (r + 1) * NPAIR)
                    pe.wait_ge(S["os_b"], (r + 1) * NPAIR)
                    for c in range(DT):
                        pe.wait_ge(S["cb_add"], r * 264 + (256 + c - (1 if c >= 2 else 0) if c >= 2 else 256))
                        mm(psum[:, 6 + c % 2, 0:T], gout[:, c::DT], selT[3]).then_inc(S["cb_mm"], 1)
                    with pe.If(r + 1 < end):
                        slots(r + 1, 0)
                        slots(r + 1, 1)

            pe.wait_ge(S["yab_ready"], 1)
            output_product(0, U_ABO, hT)
            pe.wait_ge(S["out_sb"], 4)
            sum_squares(1)
            sum_squares(2)
            moe(0)
            sum_squares(3)
            sum_squares(4)

            pe.wait_ge(S["h_ready"], 3)

            def beside_u(pos):
                if pos == 2:
                    pe.wait_ge(S["gmisc_in"], 32)
                    for g in range(8):
                        last = tr(psum[:, 4 + g // 4, (g % 4) * P:(g % 4 + 1) * P], wsn[:, g, :])
                    last.then_inc(S["ws_tr"], 1)
                elif pos == 8:
                    pe.wait_ge(S["z_sb1"], 8)
                    for g in range(8):
                        last = mm(psum[:, 6, 0:T], ones, z[:, 8 + g, :], g == 0, g == 7)
                    last.then_inc(S["vmu_mm"], 1)
                elif pos == 10:
                    for g in range(8):
                        pe.wait_ge(S["vc_ready"], g + 1)
                        last = mm(psum[:, 7, 0:T], ones, gt1[:, g, :], g == 0, g == 7)
                    last.then_inc(S["vvar_mm"], 1)
                elif pos == 13:
                    pe.wait_ge(S["v_ready"], 1)
                    pe.wait_ge(S["ws_sb"], 1)
                    for t in range(2):
                        for g in range(8):
                            last = tr(psum[:, 2 + 2 * t + g // 4, (g % 4) * P:(g % 4 + 1) * P], z[:, 8 + g, t * P:(t + 1) * P])
                        last.then_inc(S["vt_tr"], 1)
                    for g in range(8):
                        last = tr(psum[0:NSA, 6 + g // 4, (g % 4) * P:(g % 4 + 1) * P], z[:, 8 + g, NPR:T])
                    last.then_inc(S["vt_tr"], 1)
                elif pos == 14:
                    for t in range(2):
                        pe.wait_ge(S["vt_sb"], t + 1)
                        for g in range(8):
                            last = mm(psum[:, 2 + 2 * t + g // 4, (g % 4) * P:(g % 4 + 1) * P], vtok[:, t, g * P:(g + 1) * P], wsT[:, g, :])
                        last.then_inc(S["sg_mm"], 1)

            for pos in range(16):
                n = U_GMI + pos // 2
                if pos % 2 == 0:
                    arrived(n)
                if pos >= 2:
                    pe.wait_ge(S["z_sb1"], pos - 1)
                for c in range(DT):
                    last = mm(psum[:, pos % 2, 0:T], mix_view(n)[:, c, (pos % 2) * P:(pos % 2 + 1) * P], hT[:, c, :], c == 0, c == DT - 1)
                last.then_inc(S["z_mm1"], 1)
                beside_u(pos)
            pe.wait_ge(S["sg_ready"], 1)
            pe.wait_ge(S["vs_sb"], 1)
            output_product(1, U_GMO, z)
            pe.wait_ge(S["out_sb"], 12)
            sum_squares(5)
            sum_squares(6)
            moe(1)
            sum_squares(7)
            pe.wait_ge(S["y_done"], 4)
            for n in range(6):
                if n >= 2:
                    pe.wait_ge(S["fin_sb"], n - 1)
                for c in range(4):
                    last = tr(psum[0:TR, n % 2, c * P:(c + 1) * P], xT[:, (n % 2) * 4 + c, (n // 2) * TR:(n // 2 + 1) * TR])
                last.then_inc(S["fin_tr"], 1)

        @block.scalar
        def _(act):
            def f(out, in_, func, **kw):
                return nc.scalar.activation(out, in_, func, **kw)

            def root(k):
                act.wait_ge(S["ss_mm"], k + 1)
                f(rstd[:, :], psum[:, 7, 0:T], ACT.Sqrt, bias=eps[:, 0:1]).then_inc(S["sd_ready"], 1)

            act.wait_ge(S["c_in"], 32)
            f(ctok2[0:NSEQ, :], ctok[0:NSEQ, :], ACT.Silu).then_inc(S["silu_c"], 1)

            def mod_rows(k):
                act.wait_ge(S["mod_mm"], 2 * (k + 1))
                if k >= 2:
                    act.wait_ge(S["mod_tr"], k // 2)
                f(mrow[:, k % 2 * 512:(k % 2 + 1) * 512], psum[:, 6, :], ACT.Copy).then_inc(S["mod_row"], 1)

            mod_rows(0)
            mod_rows(1)
            root(0)
            mod_rows(2)
            mod_rows(3)
            def beside_projection(pos):
                if pos == 15:
                    act.wait_ge(S["small_in"], 16 * NSMALL)
                    act.wait_ge(S["mixed"], 1)
                    f(xm[0:64, 12, :], xm[0:64, 12, :], ACT.Tanh).then_inc(S["lora_in"], 1)
                    f(xm[:, 13, :], xm[:, 13, :], ACT.Sigmoid).then_inc(S["lora_in"], 1)
                elif pos == 16:
                    act.wait_ge(S["lora_mm"], 1)
                    for q in range(QT):
                        last = f(ld[:, q, :], psum[:, 2 + q, 0:T], ACT.Sigmoid, bias=w0[:, q:q + 1])
                    last.then_inc(S["lora_sb"], 1)
                elif pos == 17:
                    act.wait_ge(S["lora_mm"], 2)
                    for q in range(QT):
                        last = f(a_sig[:, q, :], psum[:, 2 + q, 0:T], ACT.Sigmoid, bias=a0[:, q:q + 1])
                    last.then_inc(S["lora_sb"], 1)
                elif pos == 18:
                    act.wait_ge(S["lora_mm"], 3)
                    f(g_t, psum[:, 2:6, 0:T], ACT.Copy).then_inc(S["lora_sb"], 1)
                elif pos == 20:
                    act.wait_ge(S["kkss_mm"], 1)
                    f(tmp, psum[:, 2:6, 0:T], ACT.Sqrt).then_inc(S["kknorm"], 1)
                elif pos == 21:
                    act.wait_ge(S["cs_ready"], 1)
                    f(px, px, ACT.Exp).then_inc(S["act"], 1)
                    f(ld, cs, ACT.Exp, scale=-1.0).then_inc(S["act"], 1)
                    act.wait_ge(S["act"], 2)
                    f(cs, cs, ACT.Exp).then_inc(S["exp_ready"], 1)

            for pos in range(PROJT):
                m = PROJ_TILE[pos]
                if m == 0:
                    act.wait_ge(S["st_sb"], 2)
                    act.wait_ge(S["conv_out"], 16)
                act.wait_ge(S["proj_mm"], pos + 1)
                f(conv_in[:, m, :] if m < 12 else proj[:, m, :], psum[:, pos % 2, 0:T], ACT.Copy).then_inc(S["proj_sb"], 1)
                if pos % 2:
                    for k in MOD_PROJ[pos // 2]:
                        mod_rows(k)
                beside_projection(pos)
            act.wait_ge(S["svec_tr"], 1)
            act.wait_ge(S["shift_out"], 32)
            f(svec_tok, psum[0:NSA, 0:6, :], ACT.Copy).then_inc(S["svec_sb"], 1)
            for k in (17, 18, 19):
                mod_rows(k)
            act.wait_ge(S["svec_out"], 16)
            act.wait_ge(S["tok_tr"], 1)
            for t in range(2):
                f(Btok[:, t, :], psum[:, 3 * t + 1, :], ACT.Copy)
                last = f(Ktok[:, t, :], psum[:, 3 * t + 2, :], ACT.Copy)
            last.then_inc(S["tok_sb"], 1)
            for k in range(20, 24):
                mod_rows(k)
            act.wait_ge(S["wkv_tr"], 1)
            f(wkv_o[0:64], psum[0:64, 0, :].rearrange("p (h j) -> p h j", h=H), ACT.Copy).then_inc(S["wkv_sb"], 1)
            act.wait_ge(S["gn_mm"], 2)
            f(tmp, psum[:, 0:4, 0:T], ACT.Sqrt, bias=eps[:, 1:2]).then_inc(S["gn_sd"], 1)

            def outputs(l, y):
                for m in range(DT):
                    act.wait_ge(S["out_mm"], 8 * l + m + 1)
                    f(y[:, m, :], psum[:, (m + 4) % 8, 0:T], ACT.Copy).then_inc(S["out_sb"], 1)

            def moe(l):
                act.wait_ge(S["logit_mm"], l + 1)
                if l == 0:
                    act.wait_ge(S["rwkv_free"], 1)
                else:
                    act.wait_ge(S["vs_stored"], 1)
                act.wait_ge(S["y_done"], 2 * l + 1)
                f(score[0:TR], psum[0:TR, 0, 0:3 * NE].rearrange("p (t e) -> p t e", t=3), ACT.Sigmoid).then_inc(S["score_ready"], 1)
                for n in range(6):
                    act.wait_ge(S["htr_mm"], 6 * l + n + 1)
                    f(htok[0:TR, n // 2, (n % 2) * 512:(n % 2 + 1) * 512], psum[0:TR, 2 + n % 2, :], ACT.Copy).then_inc(S["htr_sb"], 1)
                act.wait_ge(S["sh_mm"], 2 * l + 1)
                f(ssil, psum[:, 4:6, 0:T], ACT.Silu).then_inc(S["sh_act"], 1)
                for m in range(DT):
                    act.wait_ge(S["shd_mm"], 8 * l + m + 1)
                    f(yacc[:, m, :], psum[:, 2 + m % 2, 0:T], ACT.Copy).then_inc(S["shd_sb"], 1)
                act.wait_ge(S["round_set"], l + 1)
                first = act.value_load(nrounds[0:1, 0:1], min_val=1, max_val=MAXR) if l else 0
                end = act.value_load(nrounds[0:1, l:l + 1], min_val=1, max_val=(l + 1) * MAXR)
                with act.Fori(first, end) as r:
                    for half in range(2):
                        act.wait_ge(S["xt_mm"], r * 66 + (half + 1))
                        if half == 0:
                            act.wait_ge(S["unit_used"], r * RU)
                        f(xgT[0][:, half * 4:half * 4 + 4, :], psum[:, 5, :].rearrange("p (c s) -> p c s", c=4), ACT.Copy).then_inc(S["xt_sb"], 1)
                    with act.Fori(0, NTURN) as i:
                        for b in range(EBODY):
                            m1_ = r * NPAIR + i * EBODY + (b + 1)
                            u0_ = r * RU + i * (EBODY * PU) + b * PU
                            nb = (b + 1) % 2
                            for half in range(2):
                                act.wait_ge(S["xt_mm"], r * 66 + i * 8 + (2 * b + 3 + half))
                                if half == 0:
                                    act.wait_ge(S["unit_used"], u0_)
                                f(xgT[nb][:, half * 4:half * 4 + 4, :], psum[:, 5, :].rearrange("p (c s) -> p c s", c=4), ACT.Copy).then_inc(S["xt_sb"], 1)
                                if half == 0:
                                    act.wait_ge(S["unit_used"], u0_ + 2)
                                    act.wait_ge(S["ghid"], m1_ - 1)
                                    f(gsil, psum[:, 0, 0:DE], ACT.Silu).then_inc(S["gsil"], 1)
                            act.wait_ge(S["ht_mm"], m1_)
                            act.wait_ge(S["unit_used"], u0_)
                            f(ghT, psum[:, 5, 0:2 * P].rearrange("p (j s) -> p j s", j=2), ACT.Copy).then_inc(S["ht_sb"], 1)
                            act.wait_ge(S["unit_used"], u0_ + 6)
                            f(gout[:, 0:512], psum[:, 2, :], ACT.Copy).then_inc(S["os_a"], 1)

            outputs(0, yacc)
            root(1)
            root(2)
            moe(0)
            root(3)
            root(4)
            for pos in range(16):
                m = (pos + 8) % 16
                act.wait_ge(S["z_mm1"], pos + 1)
                if pos == 0:
                    act.wait_ge(S["y_done"], 2)
                f(z[:, m, :], psum[:, pos % 2, 0:T], ACT.Gelu_apprx_tanh, bias=gb_in[:, m:m + 1]).then_inc(S["z_sb1"], 1)
                if pos == 10:
                    act.wait_ge(S["vvar_mm"], 1)
                    f(rstd[:, :], psum[:, 7, 0:T], ACT.Sqrt, bias=eps[:, 0:1]).then_inc(S["ln_sd"], 1)
                elif pos == 13:
                    for t in range(2):
                        act.wait_ge(S["vt_tr"], t + 1)
                        f(vtok[:, t, :].rearrange("p (a n) -> p a n", a=2), psum[:, 2 + 2 * t:4 + 2 * t, :], ACT.Copy).then_inc(S["vt_sb"], 1)
                    act.wait_ge(S["vt_tr"], 3)
                    f(vs_out[0:NSA, :].rearrange("p (a n) -> p a n", a=2), psum[0:NSA, 6:8, :], ACT.Copy).then_inc(S["vs_sb"], 1)
            outputs(1, gt1)
            root(5)
            root(6)
            moe(1)
            root(7)
            act.wait_ge(S["y_done"], 4)
            for n in range(6):
                act.wait_ge(S["fin_tr"], n + 1)
                out = xo[0:TR, n // 2, :].rearrange("p (d c) -> p c d", c=DT)[:, (n % 2) * 4:(n % 2) * 4 + 4, :]
                f(out, psum[0:TR, n % 2, :].rearrange("p (c d) -> p c d", c=4), ACT.Copy).then_inc(S["fin_sb"], 1)

        @block.vector
        def _(dve):
            V = nc.vector
            done = [0]

            def v(i):
                done[0] += 1
                i.then_inc(S["vec"], 1)
                dve.wait_ge(S["vec"], done[0])

            def over(col, n):
                return col.unsqueeze(len(col.shape)).broadcast_to([*col.shape, n])

            def rms(k, src, tile_ready=None):
                for c in range(DT):
                    if tile_ready:
                        dve.wait_ge(S[tile_ready[0]], tile_ready[1] + c + 1)
                    V.scalar_tensor_tensor(squares(k)[:, c, :], src[:, c, :], 1.0 / D, src[:, c, :], ALU.mult, ALU.mult).then_inc(S["sq_ready"], 1)
                dve.wait_ge(S["ss_mm"], k + 1)
                dve.wait_ge(S["sd_ready"], k + 1)
                v(V.reciprocal(rstd[:, :], rstd[:, :]))

            wide = lambda: rstd[:, :].unsqueeze(1).broadcast_to([P, DT, T])

            def pre(k, l, half):
                normalise(k)
                modulate(l, half)

            def normalise(k):
                rms(k, xT[:, :, :])
                v(V.tensor_tensor(hT[:, :, :], xT[:, :, :], wide(), ALU.mult))

            def modulate(l, half):
                sh, sc = mod[:, l, 3 * half], mod[:, l, 3 * half + 1]
                v(V.tensor_tensor(hT[:, :, NPR:T], hT[:, :, NPR:T], sc[:, :, 1:NSEQ], ALU.mult))
                V.tensor_tensor(hT[:, :, NPR:T], hT[:, :, NPR:T], sh[:, :, 1:NSEQ], ALU.add)
                for c in range(DT):
                    last = V.tensor_scalar(hT[:, c, 0:NPR], hT[:, c, 0:NPR], sc[:, c, 0:1], sh[:, c, 0:1], ALU.mult, ALU.add)
                last.then_inc(S["h_ready"], 1)

            def post(k, l, half, y, tile_ready=None):
                rms(k, y, tile_ready)
                v(V.tensor_tensor(y, y, wide(), ALU.mult))
                g = mod[:, l, 3 * half + 2]
                v(V.tensor_tensor(y[:, :, NPR:T], y[:, :, NPR:T], g[:, :, 1:NSEQ], ALU.mult))
                V.tensor_tensor(xT[:, :, NPR:T], xT[:, :, NPR:T], y[:, :, NPR:T], ALU.add)
                for c in range(DT):
                    last = V.scalar_tensor_tensor(xT[:, c, 0:NPR], y[:, c, 0:NPR], g[:, c, 0:1], xT[:, c, 0:NPR], ALU.mult, ALU.add)
                last.then_inc(S["y_done"], 1)
                dve.wait_ge(S["y_done"], 2 * l + half + 1)

            V.memset(eps[:, 0:1], EPS)
            V.memset(eps[:, 1:2], GN_EPS)
            v(V.memset(cT[:, :, :], 0.0))
            dve.wait_ge(S["c_tr"], 1)
            V.tensor_copy(cT[:, :, 0:NSEQ], psum[:, 5, 0:DT * NSEQ].rearrange("p (c s) -> p c s", c=DT)).then_inc(S["c_sb"], 1)
            for t in range(2):
                dve.wait_ge(S["x_tr"], t + 1)
                V.tensor_copy(xT[:, :, t * P:(t + 1) * P].rearrange("p (a c) n -> p a c n", a=2),
                              psum[:, 2 * t:2 * t + 2, :].rearrange("p a (c n) -> p a c n", c=4)).then_inc(S["x_sb"], 1)
            dve.wait_ge(S["x_tr"], 3)
            V.tensor_copy(xT[:, :, NPR:T], psum[:, 4, 0:DT * NSA].rearrange("p (c s) -> p c s", c=DT)).then_inc(S["x_sb"], 1)
            dve.wait_ge(S["x_sb"], 3)
            normalise(0)

            def mod_part(g):
                l, part = g // 6, g % 6
                dve.wait_ge(S["mod_tr"], g + 1)
                m = mod[:, l, part]
                V.tensor_tensor(m, psum[:, 7, 0:DT * NSEQ].rearrange("p (c s) -> p c s", c=DT),
                                over(b_modT[:, l, part], NSEQ), ALU.add).then_inc(S["mod_set"], 1)
                dve.wait_ge(S["mod_set"], g + 1)
                if part in (1, 4):
                    v(V.tensor_scalar(m, m, 1.0, None, ALU.add))
                    v(V.tensor_tensor(m, m, over(ngT[:, l, part // 3 * 2], NSEQ), ALU.mult))
                if part in (2, 5):
                    v(V.tensor_tensor(m, m, over(ngT[:, l, part // 3 * 2 + 1], NSEQ), ALU.mult))

            dve.wait_ge(S["modp_in"], 32)
            mod_part(0)
            mod_part(1)
            modulate(0, 0)
            mod_part(2)
            dve.wait_ge(S["st_tr"], 1)
            V.tensor_copy(st_shift, psum[:, 4, 0:PBT * NSA].rearrange("p (q s) -> p q s", q=PBT)).then_inc(S["st_sb"], 1)
            V.tensor_copy(st_conv, psum[:, 4, PBT * NSA:PBT * NSA + 64].rearrange("p (w q s) -> p w q s", w=2, q=QT)).then_inc(S["st_sb"], 1)
            mod_part(3)
            dve.wait_ge(S["st_sb"], 2)
            dve.wait_ge(S["const2_in"], 32)
            dve.wait_ge(S["small_in"], 16 * NSMALL)
            dve.wait_ge(S["proj_sb"], PBT)
            V.tensor_tensor(xm[:, :, 1:NPR], pb[:, :, 0:NPR - 1], pb[:, :, 1:NPR], ALU.subtract)
            V.tensor_scalar(xm[:, :, 0:1], pb[:, :, 0:1], -1.0, None, ALU.mult)
            v(V.tensor_tensor(xm[:, :, NPR:T], st_shift, pb[:, :, NPR:T], ALU.subtract))
            for q in reversed(range(PBT)):
                last = V.scalar_tensor_tensor(xm[:, q, :], xm[:, q, :], mu[:, q:q + 1], pb[:, q, :], ALU.mult, ALU.add)
            last.then_inc(S["mixed"], 1)
            dve.wait_ge(S["mixed"], 1)
            dve.wait_ge(S["tail_tr"], 1)
            V.tensor_copy(sh_out, psum[0:NSEQ, 2:6, :].rearrange("p a b -> p (a b)")[:, 0:PB]).then_inc(S["tail_sb"], 1)
            V.memset(Uz, 0.0)
            V.memset(rhs_s, 0.0)
            mod_part(4)

            dve.wait_ge(S["lora_sb"], 1)
            v(V.tensor_scalar(ld, ld, -EMH, None, ALU.mult))
            for q in range(QT):
                for c in range(NCH):
                    s = slice(c * CH, (c + 1) * CH)
                    V.tensor_tensor_scan(cs[:, q, s], ones[:, 0:CH], ld[:, q, s], 0.0, ALU.mult, ALU.add)
            v(V.tensor_copy(cs[:, :, NPR:T], ld[:, :, NPR:T]))
            V.tensor_tensor(px, cs, ld, ALU.subtract).then_inc(S["cs_ready"], 1)
            mod_part(5)
            v(V.tensor_tensor(kk, k_, over(k_k, T), ALU.mult))
            V.tensor_tensor(tmp, kk, kk, ALU.mult).then_inc(S["kksq_ready"], 1)
            dve.wait_ge(S["lora_sb"], 2)
            v(V.tensor_scalar(kh, a_sig, -1.0, None, ALU.add))
            v(V.tensor_tensor(kh, kh, over(k_a, T), ALU.mult))
            v(V.scalar_tensor_tensor(kh, kh, 1.0, k_, ALU.add, ALU.mult))
            v(V.tensor_tensor(bonus, r_, over(r_k, T), ALU.mult))
            V.tensor_tensor(bonus, bonus, kh, ALU.mult).then_inc(S["rk_ready"], 1)
            mod_part(6)
            dve.wait_ge(S["kknorm"], 1)
            v(V.tensor_scalar(tmp, tmp, 1e-12, None, ALU.max))
            v(V.reciprocal(tmp, tmp))
            v(V.tensor_tensor(kk, kk, tmp, ALU.mult))
            v(V.tensor_tensor(bb, kk, a_sig, ALU.mult))
            dve.wait_ge(S["rk_mm"], 1)
            V.tensor_tensor(bonus, psum[:, 2:6, 0:T], v_, ALU.mult).then_inc(S["pad_ready"], 1)
            dve.wait_ge(S["pad_ready"], 1)
            dve.wait_ge(S["proj_sb"], PROJT - 4)
            gated = conv_in[:, 8:12, :]
            V.tensor_tensor(gated, gated, conv_in[:, 0:4, :], ALU.mult).then_inc(S["tail_ready"], 1)
            dve.wait_ge(S["tail_ready"], 1)
            for q in range(QT):
                y, gq = conv_t[:, q, :], gated[:, q, :]
                wq = [conv_w[:, w, q:q + 1] for w in range(3)]
                v(V.tensor_scalar(y, gq, wq[2], None, ALU.mult))
                v(V.scalar_tensor_tensor(y[:, 1:NPR], gq[:, 0:NPR - 1], wq[1], y[:, 1:NPR], ALU.mult, ALU.add))
                v(V.scalar_tensor_tensor(y[:, 2:NPR], gq[:, 0:NPR - 2], wq[0], y[:, 2:NPR], ALU.mult, ALU.add))
                v(V.scalar_tensor_tensor(y[:, NPR:T], st_conv[:, 1, q], wq[1], y[:, NPR:T], ALU.mult, ALU.add))
                v(V.scalar_tensor_tensor(y[:, NPR:T], st_conv[:, 0, q], wq[0], y[:, NPR:T], ALU.mult, ALU.add))
            dve.wait_ge(S["proj_sb"], PROJT)
            V.tensor_tensor(y_a, conv_t, conv_in[:, 4:8, :], ALU.mult).then_inc(S["conv_done"], 1)
            dve.wait_ge(S["conv_done"], 1)
            mod_part(7)
            dve.wait_ge(S["tail_tr"], 2)
            V.tensor_copy(cv_out, psum[0:10, 7, :]).then_inc(S["tail_sb"], 1)
            dve.wait_ge(S["exp_ready"], 1)
            pr = slice(0, NPR)
            for o in range(2):
                own = slice(64 * o, 64 * o + 64)
                V.tensor_tensor(Az[own, o::2, :], px[own, :, pr], kk[own, :, pr], ALU.mult)
                V.tensor_tensor(Rz[own, o::2, :], cs[own, :, pr], r_[own, :, pr], ALU.mult)
            dve.wait_ge(S["svec_tr"], 1)
            V.tensor_tensor(bb[:, :, pr], bb[:, :, pr], ld[:, :, pr], ALU.mult)
            v(V.tensor_tensor(kh[:, :, pr], kh[:, :, pr], ld[:, :, pr], ALU.mult))
            for c in range(NCH):
                last = V.tensor_copy(PC[:, c, :], cs[:, :, c * CH + CH - 1])
            last.then_inc(S["pad_ready"], 1)
            dve.wait_ge(S["pad_ready"], 2)
            dve.wait_ge(S["svec_out"], 16)
            dve.wait_ge(S["tok_tr"], 1)
            for t in range(2):
                V.tensor_copy(Vz[0:64, 0, t, :], psum[0:64, 3 * t, :])
                last = V.tensor_copy(Vz[64:128, 1, t, :], psum[64:128, 3 * t, :])
            last.then_inc(S["tok_sb"], 1)
            mod_part(8)

            def wide4(col):
                return K[:, col:col + P].unsqueeze(1).broadcast_to([P, 4, P])

            quad = lambda b: psum[:, b, :].rearrange("p (h t) -> p h t", h=4)
            gram = ((L1, C_LOS), (L1T, C_UPS), (L2T, C_UPS), (R1T, C_UPI), (R2T, C_UPI))

            def gram_masks(t, m):
                dst, mask_ = gram[m]
                for hh in range(2):
                    g = t * 10 + m * 2 + hh
                    dve.wait_ge(S["gram_mm"], g + 1)
                    V.tensor_tensor(dst[:, 4 * hh:4 * hh + 4, :], quad(gram_bank(g)), wide4(mask_), ALU.mult).then_inc(S["gram_sb"], 1)

            def start_inverse(t):
                dve.wait_ge(S["gram_sb"], t * 10 + 4)
                for hh in range(2):
                    hs = slice(4 * hh, 4 * hh + 4)
                    v(V.tensor_tensor(X[:, hs], L1[:, hs], wide4(C_LV0T), ALU.mult))
                    v(V.tensor_tensor(X[:, hs], wide4(C_ID), X[:, hs], ALU.subtract))
                    v(V.tensor_tensor(Y[t][:, hs], L1T[:, hs], wide4(C_LV), ALU.mult))
                    V.tensor_tensor(Y[t][:, hs], wide4(C_ID), Y[t][:, hs], ALU.subtract).then_inc(S["xy0"], 1)
                    dve.wait_ge(S["xy0"], 2 * t + hh + 1)

            def level_z(t, k):
                for hh in range(2):
                    hs = slice(4 * hh, 4 * hh + 4)
                    dve.wait_ge(S["z_mm"], t * 10 + (k - 1) * 2 + hh + 1)
                    V.tensor_tensor(Z[:, hs], quad(2 * hh), wide4(C_LV + k * P), ALU.mult).then_inc(S["z_sb"], 1)

            def level_xy(t, k):
                for hh in range(2):
                    hs = slice(4 * hh, 4 * hh + 4)
                    n = t * 10 + (k - 1) * 2 + hh
                    dve.wait_ge(S["d_mm"], n + 1)
                    last = V.tensor_tensor(Y[t][:, hs], Y[t][:, hs], quad(2 * hh), ALU.subtract)
                    if k < 5:
                        last = V.tensor_tensor(X[:, hs], X[:, hs], quad(2 * hh + 1), ALU.subtract)
                    last.then_inc(S["xy"], 1)
                    dve.wait_ge(S["xy"], n + 1)

            def chunk_rhs(c):
                ps = slice(64 * (c % 2), 64 * (c % 2) + 64)
                dve.wait_ge(S["rhs_mm"], c + 1)
                V.tensor_copy(rhs_s[ps, :], psum[ps, 6, :]).then_inc(S["rhs_sb"], 1)

            def chunk_u(c):
                ps = slice(64 * (c % 2), 64 * (c % 2) + 64)
                dve.wait_ge(S["u_mm"], c + 1)
                V.tensor_scalar(Uz[ps, c % 2, :], psum[ps, 7, :], -1.0, None, ALU.mult).then_inc(S["u_sb"], 1)

            def chunk_out(c):
                dve.wait_ge(S["o_mm"], c + 1)
                V.tensor_copy(outT[:, :, c * CH:(c + 1) * CH], psum[:, 4, 0:256].rearrange("p (q t) -> p q t", q=QT)).then_inc(S["o_sb"], 1)
                dve.wait_ge(S["s_mm"], c + 1)
                s_ps = psum[:, 5, 0:256].rearrange("p (q i) -> p q i", q=QT)
                if c == 0:
                    v(V.tensor_copy(S0T, s_ps))
                else:
                    v(V.tensor_tensor(S0T, S0T, s_ps, ALU.add))
                V.tensor_tensor(S0T, S0T, over(PC[:, c, :], HD), ALU.mult).then_inc(S["s_sb"], 1)
                dve.wait_ge(S["s_sb"], c + 1)

            gram_masks(0, 0)
            gram_masks(0, 1)
            start_inverse(0)
            for k in range(1, 6):
                level_z(0, k)
                if k <= 3:
                    gram_masks(0, k + 1)
                level_xy(0, k)
                if k in (1, 3):
                    mod_part(9 + k // 2)
            mod_part(11)
            gram_masks(1, 0)
            gram_masks(1, 1)
            start_inverse(1)
            level_z(1, 1)
            chunk_rhs(0)
            level_xy(1, 1)
            chunk_u(0)
            level_z(1, 2)
            chunk_out(0)
            level_xy(1, 2)
            chunk_rhs(1)
            level_z(1, 3)
            chunk_u(1)
            level_xy(1, 3)
            chunk_out(1)
            level_z(1, 4)
            gram_masks(1, 2)
            level_xy(1, 4)
            gram_masks(1, 3)
            level_z(1, 5)
            gram_masks(1, 4)
            level_xy(1, 5)
            for c in (2, 3):
                chunk_rhs(c)
                chunk_u(c)
                chunk_out(c)
            dve.wait_ge(S["samp_tr"], 1)
            V.tensor_copy(outT[:, :, NPR:T], psum[:, 1, 0:QT * NSA].rearrange("p (q s) -> p q s", q=QT)).then_inc(S["samp_sb"], 1)
            dve.wait_ge(S["samp_sb"], 1)
            dve.wait_ge(S["o_sb"], NCH)
            dve.wait_ge(S["gn_mm"], 1)
            v(V.scalar_tensor_tensor(outT, psum[:, 0:4, 0:T], -1.0 / HD, outT, ALU.mult, ALU.add))
            V.scalar_tensor_tensor(tmp, outT, 1.0 / HD, outT, ALU.mult, ALU.mult).then_inc(S["gn_c"], 1)
            dve.wait_ge(S["gn_mm"], 2)
            dve.wait_ge(S["gn_sd"], 1)
            v(V.reciprocal(tmp, tmp))
            v(V.tensor_tensor(outT, outT, tmp, ALU.mult))
            for q in range(QT):
                last = V.tensor_scalar(outT[:, q], outT[:, q], gn_g[:, q:q + 1], gn_b[:, q:q + 1], ALU.mult, ALU.add)
            v(last)
            v(V.tensor_tensor(outT, outT, bonus, ALU.add))
            V.tensor_tensor(outT, outT, g_t, ALU.mult).then_inc(S["yab_ready"], 1)

            def moe(l):
                if l == 0:
                    dve.wait_ge(S["rwkv_free"], 1)
                g3 = lambda a: a[0:TR]
                dve.wait_ge(S["score_ready"], l + 1)
                v(V.tensor_tensor(g3(sel), g3(score), brout[:, l].unsqueeze(1).broadcast_to([TR, 3, NE]), ALU.add))
                for t in range(3):
                    for g in range(NG):
                        last = V.max(out=gt8[0:TR, t, g, :], in_=sel[0:TR, t, g * 8:(g + 1) * 8])
                v(last)
                v(V.tensor_tensor(g3(grp), gt8[0:TR, :, :, 0], gt8[0:TR, :, :, 1], ALU.add))
                for t in range(3):
                    a = grp[0:TR, t].unsqueeze(1).broadcast_to([TR, NG, NG])
                    b = grp[0:TR, t].unsqueeze(2).broadcast_to([TR, NG, NG])
                    c1, c2 = (c[0:TR, t].rearrange("p (g h) -> p g h", g=NG) for c in (cmp1, cmp2))
                    V.tensor_tensor(c1, a, b, ALU.is_gt)
                    v(V.tensor_tensor(c2, a, b, ALU.is_equal))
                v(V.tensor_tensor(g3(cmp2), g3(cmp2), K[0:TR, C_TRI:C_TRI + 64].unsqueeze(1).broadcast_to([TR, 3, 64]), ALU.mult))
                v(V.tensor_tensor(g3(cmp1), g3(cmp1), g3(cmp2), ALU.add))
                v(V.tensor_reduce(g3(rank), g3(cmp1).rearrange("p t (g h) -> p t g h", g=NG), AX.X, ALU.add))
                v(V.tensor_scalar(g3(gm), g3(rank), float(TOPG), None, ALU.is_lt))
                eg = lambda a: a[0:TR].rearrange("p t (g e) -> p t g e", g=NG)
                v(V.tensor_tensor(eg(selm), eg(sel), over(g3(gm), 8), ALU.mult))
                v(V.tensor_scalar(g3(gm), g3(gm), -1.0, BIG, ALU.add, ALU.mult))
                v(V.tensor_tensor(eg(selm), eg(selm), over(g3(gm), 8), ALU.add))
                for t in range(3):
                    v(V.max(out=top8[0:TR, t, :], in_=selm[0:TR, t, :]))
                    v(V.match_replace(out=rep[0:TR, t, :], in_to_replace=top8[0:TR, t, :], in_values=selm[0:TR, t, :], imm_value=-2 * BIG))
                V.tensor_tensor(g3(mask), g3(rep), g3(selm), ALU.is_lt).then_inc(S["mask_ready"], 1)
                dve.wait_ge(S["mask_ready"], l + 1)
                v(V.tensor_tensor(g3(score), g3(score), g3(mask), ALU.mult))
                v(V.tensor_reduce(csum[0:TR], g3(score), AX.X, ALU.add))
                v(V.reciprocal(csum[0:TR], csum[0:TR]))
                v(V.tensor_scalar(csum[0:TR], csum[0:TR], ROUTE_SCALE, None, ALU.mult))
                V.memset(comb[0:TR, :, NE:NE + 4], 0.0)
                V.memset(posm[0:TR, :, NE:NE + 4], -1.0)
                v(V.tensor_tensor(comb[0:TR, :, 0:NE], g3(score), over(csum[0:TR], NE), ALU.mult))
                dve.wait_ge(S["rank_mm"], l + 1)
                pm = posm[0:TR, :, 0:NE]
                v(V.scalar_tensor_tensor(pm, psum[0:TR, 1, 0:3 * NE].rearrange("p (t e) -> p t e", t=3), 1.0, g3(mask), ALU.add, ALU.mult))
                v(V.tensor_scalar(pm, pm, -1.0, None, ALU.add))
                v(V.tensor_reduce(cmax[0:TR], psum[0:TR, 1, 3 * NE:4 * NE], AX.X, ALU.max))
                for n in range(1, MAXR):
                    v(V.tensor_scalar(cthr[0:TR, n - 1:n], cmax[0:TR], float(CAP * n), None, ALU.is_gt))
                v(V.tensor_reduce(cmax[0:TR], cthr[0:TR, 0:MAXR - 1], AX.X, ALU.add))
                v(V.tensor_scalar(rounds[0:TR, l:l + 1], cmax[0:TR], 1.0, None, ALU.add))
                if l:
                    v(V.tensor_tensor(rounds[0:TR, 1:2], rounds[0:TR, 0:1], rounds[0:TR, 1:2], ALU.add))
                V.memset(gout, 0.0)
                V.memset(selT[3], 0.0)
                V.tensor_copy(nrounds[0:TR, l:l + 1], rounds[0:TR, l:l + 1]).then_inc(S["round_set"], 1)
                dve.wait_ge(S["round_set"], l + 1)
                first = dve.value_load(nrounds[0:1, 0:1], min_val=1, max_val=MAXR) if l else 0
                end = dve.value_load(nrounds[0:1, l:l + 1], min_val=1, max_val=(l + 1) * MAXR)
                vl = S["idxf"]

                def choose(j2):
                    iota = K[0:TR, C_IOTA:C_IOTA + CAP].unsqueeze(1).broadcast_to([TR, 2, CAP])
                    for t in range(3):
                        p = posm[0:TR, t, bass.ds(j2, 2)] if not isinstance(j2, int) else posm[0:TR, t, j2:j2 + 2]
                        last = V.tensor_tensor(slotsel[0:TR, t], iota, over(p, CAP), ALU.is_equal)
                    last.then_inc(S["sel"], 1)

                def take_slots(jj, count):
                    dve.wait_ge(S["slot_mm"], count)
                    V.tensor_copy(idxf[:, jj:jj + 1], psum[:, 4, 0:1])
                    V.tensor_copy(wt[0:64, jj:jj + 1], psum[0:64, 4, 2:3])
                    V.tensor_copy(wt[64:128, jj:jj + 1], psum[64:128, 4, 3:4]).then_inc(vl, 1)
                    dve.wait_ge(vl, count)
                    V.tensor_copy(slot_idx[:, jj:jj + 1], idxf[:, jj:jj + 1])
                    V.tensor_scalar(selT[jj], K[:, C_IOTA:C_IOTA + T], idxf[:, jj:jj + 1], None, ALU.is_equal).then_inc(S["idx"], 1)

                def add_back(base, tiles=range(DT)):
                    for c in tiles:
                        dve.wait_ge(S["cb_mm"], base + (c + 1))
                        V.tensor_tensor(yacc[:, c, :], yacc[:, c, :], psum[:, 6 + c % 2, 0:T], ALU.add).then_inc(S["cb_add"], 1)

                choose(0)
                dve.wait_ge(S["sh_act"], l + 1)
                dve.wait_ge(S["sh_mm"], 2 * l + 2)
                V.tensor_tensor(shid, ssil, psum[:, 6:8, 0:T], ALU.mult).then_inc(S["sh_hid"], 1)
                take_slots(0, first * 34 + 1)
                choose(2)
                take_slots(1, first * 34 + 2)
                dve.wait_ge(S["shd_sb"], 8 * l + 8)
                with dve.Fori(first, end) as r:
                    with dve.Fori(0, NTURN) as i:
                        for b in range(EBODY):
                            m1_ = r * NPAIR + i * EBODY + (b + 1)
                            u0_ = r * RU + i * (EBODY * PU) + b * PU
                            choose(i * 8 + (2 * b + 4))
                            take_slots((b + 2) % 4, r * 34 + i * EBODY + (b + 3))
                            dve.wait_ge(S["cb_add"], r * 264 + i * 32 + 8 * b)
                            add_back(r * 264 + i * 32 + 8 * b, range(3))
                            dve.wait_ge(S["gsil"], m1_)
                            dve.wait_ge(S["unit_used"], u0_ + 4)
                            dve.wait_ge(S["ht_mm"], m1_ - 1)
                            V.scalar_tensor_tensor(ghid, gsil, wt[:, b:b + 1], psum[:, 1, 0:DE], ALU.mult, ALU.mult).then_inc(S["ghid"], 1)
                            add_back(r * 264 + i * 32 + 8 * b, range(3, DT))
                            dve.wait_ge(S["unit_used"], u0_ + 6)
                            V.tensor_copy(gout[:, 512:D], psum[:, 3, :]).then_inc(S["os_b"], 1)
                    dve.wait_ge(S["cb_add"], r * 264 + 256)
                    add_back(r * 264 + 256)
                    dve.wait_ge(S["cb_add"], r * 264 + 264)
                    V.memset(selT[3], 0.0)
                    V.tensor_scalar(posm[0:TR, :, :], posm[0:TR, :, :], -float(CAP), None, ALU.add).then_inc(S["next"], 1)
                    with dve.If(r + 1 < end):
                        dve.wait_ge(S["next"], r + 1)
                        for j in range(2):
                            choose(2 * j)
                            take_slots(j, (r + 1) * 34 + (j + 1))

            post(1, 0, 0, yacc, ("out_sb", 0))
            pre(2, 0, 1)
            moe(0)
            post(3, 0, 1, yacc)
            pre(4, 1, 0)
            vz, uz = z[:, 8:16, :], z[:, 0:8, :]
            dve.wait_ge(S["ws_tr"], 1)
            V.tensor_tensor(wsT.rearrange("p (a g) n -> p a g n", a=2), psum[:, 4:6, :].rearrange("p a (g n) -> p a g n", g=4),
                            upi_full.unsqueeze(1).unsqueeze(1).broadcast_to([P, 2, 4, P]), ALU.mult).then_inc(S["ws_sb"], 1)
            dve.wait_ge(S["z_sb1"], 8)
            dve.wait_ge(S["vmu_mm"], 1)
            v(V.tensor_scalar(mu_b, psum[:, 6, 0:T], 1.0 / D, None, ALU.mult))
            v(V.tensor_tensor(vz, vz, mu_b.unsqueeze(1).broadcast_to([P, 8, T]), ALU.subtract))
            for g in range(DT):
                V.scalar_tensor_tensor(gt1[:, g], vz[:, g], 1.0 / D, vz[:, g], ALU.mult, ALU.mult).then_inc(S["vc_ready"], 1)
            dve.wait_ge(S["vvar_mm"], 1)
            dve.wait_ge(S["ln_sd"], 1)
            v(V.reciprocal(rstd[:, :], rstd[:, :]))
            v(V.tensor_tensor(vz, vz, wide(), ALU.mult))
            for g in range(8):
                last = V.tensor_scalar(vz[:, g], vz[:, g], ln_g[:, g:g + 1], ln_b[:, g:g + 1], ALU.mult, ALU.add)
            last.then_inc(S["v_ready"], 1)
            dve.wait_ge(S["v_ready"], 1)
            dve.wait_ge(S["gmisc_in"], 32)
            for g in range(8):
                last = V.tensor_scalar(gt2[:, g, NPR:T], vz[:, g, NPR:T], ws00[:, g:g + 1], bsb[:, g, 0:1], ALU.mult, ALU.add)
            v(last)
            for t in range(2):
                dve.wait_ge(S["sg_mm"], t + 1)
                for a in range(2):
                    v(V.tensor_tensor(gt2[:, 4 * a:4 * a + 4, t * P:(t + 1) * P], psum[:, 2 + 2 * t + a, :].rearrange("p (g n) -> p g n", g=4), bsb[:, 4 * a:4 * a + 4, :], ALU.add))
            dve.wait_ge(S["z_sb1"], 16)
            V.tensor_tensor(uz, uz, gt2, ALU.mult).then_inc(S["sg_ready"], 1)
            post(5, 1, 0, gt1, ("out_sb", 8))
            pre(6, 1, 1)
            moe(1)
            post(7, 1, 1, yacc)


_INS = ['x_prompt', 'x_sample', 'c_prompt', 'c_sample', 'state_conv', 'state_shift', 'state_wkv', 'w_mod', 'b_mod', 'norm_g',
        'ab_w_in', 'ab_conv_w', 'ab_mu', 'ab_w0', 'ab_w_decay_up', 'ab_a0', 'ab_a_up', 'ab_g_up', 'ab_k_k', 'ab_k_a', 'ab_r_k',
        'ab_gn_g', 'ab_gn_b', 'ab_w_out', 'gm_w_in', 'gm_b_in', 'gm_ln_g', 'gm_ln_b', 'gm_w_s', 'gm_b_s', 'gm_w_out',
        'moe_w_router', 'moe_b_router', 'moe_w_gate', 'moe_w_up', 'moe_w_down', 'moe_ws_gate', 'moe_ws_up', 'moe_ws_down']
_OUTS = [(1, NPR, D), (NSA, 1, D), (1, 1, 2, DA), (1, NSA, 2, DA), (1, 1, PB), (1, NSA, PB), (1, 1, H, HD, HD), (1, NSA, H, HD, HD), (1, NSA, 1, D)]


def kernel(**inputs):
    import concourse.bacc as _bacc
    from concourse.bass_utils import run_bass_kernel_spmd as _run

    nc = _bacc.Bacc("TRN2", target_bir_lowering=False, num_devices=1)
    arrays, ins, outs = {}, [], []
    for name in _INS:
        a = np.ascontiguousarray(inputs[name])
        arrays[f"in_{name}"] = a
        ins.append(nc.dram_tensor(f"in_{name}", a.shape, F32, kind="ExternalInput").ap())
    arrays["shape_constants"] = shape_constants()
    ins.append(nc.dram_tensor("shape_constants", (P, NCONST), F32, kind="ExternalInput").ap())
    for i, shape in enumerate(_OUTS):
        outs.append(nc.dram_tensor(f"out_{i}_dram", shape, F32, kind="ExternalOutput").ap())
    build(nc, ins, outs)
    r = _run(nc, [arrays], core_ids=[0])
    return tuple(r.results[0][f"out_{i}_dram"] for i in range(len(_OUTS)))
```

```python
from contextlib import ExitStack

import numpy as np

import concourse.bass as bass
from concourse import mybir

F32 = mybir.dt.float32
ALU = mybir.AluOpType
ACT = mybir.ActivationFunctionType
AX = mybir.AxisListType

P = 128
D = 1024
DT = D // P
NPR, NSA = 256, 8
T = NPR + NSA
NSEQ = 1 + NSA
DA = DB = 512
H, HD = 8, 64
QT = DB // P
PB = 3 * DB + 256
PBT = PB // P
PROJ = 3 * DA + PB
PROJT = PROJ // P
CH = 64
NCH = NPR // CH
NE, DE = 64, 256
NG, TOPG = 8, 4
TR = T // 3
EPS, GN_EPS = 1e-6, 64e-5
ROUTE_SCALE = 2.5
BIG = 1e30
EMH = float(np.exp(-0.5))

NSMALL = 20
UNIT = 2048
MSLOTS = 5
ESLOTS = 12
ONE = 1
CAP = 64
MAXR = -(-T // CAP)
MOD_FIRST = 4
PROJ_ORDER = [12, 6, 7, 8, 9, 10, 11, 0, 1, 4, 5, 2, 3]
PROJ_TILE = [2 * u + i for u in PROJ_ORDER for i in range(2)]
MOD_PROJ = [[MOD_FIRST + u] for u in range(13)]
MOD_LATE = MOD_FIRST + sum(len(x) for x in MOD_PROJ)
NPAIR = NE // 2
EBODY = 4
NTURN = NPAIR // EBODY
PU = 6
RU = NPAIR * PU
SEL_R = NPAIR + 2
GAT_R = SEL_R // 2 * 16
XT_R = 2 * (NPAIR + 1)
CB_R = DT * (NPAIR + 1)

C_ID, C_ONE, C_BLK, C_UPS, C_UPI, C_LOS, C_LV0T, C_LV, C_S4 = 0, 128, 256, 384, 512, 640, 768, 896, 896 + 6 * 128
C_TRI = C_S4 + NSEQ
C_IOTA = C_TRI + 64
C_TOK = C_IOTA + T
C_UPT = C_TOK + 3
C_UPF = C_UPT + P
NCONST = C_UPF + P


def shape_constants():
    c = np.zeros((P, NCONST), np.float32)
    i = np.arange(P)
    same = (i[:, None] // CH) == (i[None, :] // CH)
    c[:, C_ID:C_ID + P] = np.eye(P)
    c[:, C_ONE:C_ONE + P] = 1.0
    c[:, C_BLK:C_BLK + P] = same
    c[:, C_UPS:C_UPS + P] = same & (i[:, None] < i[None, :])
    c[:, C_UPI:C_UPI + P] = same & (i[:, None] <= i[None, :])
    c[:, C_LOS:C_LOS + P] = same & (i[:, None] > i[None, :])
    for k in range(6):
        b = 1 << k
        m = ((i[:, None] // (2 * b)) == (i[None, :] // (2 * b))) & (i[:, None] // b % 2 == 0) & (i[None, :] // b % 2 == 1)
        c[:, C_LV + k * P:C_LV + (k + 1) * P] = m
        if k == 0:
            c[:, C_LV0T:C_LV0T + P] = m.T
    for j in range(4):
        for s in range(NSEQ):
            c[32 * j + s, C_S4 + s] = 1.0
    g = np.arange(8)
    c[:, C_TRI:C_TRI + 64] = (g[None, :] < g[:, None]).reshape(1, 64)
    c[:, C_IOTA:C_IOTA + T] = np.arange(T)
    c[:, C_TOK:C_TOK + 3] = i[:, None] + TR * np.arange(3)[None, :]
    c[:, C_UPF:C_UPF + P] = i[:, None] <= i[None, :]
    c[:, C_UPT:C_UPT + P] = i[:, None] < i[None, :]
    return c


def build(nc, ins, outs):
    (x_prompt, x_sample, c_prompt, c_sample, state_conv, state_shift, state_wkv, w_mod, b_mod, norm_g,
     ab_w_in, ab_conv_w, ab_mu, ab_w0, ab_w_decay_up, ab_a0, ab_a_up, ab_g_up, ab_k_k, ab_k_a, ab_r_k,
     ab_gn_g, ab_gn_b, ab_w_out, gm_w_in, gm_b_in, gm_ln_g, gm_ln_b, gm_w_s, gm_b_s, gm_w_out,
     moe_w_router, moe_b_router, moe_w_gate, moe_w_up, moe_w_down, moe_ws_gate, moe_ws_up, moe_ws_down,
     constants) = ins
    (y_prompt, y_sample, conv_p, conv_s, shift_p, shift_s, wkv_p, wkv_s, chunk_v_s) = outs
    vec_scratch = nc.dram_tensor("vec_scratch", (NSA, 6, DB), F32).ap()
    out_scratch = nc.dram_tensor("out_scratch", (NSA * H, HD), F32).ap()

    with ExitStack() as ctx:
        def sb(name, shape):
            return ctx.enter_context(nc.sbuf_tensor(name, shape, F32))

        def sem(name):
            return ctx.enter_context(nc.semaphore(name))

        ring = sb("ring", [P, ESLOTS, UNIT])
        arena = sb("arena", [P, 17600])
        xT = sb("xT", [P, DT, T])
        hT = sb("hT", [P, DT, T])
        K = sb("K", [P, NCONST])
        mod = sb("mod", [P, 2, 6, DT, NSEQ])
        b_modT = sb("b_modT", [P, 2, 6, DT])
        ngT = sb("ngT", [P, 2, 4, DT])
        lora = sb("lora", [P, DB])
        gup = sb("gup", [P, DB])
        router = sb("router", [P, 2, DT, NE])
        brout = sb("brout", [TR, 2, NE])
        vecs = sb("vecs", [P, 64])
        gvec = sb("gvec", [P, 16 + 8 + 8 + 8])
        rstd = sb("rstd", [P, T])
        eps = sb("eps", [P, 2])
        psum = ctx.enter_context(nc.psum_tensor("psum", [P, 8, 512], F32))

        ident = K[:, C_ID:C_ID + P]
        ones = K[:, C_ONE:C_ONE + P]
        blk = K[:, C_BLK:C_BLK + P]
        conv_w, mu = vecs[:, 0:12].rearrange("p (w q) -> p w q", w=3), vecs[:, 12:26]
        w0, a0, k_k, k_a = vecs[:, 26:30], vecs[:, 30:34], vecs[:, 34:38], vecs[:, 38:42]
        r_k, gn_g, gn_b = vecs[:, 42:46], vecs[:, 46:50], vecs[:, 50:54]
        gb_in, ln_g, ln_b, ws00 = gvec[:, 0:16], gvec[:, 16:24], gvec[:, 24:32], gvec[:, 32:40]

        class Arena:
            def __init__(self, base, size):
                self.base, self.at, self.size = base, 0, size

            def take(self, *shape):
                n = int(np.prod(shape))
                v = self.base[:, self.at:self.at + n]
                self.at += n
                assert self.at <= self.size, self.at
                if len(shape) == 2:
                    v = v.rearrange("p (a b) -> p a b", a=shape[0])
                if len(shape) == 3:
                    v = v.rearrange("p (a b c) -> p a b c", a=shape[0], b=shape[1])
                return v

        st = Arena(arena, 17600)
        xtok = st.take(3, D)
        ctok = st.take(D)
        ctok2 = st.take(D)
        cT = ring[:, 5, 0:DT * 32].rearrange("p (c s) -> p c s", c=DT)
        mrow = ring[:, 5, 512:512 + D]

        m0 = Arena(arena, 17600)
        proj = m0.take(PROJT, T)
        xm = m0.take(PBT, T)
        kh, bb, bonus, tmp = (m0.take(QT, T) for _ in range(4))
        Uz = m0.take(2, 512)
        rhs_s = m0.take(512)
        S0T = m0.take(QT, HD)
        s_tmp = m0.take(16, HD)
        side_mem = sb("side_mem", [P, 16 + 2 * HD + 6 * HD])
        PC = side_mem[:, 0:16].rearrange("p (c q) -> p c q", c=NCH)
        s_u, s_o = side_mem[:, 16:80], side_mem[:, 80:144]
        svec = side_mem[:, 144:528].rearrange("p (v j) -> p v j", v=6)
        a_sig = proj[:, 0:4, :]
        kk = proj[:, 4:8, :]
        g_t = proj[:, 8:12, :]
        pb = proj[:, 12:26, :]
        ld = proj[:, 12:16, :]
        cs = proj[:, 16:20, :]
        px = proj[:, 20:24, :]
        r_, k_, v_ = xm[:, 0:4, :], xm[:, 4:8, :], xm[:, 8:12, :]
        flat = lambda a, b: arena[:, a * T:b * T]
        Lmat = flat(12, 26)[:, 0:2048].rearrange("p (m h t) -> p m h t", m=2, h=H)
        L1, L2T = Lmat[:, 0], Lmat[:, 1]
        Rmat = flat(0, 8)[:, 0:2048].rearrange("p (m h t) -> p m h t", m=2, h=H)
        R1T, R2T = Rmat[:, 0], Rmat[:, 1]
        XY = flat(26, 34)[:, 0:2048].rearrange("p (m h t) -> p m h t", m=2, h=H)
        X = XY[:, 0]
        Y = (XY[:, 1], flat(52, 56)[:, 0:1024].rearrange("p (h t) -> p h t", h=H))
        Z = flat(34, 38)[:, 0:1024].rearrange("p (h t) -> p h t", h=H)
        chunk_mem = Arena(ring[:, 8:12, :].rearrange("p s n -> p (s n)"), 8192)
        Az, Rz = chunk_mem.take(H, NPR), chunk_mem.take(H, NPR)
        Vz = chunk_mem.take(2, 2, 512)
        Btok, Ktok = chunk_mem.take(2, 512), chunk_mem.take(2, 512)
        sh_in = ring[0:NSA, 8, 0:PB]
        cv_in = ring[0:NSA, 9, 0:2 * DA].rearrange("p (w n) -> p w n", w=2)
        conv_mem = Arena(ring[:, 8:12, :].rearrange("p s n -> p (s n)"), 8192)
        conv_in, conv_t = conv_mem.take(12, T), conv_mem.take(QT, T)
        sh_out = ring[0:NSEQ, 10, 256:256 + PB]
        cv_out = s_tmp[0:10].rearrange("p i j -> p (i j)")[:, 0:DA]
        stT = sb("stT", [P, 176])
        st_shift = stT[:, 0:112].rearrange("p (q s) -> p q s", q=PBT)
        st_conv = stT[:, 112:176].rearrange("p (w q s) -> p w q s", w=2, q=QT)
        upi_full = K[:, C_UPF:C_UPF + P]
        wkv_o = flat(34, 38)[:, 0:512].rearrange("p (h j) -> p h j", h=H)
        S_s = ring[0:64, 6:8, :].rearrange("p s (i j) -> p (s i) j", j=HD)
        outT = hT[:, 4:8, :]

        ACT_NORMS, DVE_NORMS = (2, 4, 6), (0, 1, 3, 5, 7)

        def squares(k):
            return arena[:, 12 * T:20 * T].rearrange("p (c t) -> p c t", c=DT) if k == 1 else hT

        y_a = hT[:, 0:4, :]

        m1 = Arena(arena, 17600)
        z = m1.take(16, T)
        gt1, gt2 = m1.take(8, T), m1.take(8, T)
        vtok = m1.take(2, D)
        wsn = m1.take(8, P)
        wsT = m1.take(8, P)
        bsb = m1.take(8, P)
        vs_out = m1.take(D)
        mu_b = m1.take(T)

        me = Arena(arena, 17600)
        yacc = me.take(DT, T)
        xg = [me.take(DT, P) for _ in range(2)]
        xgT = [me.take(DT, P) for _ in range(2)]
        slotsel = me.take(3, 2, CAP)
        selT = [me.take(T) for _ in range(4)]
        wt = me.take(4)
        idxf = me.take(4)
        gsil, ghid = me.take(DE), me.take(DE)
        ghT = me.take(2, P)
        gout = me.take(D)
        posm = me.take(3, NE + 4)
        comb = me.take(3, NE + 4)
        htok = me.take(3, D)
        score, sel, selm, rep, mask = (me.take(3, NE) for _ in range(5))
        gt8 = me.take(3, NG, 8)
        grp, rank, gm = me.take(3, NG), me.take(3, NG), me.take(3, NG)
        cmp1, cmp2 = me.take(3, 64), me.take(3, 64)
        top8 = me.take(3, 8)
        csum, cmax, cthr = me.take(3), me.take(1), me.take(4)
        ssil, shid = me.take(2, T), me.take(2, T)
        mx = Arena(arena, 17600)
        mx.at = DT * T
        xo = mx.take(3, D)

        S = {}

        def signals(*names):
            for n in names:
                S[n] = sem(n)

        signals("const_in", "const2_in", "c_in", "x_in", "modp_in", "small_in", "state_in", "swkv_in", "gmisc_in")
        signals("vec", "pool_step", "store", "conv_out", "shift_out")
        signals("silu_c", "c_tr", "c_sb", "x_tr", "x_sb", "mod_mm", "mod_row", "mod_tr", "mod_set")
        signals("sq_ready", "sq_act", "ss_mm", "sd_ready", "y_done", "norm_half", "h_ready", "h_act")
        signals("proj_mm", "proj_sb", "st_tr", "st_sb", "mixed", "tail_ready", "tail_tr", "tail_sb", "conv_done", "zeros")
        signals("lora_in", "lora_mm", "lora_sb", "cs_ready", "exp_step", "exp_ready", "kksq_ready", "kkss_mm", "kknorm",
                "rk_ready", "rk_mm", "pad_ready", "ops_ready", "tok_tr", "tok_sb")
        signals("gram_mm", "gram_sb", "xy0", "z_mm", "z_sb", "d_mm", "xy", "rhs_mm", "rhs_sb", "u_mm", "u_sb",
                "o_mm", "o_sb", "s_mm", "s_sb", "wkv_tr", "wkv_sb", "rwkv_free")
        signals("svec_tr", "svec_sb", "svec_out", "svec_in", "samp_out", "samp_in", "samp_tr", "samp_sb")
        signals("gn_mm", "gn_c", "gn_sd", "yab_ready", "out_mm", "out_sb")
        signals("z_mm1", "z_sb1", "vmu_mm", "vc_ready", "vvar_mm", "ln_sd", "v_ready", "ws_tr", "ws_sb", "vt_tr", "vt_sb",
                "vs_sb", "vs_stored", "sg_mm", "sg_ready")
        signals("logit_mm", "score_ready", "mask_ready", "rank_mm", "htr_mm", "htr_sb", "htok_out",
                "sh_mm", "sh_act", "sh_hid", "shd_mm", "shd_sb", "fin_tr", "fin_sb")
        signals("round_set", "sel", "slot_mm", "idx", "gat_a", "gat_b", "gather_go", "xt_mm", "xt_sb", "gsil", "ghid",
                "ht_mm", "ht_sb", "os_a", "os_b", "cb_mm", "cb_add", "unit_used", "idxf", "next")
        mload = [sem(f"mload{i}") for i in range(MSLOTS)]
        eload = [sem(f"eload{i}") for i in range(ESLOTS)]
        h_rows = [nc.dram_tensor(f"h_rows{l}", (T, D), F32).ap() for l in range(2)]
        nrounds = ctx.enter_context(nc.sbuf_tensor("nrounds", [P, 2], mybir.dt.int32))
        rounds = sb("rounds", [P, 2])
        slot_idx = ctx.enter_context(nc.sbuf_tensor("slot_idx", [P, 4], mybir.dt.uint32))
        so_tok = s_tmp[0:NSA].rearrange("p i j -> p (i j)")[:, 0:DB]

        def gram_bank(g):
            return g % 4 if g < 4 or 10 <= g < 14 else 4 + g % 2 if g < 10 else 4 + g % 4

        svec_tok = [(v, n, b.rearrange("p (v n) -> p v n", v=n)) for v, n, b in (
            (0, 2, tmp[0:NSA].rearrange("p a t -> p (a t)")[:, 0:2 * DB]),
            (2, 2, outT[0:NSA].rearrange("p a t -> p (a t)")[:, 0:2 * DB]),
            (4, 1, Uz[0:NSA, 0]), (5, 1, rhs_s[0:NSA]))]

        mix_units, mod_unit, proj_unit = [], [], []
        wm = w_mod.rearrange("l (p c) n -> l p c n", c=DT)
        wi = ab_w_in[0].rearrange("(p c) n -> p c n", c=DT)

        def half_units(k):
            for u in (2 * k, 2 * k + 1):
                mod_unit.append(len(mix_units))
                mix_units.append(("mod", wm[u // 24, :, :, u % 24 * 256:(u % 24 + 1) * 256], DT))

        for k in range(MOD_FIRST):
            half_units(k)
        for u in range(PROJT // 2):
            proj_unit.append(len(mix_units))
            mix_units.append(("proj", wi[:, :, PROJ_ORDER[u] * 256:(PROJ_ORDER[u] + 1) * 256], DT))
            for k in MOD_PROJ[u]:
                half_units(k)
        for k in range(MOD_LATE, 24):
            half_units(k)
        U_ABO = len(mix_units)
        wo = ab_w_out[0].rearrange("(q p) n -> p q n", p=P)
        for u in range(4):
            mix_units.append(("abo", wo[:, 2 * u:2 * u + 2, :], 2))

        def shared_units(l):
            mix_units.append(("shg", moe_ws_gate[l].rearrange("(p c) f -> p c f", c=DT), DT))
            mix_units.append(("shu", moe_ws_up[l].rearrange("(p c) f -> p c f", c=DT), DT))
            mix_units.append(("shd", moe_ws_down[l].rearrange("(p j) n -> p j n", j=2), 2))

        shared_units(0)
        N0 = len(mix_units)
        gi = gm_w_in[0].rearrange("(p c) n -> p c n", c=DT)
        for u in (4, 5, 6, 7, 0, 1, 2, 3):
            mix_units.append(("gmi", gi[:, :, u * 256:(u + 1) * 256], DT))
        go = gm_w_out[0].rearrange("(q p) n -> p q n", p=P)
        for u in range(4):
            mix_units.append(("gmo", go[:, 2 * u:2 * u + 2, :], 2))
        shared_units(1)
        N1 = len(mix_units)
        U_GMI, U_GMO = N0, N0 + 8
        U_SH = (N0 - 3, N1 - 3)

        def mix_view(n):
            kind, src, a = mix_units[n]
            return ring[:, n % MSLOTS, :].rearrange("p (a n) -> p a n", a=a)

        def eslot(j):
            return (j + PU) % ESLOTS

        block = ctx.enter_context(nc.Block())

        @block.sync
        def _(sp):
            def load(dst, src, s):
                sp.dma_start(dst, src).then_inc(S[s], 16)

            load(ctok[0:1, :], c_prompt, "c_in")
            load(ctok[1:NSEQ, :], c_sample, "c_in")
            load(K[:, 0:C_BLK], constants[:, 0:C_BLK], "const_in")
            load(K[:, C_S4:C_TRI], constants[:, C_S4:C_TRI], "const_in")

            def wait_used(n):
                kind, l = mix_units[n][0], int(n >= N0)
                if kind == "mod":
                    sp.wait_ge(S["mod_mm"], mod_unit.index(n) + 1)
                elif kind == "proj":
                    sp.wait_ge(S["proj_mm"], 2 * (proj_unit.index(n) + 1))
                elif kind == "gmi":
                    sp.wait_ge(S["z_mm1"], 2 * (n - U_GMI + 1))
                elif kind in ("abo", "gmo"):
                    sp.wait_ge(S["out_mm"], 8 * (l + 1))
                elif kind in ("shg", "shu"):
                    sp.wait_ge(S["sh_mm"], 2 * l + (1 if kind == "shg" else 2))
                else:
                    sp.wait_ge(S["shd_mm"], 8 * (l + 1))

            def mix_load(n):
                if n >= MSLOTS:
                    wait_used(n - MSLOTS)
                sp.dma_start(mix_view(n), mix_units[n][1]).then_inc(mload[n % MSLOTS], 16)

            for n in range(2):
                mix_load(n)
            load(xtok[:, 0:2, :], x_prompt[0].rearrange("(t p) d -> p t d", p=P), "x_in")
            load(xtok[0:NSA, 2, :], x_sample[:, 0, :], "x_in")
            for n in range(2, 12):
                mix_load(n)
            load(sh_in, state_shift[0], "state_in")
            load(cv_in, state_conv[0], "state_in")
            for n in range(12, 26):
                mix_load(n)
            load(K[:, C_BLK:C_S4], constants[:, C_BLK:C_S4], "const2_in")
            load(K[:, C_TRI:NCONST], constants[:, C_TRI:NCONST], "const2_in")
            load(S_s, state_wkv[0].rearrange("b h i j -> (b h) i j"), "swkv_in")
            for n in range(26, N0 - 2):
                mix_load(n)

            def expert_load(l, pair2, j):
                sp.dma_start(ring[:, eslot(j), :], expert_src(l, pair2 + (j // PU * 2 + j % 2), j % PU // 2)).then_inc(eload[eslot(j)], 16)

            def experts(l, last):
                for n, j in sorted((last - 1 - ((last - 1 - j) % MSLOTS), j) for j in range(MSLOTS)):
                    wait_used(n)
                    expert_load(l, 0, PU + j)
                sp.wait_ge(S["round_set"], l + 1)
                first = sp.value_load(nrounds[0:1, 0:1], min_val=1, max_val=MAXR) if l else 0
                end = sp.value_load(nrounds[0:1, l:l + 1], min_val=1, max_val=(l + 1) * MAXR)
                with sp.Fori(first, end) as r:
                    with sp.Fori(0, RU // ESLOTS - 1) as i:
                        for j in range(ESLOTS):
                            sp.wait_ge(S["unit_used"], r * RU + i * ESLOTS + (j + 1) + ONE)
                            expert_load(l, (i + 1) * 4, j)
                    with sp.If(r + 1 < end):
                        for j in range(ESLOTS):
                            sp.wait_ge(S["unit_used"], r * RU + (RU - ESLOTS) + (j + 1) + ONE)
                            expert_load(l, 0, j)

                if l == 0:
                    sp.wait_ge(S["unit_used"], end * RU + ONE)

            def expert_src(l, e, kind):
                w = (moe_w_gate, moe_w_up, moe_w_down)[kind]
                src = w[l, e] if isinstance(e, int) else w[l, bass.ds(e, 1)].rearrange("o a b -> (o a) b")
                return src.rearrange("(p c) n -> p (c n)", p=P)

            def free_slots(l):
                for j in range(PU):
                    expert_load(l, 0, j)
                expert_load(l, 0, PU + MSLOTS)

            sp.wait_ge(S["mod_tr"], 12)
            sp.wait_ge(S["rwkv_free"], 1)
            sp.wait_ge(S["wkv_sb"], 1)
            free_slots(0)
            mix_load(N0 - 2)
            mix_load(N0 - 1)
            experts(0, N0)
            for n in range(N0, N1):
                if n == N0 + MSLOTS:
                    free_slots(1)
                mix_load(n)
            experts(1, N1)

        @block.gpsimd
        def _(pool):
            def load(dst, src, s):
                pool.dma_start(dst, src).then_inc(S[s], 16)

            for name in ("ht_sb", "gsil", "ghid", "os_a", "os_b", "cb_add", "unit_used", "ht_mm"):
                pool.sem_inc(S[name], ONE)

            with nc.allow_non_contiguous_dma(reason="small vectors"):
                load(b_modT[:, :, :, :].rearrange("p l a c -> p (l a) c"), b_mod.rearrange("l (a p c) -> p (l a) c", a=6, c=DT), "modp_in")
                load(ngT[:, :, :, :].rearrange("p l a c -> p (l a) c"), norm_g.rearrange("l a (p c) -> p (l a) c", c=DT), "modp_in")
                pool.wait_ge(S["mod_mm"], 2 * MOD_FIRST)
                load(conv_w, ab_conv_w[0].rearrange("w (q p) -> p w q", p=P), "small_in")
                load(mu, ab_mu[0].rearrange("(q p) -> p q", p=P), "small_in")
                for dst, src in ((w0, ab_w0), (a0, ab_a0), (k_k, ab_k_k), (k_a, ab_k_a), (gn_g, ab_gn_g), (gn_b, ab_gn_b)):
                    load(dst, src[0].rearrange("(q p) -> p q", p=P), "small_in")
                load(r_k, ab_r_k[0].rearrange("(q a) j -> (a j) q", a=2), "small_in")
                load(lora[0:64, :], ab_w_decay_up[0], "small_in")
                load(lora[64:128, :], ab_a_up[0], "small_in")
                load(gup[:, :], ab_g_up[0], "small_in")
                for l in range(2):
                    load(router[:, l], moe_w_router[l].rearrange("(p c) n -> p c n", c=DT), "small_in")
                    load(brout[:, l], moe_b_router[l].partition_broadcast(TR), "small_in")
                load(gb_in, gm_b_in[0].rearrange("(q p) -> p q", p=P), "small_in")
                load(ln_g, gm_ln_g[0].rearrange("(q p) -> p q", p=P), "small_in")
                load(ln_b, gm_ln_b[0].rearrange("(q p) -> p q", p=P), "small_in")
                load(ws00, gm_w_s[0, :, 0, 0].partition_broadcast(P), "small_in")

                pool.wait_ge(S["state_in"], 32)
                pool.dma_start(conv_s[0, :, 0, :], cv_in[:, 1, :]).then_inc(S["conv_out"], 16)
                pool.wait_ge(S["tail_sb"], 1)
                pool.dma_start(shift_p[0], sh_out[0:1, :]).then_inc(S["shift_out"], 16)
                pool.dma_start(shift_s[0], sh_out[1:NSEQ, :]).then_inc(S["shift_out"], 16)

                pool.wait_ge(S["svec_sb"], 1)
                for v, n, buf in svec_tok:
                    pool.dma_start(vec_scratch[:, v:v + n, :], buf).then_inc(S["svec_out"], 16)
                pool.wait_ge(S["conv_done"], 1)
                pool.wait_ge(S["tail_tr"], 2)
                pool.wait_ge(S["shift_out"], 32)
                for o in range(2):
                    other = slice(64 - 64 * o, 128 - 64 * o)
                    nc.gpsimd.memset(Az[other, o::2, :], 0.0).then_inc(S["zeros"], 1)
                    nc.gpsimd.memset(Rz[other, o::2, :], 0.0).then_inc(S["zeros"], 1)
                nc.gpsimd.memset(Vz[64:128, 0], 0.0).then_inc(S["zeros"], 1)
                nc.gpsimd.memset(Vz[0:64, 1], 0.0).then_inc(S["zeros"], 1)
                pool.wait_ge(S["svec_out"], 64)
                for b in range(NSA):
                    pool.dma_start(svec[8 * b:8 * b + 8], vec_scratch[b].rearrange("v (h j) -> h v j", j=HD)).then_inc(S["svec_in"], 16)
                pool.wait_ge(S["tail_sb"], 2)
                pool.dma_start(conv_p[0, 0], cv_out[0:2, :]).then_inc(S["store"], 16)
                pool.dma_start(conv_s[0, :, 1, :], cv_out[2:10, :]).then_inc(S["store"], 16)
            pool.wait_ge(S["store"], 32)
            pool.wait_ge(S["svec_in"], 16 * NSA)
            pool.wait_ge(S["swkv_in"], 16)

            n = [0]

            def step(i):
                n[0] += 1
                i.then_inc(S["pool_step"], 1)
                pool.wait_ge(S["pool_step"], n[0])

            r_v, w_v, k_v, v_v, kk_v, b_v = (svec[0:64, i, :] for i in range(6))
            rows = lambda v, i0: v.unsqueeze(1).broadcast_to([64, 16, HD])
            cols = lambda v, i0: v[:, i0:i0 + 16].unsqueeze(2).broadcast_to([64, 16, HD])
            t = s_tmp[0:64]

            def row_sums(out):
                for n in (32, 16, 8, 4, 2):
                    step(nc.gpsimd.tensor_tensor(t[:, :, 0:n], t[:, :, 0:n], t[:, :, n:2 * n], ALU.add))
                step(nc.gpsimd.tensor_tensor(out, t[:, :, 0], t[:, :, 1], ALU.add))

            for i0 in range(0, HD, 16):
                Sp = S_s[:, i0:i0 + 16, :]
                step(nc.gpsimd.tensor_tensor(t, Sp, rows(kk_v, i0), ALU.mult))
                row_sums(s_u[0:64, i0:i0 + 16])
                step(nc.gpsimd.tensor_tensor(Sp, Sp, rows(w_v, i0), ALU.mult))
                step(nc.gpsimd.tensor_tensor(t, cols(s_u[0:64], i0), rows(b_v, i0), ALU.mult))
                step(nc.gpsimd.tensor_tensor(Sp, Sp, t, ALU.subtract))
                step(nc.gpsimd.tensor_tensor(t, cols(v_v, i0), rows(k_v, i0), ALU.mult))
                step(nc.gpsimd.tensor_tensor(Sp, Sp, t, ALU.add))
                step(nc.gpsimd.tensor_tensor(t, Sp, rows(r_v, i0), ALU.mult))
                row_sums(s_o[0:64, i0:i0 + 16])
            pool.dma_start(wkv_s[0].rearrange("b h i j -> (b h) i j"), S_s).then_inc(S["store"], 16)
            pool.dma_start(out_scratch, s_o[0:64, :]).then_inc(S["samp_out"], 16)
            pool.wait_ge(S["samp_out"], 16)
            pool.dma_start(so_tok, out_scratch.rearrange("(b h) i -> b (h i)", h=H)).then_inc(S["samp_in"], 16)
            pool.wait_ge(S["store"], 48)
            pool.wait_ge(S["wkv_sb"], 1)
            pool.dma_start(wkv_p[0, 0].rearrange("h i j -> i h j"), wkv_o[0:64]).then_inc(S["store"], 16)
            pool.wait_ge(S["store"], 64)
            pool.wait_ge(S["s_sb"], NCH)
            pool.sem_inc(S["rwkv_free"], 1)

            def moe(l):
                pool.wait_ge(S["htr_sb"], 6 * l + 6)
                pool.dma_start(h_rows[l].rearrange("(t p) d -> p t d", p=TR), htok[0:TR]).then_inc(S["htok_out"], 16)
                pool.wait_ge(S["htok_out"], 16 * (l + 1))
                pool.wait_ge(S["round_set"], l + 1)
                first = pool.value_load(nrounds[0:1, 0:1], min_val=1, max_val=MAXR) if l else 0
                end = pool.value_load(nrounds[0:1, l:l + 1], min_val=1, max_val=(l + 1) * MAXR)

                def gather(jj, count):
                    pool.wait_ge(S["idx"], count)
                    pool.sem_inc(S["gather_go"], 1)
                    pool.indirect_dma_start(xg[jj % 2].rearrange("p c d -> p (c d)"), None, h_rows[l],
                                            bass.IndirectOffsetOnAxis(slot_idx[:, jj:jj + 1], 0)).then_inc(S["gat_" + "ab"[jj % 2]], 16)

                def first_pairs(r):
                    for j in range(2):
                        if not isinstance(r, int):
                            pool.wait_ge(S["xt_mm"], r * XT_R)
                        gather(j, r * SEL_R + (j + 1))

                first_pairs(first)
                with pool.Fori(first, end) as r:
                    with pool.Fori(0, NTURN) as i:
                        for b in range(EBODY):
                            pool.wait_ge(S["xt_mm"], r * XT_R + i * 8 + (2 * b + 2))
                            gather((b + 2) % 4, r * SEL_R + i * EBODY + (b + 3))
                    with pool.If(r + 1 < end):
                        first_pairs(r + 1)

            moe(0)
            pool.wait_ge(S["y_done"], 2 * DT)
            pool.dma_start(wsn, gm_w_s[0].rearrange("g i j -> i g j")).then_inc(S["gmisc_in"], 16)
            pool.dma_start(bsb, gm_b_s[0].partition_broadcast(P)).then_inc(S["gmisc_in"], 16)
            pool.wait_ge(S["vs_sb"], 1)
            pool.dma_start(chunk_v_s[0, :, 0, :], vs_out[0:NSA, :]).then_inc(S["store"], 16)
            pool.wait_ge(S["store"], 80)
            pool.sem_inc(S["vs_stored"], 1)
            moe(1)
            pool.wait_ge(S["fin_sb"], 6)
            pool.dma_start(y_prompt[0, 0:2 * TR, :].rearrange("(t p) d -> p t d", p=TR), xo[0:TR, 0:2, :]).then_inc(S["store"], 16)
            pool.dma_start(y_prompt[0, 2 * TR:NPR, :], xo[0:NPR - 2 * TR, 2, :]).then_inc(S["store"], 16)
            pool.dma_start(y_sample[:, 0, :], xo[NPR - 2 * TR:TR, 2, :]).then_inc(S["store"], 16)
            pool.wait_ge(S["store"], 128)
            pool.wait_ge(S["conv_out"], 16)
            pool.wait_ge(S["shift_out"], 32)

        @block.tensor
        def _(pe):
            def mm(out, lhsT, rhs, start=True, stop=True):
                return nc.tensor.matmul(out, lhsT, rhs, start=start, stop=stop)

            def tr(out, in_):
                return nc.tensor.transpose(out, in_, ident[0:in_.shape[0], 0:in_.shape[0]])

            def arrived(n):
                pe.wait_ge(mload[n % MSLOTS], 16 * (n // MSLOTS + 1))

            def sum_squares(k):
                for c in range(DT):
                    if k in ACT_NORMS:
                        pe.wait_ge(S["sq_act"], DT * ACT_NORMS.index(k) + c + 1)
                    else:
                        pe.wait_ge(S["sq_ready"], DT * DVE_NORMS.index(k) + c + 1)
                    last = mm(psum[:, 7, 0:T], ones, squares(k)[:, c, :], c == 0, c == DT - 1)
                last.then_inc(S["ss_mm"], 1)

            pe.wait_ge(S["const_in"], 32)
            pe.wait_ge(S["silu_c"], 1)
            for c in range(DT):
                last = tr(psum[:, 5, c * NSEQ:(c + 1) * NSEQ], ctok2[0:NSEQ, c::DT])
            last.then_inc(S["c_tr"], 1)
            def mod_turn(g):
                pe.wait_ge(S["mod_row"], 2 * (g + 1))
                if g >= 1:
                    pe.wait_ge(S["mod_set"], g)
                for c in range(DT):
                    last = mm(psum[:, 7, c * NSEQ:(c + 1) * NSEQ], mrow[:, c::DT], K[:, C_S4:C_S4 + NSEQ])
                last.then_inc(S["mod_tr"], 1)

            def mod_half(k):
                if k >= 1:
                    pe.wait_ge(S["mod_row"], k)
                if k % 2 == 0 and k not in (0, MOD_FIRST):
                    mod_turn(k // 2 - 1)
                for u in (2 * k, 2 * k + 1):
                    arrived(mod_unit[u])
                    w = mix_view(mod_unit[u])
                    for k2 in range(2):
                        for j in range(4):
                            last = mm(psum[32 * j:32 * j + 32, 6, (u % 2) * 256:(u % 2 + 1) * 256], cT[:, 4 * k2 + j, :],
                                      w[:, 4 * k2 + j, :], k2 == 0, k2 == 1)
                    last.then_inc(S["mod_mm"], 1)

            pe.wait_ge(S["c_sb"], 1)
            mod_half(0)
            pe.wait_ge(S["x_in"], 32)
            for t in range(2):
                for c in range(DT):
                    last = tr(psum[:, 2 * t + c // 4, (c % 4) * P:(c % 4 + 1) * P], xtok[:, t, c::DT])
                last.then_inc(S["x_tr"], 1)
            for c in range(DT):
                last = tr(psum[:, 4, c * NSA:(c + 1) * NSA], xtok[0:NSA, 2, c::DT])
            last.then_inc(S["x_tr"], 1)
            mod_half(1)
            sum_squares(0)
            pe.wait_ge(S["sd_ready"], 1)
            mod_half(2)
            mod_half(3)
            mod_turn(1)

            pe.wait_ge(S["x_sb"], 3)
            pe.wait_ge(S["h_ready"], 1)

            def beside_projection(pos):
                if pos == 5:
                    pe.wait_ge(S["state_in"], 32)
                    for q in range(PBT):
                        tr(psum[:, 4, q * NSA:(q + 1) * NSA], sh_in[:, q * P:(q + 1) * P])
                    for w in range(2):
                        for q in range(QT):
                            last = tr(psum[:, 4, (PBT + w * QT + q) * NSA:(PBT + w * QT + q + 1) * NSA], cv_in[:, w, q * P:(q + 1) * P])
                    last.then_inc(S["st_tr"], 1)
                elif pos == 14:
                    pe.wait_ge(S["const2_in"], 32)
                    pe.wait_ge(S["proj_sb"], 14)
                    pe.wait_ge(S["st_sb"], 2)
                    for q in range(PBT):
                        last = tr(psum[0:NSEQ, 2 + q // 4, (q % 4) * P:(q % 4 + 1) * P], pb[:, q, NPR - 1:T])
                    last.then_inc(S["tail_tr"], 1)
                elif pos == 16:
                    pe.wait_ge(S["small_in"], 16 * NSMALL)
                    pe.wait_ge(S["lora_in"], 2)
                    pe.wait_ge(S["tail_sb"], 1)
                    for q in range(QT):
                        last = mm(psum[:, 2 + q, 0:T], lora[0:64, q * P:(q + 1) * P], xm[0:64, 12, :])
                    last.then_inc(S["lora_mm"], 1)
                elif pos == 17:
                    pe.wait_ge(S["lora_sb"], 1)
                    for q in range(QT):
                        last = mm(psum[:, 2 + q, 0:T], lora[64:128, q * P:(q + 1) * P], xm[64:128, 12, :])
                    last.then_inc(S["lora_mm"], 1)
                elif pos == 18:
                    pe.wait_ge(S["lora_sb"], 2)
                    for q in range(QT):
                        last = mm(psum[:, 2 + q, 0:T], gup[:, q * P:(q + 1) * P], xm[:, 13, :])
                    last.then_inc(S["lora_mm"], 1)
                elif pos == 20:
                    pe.wait_ge(S["lora_sb"], 3)
                    pe.wait_ge(S["kksq_ready"], 1)
                    for q in range(QT):
                        last = mm(psum[:, 2 + q, 0:T], blk, tmp[:, q, :])
                    last.then_inc(S["kkss_mm"], 1)
                elif pos == 22:
                    pe.wait_ge(S["kknorm"], 1)
                    pe.wait_ge(S["rk_ready"], 1)
                    for q in range(QT):
                        last = mm(psum[:, 2 + q, 0:T], blk, bonus[:, q, :])
                    last.then_inc(S["rk_mm"], 1)

            for pos in range(PROJT):
                m, n = PROJ_TILE[pos], proj_unit[pos // 2]
                if pos % 2 == 0:
                    arrived(n)
                if pos >= 2:
                    pe.wait_ge(S["proj_sb"], pos - 1)
                w = mix_view(n)
                for c in range(DT):
                    last = mm(psum[:, pos % 2, 0:T], w[:, c, (m % 2) * P:(m % 2 + 1) * P], hT[:, c, :], c == 0, c == DT - 1)
                last.then_inc(S["proj_mm"], 1)
                if pos % 2:
                    for k in MOD_PROJ[pos // 2]:
                        mod_half(k)
                beside_projection(pos)

            pe.wait_ge(S["proj_sb"], PROJT)
            pe.wait_ge(S["pad_ready"], 1)
            pe.wait_ge(S["exp_ready"], 1)
            for v, src in enumerate((r_, cs, kh, v_, kk, bb)):
                for q in range(QT):
                    last = tr(psum[0:NSA, v, q * P:(q + 1) * P], src[:, q, NPR:T])
            last.then_inc(S["svec_tr"], 1)
            pe.wait_ge(S["mod_set"], 8)
            pe.wait_ge(S["tail_ready"], 1)
            for q in range(QT):
                last = tr(psum[0:10, 7, q * P:(q + 1) * P], conv_in[:, 8 + q, NPR - 2:T])
            last.then_inc(S["tail_tr"], 1)
            mod_half(17)
            pe.wait_ge(S["svec_sb"], 1)
            pe.wait_ge(S["pad_ready"], 2)
            for t in range(2):
                for v, src in enumerate((v_, bb, kh)):
                    for q in range(QT):
                        last = tr(psum[:, 3 * t + v, q * P:(q + 1) * P], src[:, q, t * P:(t + 1) * P])
            last.then_inc(S["tok_tr"], 1)
            pe.wait_ge(S["tail_sb"], 2)
            mod_half(18)
            mod_half(19)
            pe.wait_ge(S["ops_ready"], 1)
            pe.wait_ge(S["tok_sb"], 2)

            pairs = ((Az, bb), (bb, Az), (kh, Az), (bb, Rz), (kh, Rz))

            def side(a, h, t):
                return a[:, h if a.shape[1] == H else h // 2, t * P:(t + 1) * P]

            def gram_products(t, m):
                for hh in range(2):
                    g = t * 10 + m * 2 + hh
                    if 6 <= g < 10:
                        pe.wait_ge(S["gram_sb"], g - 1)
                    elif g >= 18:
                        pe.wait_ge(S["gram_sb"], g - 3)
                    for h in range(4 * hh, 4 * hh + 4):
                        last = mm(psum[:, gram_bank(g), (h % 4) * P:(h % 4 + 1) * P], side(pairs[m][0], h, t), side(pairs[m][1], h, t))
                    last.then_inc(S["gram_mm"], 1)

            def level_z(t, k):
                for hh in range(2):
                    n = t * 10 + (k - 1) * 2 + hh
                    if n >= 2:
                        pe.wait_ge(S["xy"], n - 1)
                    for h in range(4 * hh, 4 * hh + 4):
                        last = mm(psum[:, 2 * hh, (h % 4) * P:(h % 4 + 1) * P], L1[:, h, :], Y[t][:, h, :])
                    last.then_inc(S["z_mm"], 1)

            def level_d(t, k):
                for hh in range(2):
                    pe.wait_ge(S["z_sb"], t * 10 + (k - 1) * 2 + hh + 1)
                    for h in range(4 * hh, 4 * hh + 4):
                        last = mm(psum[:, 2 * hh, (h % 4) * P:(h % 4 + 1) * P], X[:, h, :], Z[:, h, :])
                    for h in range(4 * hh, 4 * hh + 4):
                        if k == 5:
                            break
                        last = mm(psum[:, 2 * hh + 1, (h % 4) * P:(h % 4 + 1) * P], Z[:, h, :], X[:, h, :])
                    last.then_inc(S["d_mm"], 1)

            def chunk_rhs(c):
                t, p0, par = c // 2, 64 * (c % 2), c % 2
                if c >= 1:
                    pe.wait_ge(S["s_sb"], c)
                for h in range(H):
                    o = psum[p0:p0 + 64, 6, h * 64:(h + 1) * 64]
                    if c >= 1:
                        mm(o, Az[:, h, c * CH:(c + 1) * CH], S0T[:, h // 2, :], True, False)
                    last = mm(o, L2T[:, h, p0:p0 + 64], Vz[:, par, t, h * 64:(h + 1) * 64], c == 0, True)
                last.then_inc(S["rhs_mm"], 1)

            def chunk_u(c):
                pe.wait_ge(S["rhs_sb"], c + 1)
                p0 = 64 * (c % 2)
                for h in range(H):
                    last = mm(psum[p0:p0 + 64, 7, h * 64:(h + 1) * 64], Y[c // 2][:, h, p0:p0 + 64], rhs_s[:, h * 64:(h + 1) * 64])
                last.then_inc(S["u_mm"], 1)

            def chunk_out(c):
                pe.wait_ge(S["u_sb"], c + 1)
                t, p0, par = c // 2, 64 * (c % 2), c % 2
                for h in range(H):
                    ps = slice(64 * (h % 2), 64 * (h % 2) + 64)
                    o = psum[ps, 4, (h // 2) * 64:(h // 2 + 1) * 64]
                    if c >= 1:
                        mm(o, S0T[:, h // 2, :], Rz[:, h, c * CH:(c + 1) * CH], True, False)
                    mm(o, Uz[:, par, h * 64:(h + 1) * 64], R1T[:, h, p0:p0 + 64], c == 0, False)
                    last = mm(o, Vz[:, par, t, h * 64:(h + 1) * 64], R2T[:, h, p0:p0 + 64], False, True)
                last.then_inc(S["o_mm"], 1)
                for h in range(H):
                    ps = slice(64 * (h % 2), 64 * (h % 2) + 64)
                    o = psum[ps, 5, (h // 2) * 64:(h // 2 + 1) * 64]
                    mm(o, Btok[:, t, h * 64:(h + 1) * 64], Uz[:, par, h * 64:(h + 1) * 64], True, False)
                    last = mm(o, Ktok[:, t, h * 64:(h + 1) * 64], Vz[:, par, t, h * 64:(h + 1) * 64], False, True)
                last.then_inc(S["s_mm"], 1)

            pe.wait_ge(S["zeros"], 6)
            gram_products(0, 0)
            gram_products(0, 1)
            mod_half(20)
            pe.wait_ge(S["xy0"], 2)
            for k in range(1, 6):
                level_z(0, k)
                if k <= 3:
                    gram_products(0, k + 1)
                if k in (2, 4):
                    mod_half(20 + k // 2)
                level_d(0, k)
            pe.wait_ge(S["xy"], 10)
            gram_products(1, 0)
            gram_products(1, 1)
            mod_half(23)
            mod_turn(11)
            pe.wait_ge(S["xy0"], 4)
            pe.wait_ge(S["gram_sb"], 10)
            pe.wait_ge(S["mod_row"], 24)
            level_z(1, 1)
            chunk_rhs(0)
            level_d(1, 1)
            pe.wait_ge(S["mod_set"], 12)
            chunk_u(0)
            level_z(1, 2)
            chunk_out(0)
            level_d(1, 2)
            chunk_rhs(1)
            level_z(1, 3)
            chunk_u(1)
            level_d(1, 3)
            chunk_out(1)
            level_z(1, 4)
            pe.wait_ge(S["s_sb"], 2)
            gram_products(1, 2)
            level_d(1, 4)
            gram_products(1, 3)
            level_z(1, 5)
            gram_products(1, 4)
            level_d(1, 5)
            pe.wait_ge(S["gram_sb"], 20)
            pe.wait_ge(S["xy"], 20)
            for c in (2, 3):
                chunk_rhs(c)
                chunk_u(c)
                chunk_out(c)
            pe.wait_ge(S["s_sb"], NCH)
            for q in range(QT):
                last = tr(psum[0:64, 0, q * P:(q + 1) * P], S0T[:, q, :])
            last.then_inc(S["wkv_tr"], 1)
            pe.wait_ge(S["samp_in"], 16)
            for q in range(QT):
                last = tr(psum[:, 1, q * NSA:(q + 1) * NSA], so_tok[:, q * P:(q + 1) * P])
            last.then_inc(S["samp_tr"], 1)
            pe.wait_ge(S["wkv_sb"], 1)
            pe.wait_ge(S["samp_sb"], 1)
            for q in range(QT):
                last = mm(psum[:, q, 0:T], blk, outT[:, q, :])
            last.then_inc(S["gn_mm"], 1)
            arrived(U_ABO)
            arrived(U_ABO + 1)
            def mixer_a_part(tiles):
                for m in tiles:
                    for q in range(QT):
                        mm(psum[:, 4 + m, 0:T], mix_view(U_ABO + q // 2)[:, q % 2, m::DT], y_a[:, q, :], q == 0, False)

            mixer_a_part((0, 1))
            pe.wait_ge(S["gn_c"], 1)
            for q in range(QT):
                last = mm(psum[:, q, 0:T], blk, tmp[:, q, :])
            last.then_inc(S["gn_mm"], 1)
            mixer_a_part((2, 3))

            def output_product(l, u0, rhs):
                for u in range(4):
                    arrived(u0 + u)

                def add(m, sources):
                    for q in sources:
                        if l == 1 and m == 0:
                            pe.wait_ge(S["sg_ready"], q + 1)
                        last = mm(psum[:, (m + 4) % 8, 0:T], mix_view(u0 + q // 2)[:, q % 2, m::DT], rhs[:, q, :], q == 0, q == 7)
                    return last

                if l == 0:
                    pe.wait_ge(S["yab_ready"], 1)
                    for m in range(4):
                        add(m, (4, 5))
                    pe.wait_ge(S["yab_ready"], 2)
                for m in range(DT):
                    add(m, (6, 7) if l == 0 and m < 4 else range(8)).then_inc(S["out_mm"], 1)

            def moe(l):
                pe.wait_ge(S["h_ready"], 2 * l + 2)
                pe.wait_ge(S["h_act"], 2 * l + 1)
                for t in range(3):
                    for c in range(DT):
                        last = mm(psum[0:TR, 0, t * NE:(t + 1) * NE], hT[:, c, t * TR:(t + 1) * TR], router[:, l, c, :], c == 0, c == DT - 1)
                last.then_inc(S["logit_mm"], 1)
                for n in range(6):
                    if n >= 2:
                        pe.wait_ge(S["htr_sb"], 6 * l + n - 1)
                    for c in range(4):
                        last = tr(psum[0:TR, 2 + n % 2, c * P:(c + 1) * P], hT[:, (n % 2) * 4 + c, (n // 2) * TR:(n // 2 + 1) * TR])
                    last.then_inc(S["htr_mm"], 1)
                u0 = U_SH[l]
                def shared_in(b, n):
                    arrived(n)
                    for j in range(2):
                        for c in range(DT):
                            last = mm(psum[:, b + j, 0:T], mix_view(n)[:, c, j::2], hT[:, c, :], c == 0, c == DT - 1)
                    last.then_inc(S["sh_mm"], 1)

                shared_in(4, u0)
                pe.wait_ge(S["mask_ready"], l + 1)
                earlier = K[0:TR, C_UPT:C_UPT + TR]
                for t in range(3):
                    for s in range(t + 1):
                        last = mm(psum[0:TR, 1, t * NE:(t + 1) * NE], earlier if s == t else ones[0:TR, 0:TR],
                                  mask[0:TR, s, :], s == 0, s == t)
                for s in range(3):
                    last = mm(psum[0:TR, 1, 3 * NE:4 * NE], ones[0:TR, 0:TR], mask[0:TR, s, :], s == 0, s == 2)
                last.then_inc(S["rank_mm"], 1)
                shared_in(6, u0 + 1)
                pe.wait_ge(S["round_set"], l + 1)
                first = pe.value_load(nrounds[0:1, 0:1], min_val=1, max_val=MAXR) if l else 0
                end = pe.value_load(nrounds[0:1, l:l + 1], min_val=1, max_val=(l + 1) * MAXR)

                def slots(r, j):
                    pe.wait_ge(S["sel"], r * SEL_R + (j + 1))
                    for t in range(3):
                        mm(psum[:, 4, 0:1], slotsel[0:TR, t].rearrange("p a s -> p (a s)"), K[0:TR, C_TOK + t:C_TOK + t + 1], t == 0, t == 2)
                    for t in range(3):
                        last = mm(psum[:, 4, 2:4], slotsel[0:TR, t].rearrange("p a s -> p (a s)"), comb[0:TR, t, 2 * j:2 * j + 2], t == 0, t == 2)
                    last.then_inc(S["slot_mm"], 1)

                pe.wait_ge(S["sh_act"], l + 1)
                slots(first, 0)
                pe.wait_ge(S["htr_sb"], 6 * l + 6)
                pe.wait_ge(S["sh_hid"], l + 1)
                arrived(u0 + 2)
                for m in range(DT):
                    if m >= 2:
                        pe.wait_ge(S["shd_sb"], 8 * l + m - 1)
                    for j in range(2):
                        last = mm(psum[:, 2 + m % 2, 0:T], mix_view(u0 + 2)[:, j, m::DT], shid[:, j, :], j == 0, j == 1)
                    last.then_inc(S["shd_mm"], 1)
                    if m == 2:
                        slots(first, 1)
                pe.wait_ge(S["shd_sb"], 8 * l + 8)
                with pe.Fori(first, end) as r:
                    pe.wait_ge(S["gat_a"], r * GAT_R + 16)
                    pe.wait_ge(S["ht_sb"], r * NPAIR + ONE)
                    for half in range(2):
                        if half:
                            pe.wait_ge(S["xt_sb"], r * XT_R + 1)
                        for c in range(4):
                            last = tr(psum[:, 5, c * P:(c + 1) * P], xg[0][:, half * 4 + c, :])
                        last.then_inc(S["xt_mm"], 1)
                    with pe.Fori(0, NTURN) as i:
                        for b in range(EBODY):
                            done1 = r * NPAIR + i * EBODY + (b + 1)
                            nb = (b + 1) % 2
                            pe.wait_ge(S["gat_" + "ab"[nb]], r * GAT_R + i * 32 + 16 * ((b + 1) // 2 + 1))
                            pe.wait_ge(S["ht_sb"], done1 - 1 + ONE)
                            pe.wait_ge(S["xt_sb"], r * XT_R + i * 8 + (2 * b + 2))
                            for c in range(4):
                                last = tr(psum[:, 5, c * P:(c + 1) * P], xg[nb][:, c, :])
                            last.then_inc(S["xt_mm"], 1)
                            s0 = eslot((b % 2) * PU)

                            def put_back(c):
                                if b or c >= 2:
                                    pe.wait_ge(S["cb_add"], r * CB_R + i * 32 + (8 * b + c) - 1 + ONE)
                                else:
                                    pe.wait_ge(S["cb_add"], r * CB_R + i * 32 + ONE)
                                mm(psum[:, 6 + c % 2, 0:T], gout[:, c::DT], selT[(b + 3) % 4]).then_inc(S["cb_mm"], 1)

                            def product(kind, bank, inp):
                                for e in range(2):
                                    pe.wait_ge(eload[s0 + 2 * kind + e], r * (RU // ESLOTS * 16) + i * 32 + 16 * (b // 2 + 1))
                                for c in range(DT):
                                    for e in range(2):
                                        x = mm(psum[64 * e:64 * e + 64, bank, 0:DE], inp[:, c, 64 * e:64 * e + 64],
                                               ring[:, s0 + 2 * kind + e, c * DE:(c + 1) * DE], c == 0, c == DT - 1)
                                        if c == DT - 1:
                                            x.then_inc(S["unit_used"], 1)
                                    if kind == 1 and c in (1, 3, 5):
                                        put_back(c // 2)

                            pe.wait_ge(S["gsil"], done1 - 1 + ONE)
                            product(0, 0, xgT[b % 2])
                            pe.wait_ge(S["sel"], r * SEL_R + i * EBODY + (b + 3))
                            for t in range(3):
                                mm(psum[:, 4, 0:1], slotsel[0:TR, t].rearrange("p a s -> p (a s)"), K[0:TR, C_TOK + t:C_TOK + t + 1], t == 0, t == 2)
                            for t in range(3):
                                last = mm(psum[:, 4, 2:4], slotsel[0:TR, t].rearrange("p a s -> p (a s)"),
                                          comb[0:TR, t, bass.ds(i * 8 + (2 * b + 4), 2)], t == 0, t == 2)
                            last.then_inc(S["slot_mm"], 1)
                            pe.wait_ge(S["xt_sb"], r * XT_R + i * 8 + (2 * b + 3))
                            for c in range(4):
                                last = tr(psum[:, 5, c * P:(c + 1) * P], xg[nb][:, 4 + c, :])
                            last.then_inc(S["xt_mm"], 1)
                            pe.wait_ge(S["ghid"], done1 - 1 + ONE)
                            pe.wait_ge(S["os_a"], done1 - 1 + ONE)
                            pe.wait_ge(S["os_b"], done1 - 1 + ONE)
                            product(1, 1, xgT[b % 2])
                            for c in (3, 4, 5):
                                put_back(c)
                            pe.wait_ge(S["ghid"], done1 + ONE)
                            pe.wait_ge(S["xt_sb"], r * XT_R + i * 8 + (2 * b + 4))
                            for j in range(2):
                                last = tr(psum[:, 5, j * P:(j + 1) * P], ghid[:, j::2])
                            last.then_inc(S["ht_mm"], 1)
                            for c in (6, 7):
                                put_back(c)
                            pe.wait_ge(S["ht_sb"], done1 + ONE)
                            for e in range(2):
                                pe.wait_ge(eload[s0 + 4 + e], r * (RU // ESLOTS * 16) + i * 32 + 16 * (b // 2 + 1))
                            for n in range(2):
                                for j in range(2):
                                    for e in range(2):
                                        x = mm(psum[64 * e:64 * e + 64, 2 + n, :], ghT[:, j, 64 * e:64 * e + 64],
                                               ring[:, s0 + 4 + e, j * D + n * 512:j * D + n * 512 + 512], j == 0, j == 1)
                                        if n == 1 and j == 1:
                                            x.then_inc(S["unit_used"], 1)
                    pe.wait_ge(S["gat_b"], (r + 1) * GAT_R)
                    pe.wait_ge(S["os_a"], (r + 1) * NPAIR + ONE)
                    pe.wait_ge(S["os_b"], (r + 1) * NPAIR + ONE)
                    for c in range(DT):
                        pe.wait_ge(S["cb_add"], r * CB_R + (DT * NPAIR + max(c - 1, 0)) + ONE)
                        mm(psum[:, 6 + c % 2, 0:T], gout[:, c::DT], selT[3]).then_inc(S["cb_mm"], 1)
                    with pe.If(r + 1 < end):
                        slots(r + 1, 0)
                        slots(r + 1, 1)

            output_product(0, U_ABO, hT)
            pe.wait_ge(S["out_sb"], 4)
            sum_squares(1)
            sum_squares(2)
            moe(0)
            sum_squares(3)
            sum_squares(4)

            pe.wait_ge(S["h_ready"], 3)
            pe.wait_ge(S["h_act"], 2)

            def beside_u(pos):
                if pos == 2:
                    pe.wait_ge(S["gmisc_in"], 32)
                    for g in range(8):
                        last = tr(psum[:, 4 + g // 4, (g % 4) * P:(g % 4 + 1) * P], wsn[:, g, :])
                    last.then_inc(S["ws_tr"], 1)
                elif pos == 8:
                    pe.wait_ge(S["z_sb1"], 8)
                    for g in range(8):
                        last = mm(psum[:, 6, 0:T], ones, z[:, 8 + g, :], g == 0, g == 7)
                    last.then_inc(S["vmu_mm"], 1)
                elif pos == 10:
                    for g in range(8):
                        pe.wait_ge(S["vc_ready"], g + 1)
                        last = mm(psum[:, 7, 0:T], ones, gt1[:, g, :], g == 0, g == 7)
                    last.then_inc(S["vvar_mm"], 1)
                elif pos == 13:
                    pe.wait_ge(S["v_ready"], 1)
                    pe.wait_ge(S["ws_sb"], 1)
                    for t in range(2):
                        for g in range(8):
                            last = tr(psum[:, 2 + 2 * t + g // 4, (g % 4) * P:(g % 4 + 1) * P], z[:, 8 + g, t * P:(t + 1) * P])
                        last.then_inc(S["vt_tr"], 1)
                    for g in range(8):
                        last = tr(psum[0:NSA, 6 + g // 4, (g % 4) * P:(g % 4 + 1) * P], z[:, 8 + g, NPR:T])
                    last.then_inc(S["vt_tr"], 1)
                elif pos == 14:
                    for t in range(2):
                        pe.wait_ge(S["vt_sb"], t + 1)
                        for g in range(8):
                            last = mm(psum[:, 2 + 2 * t + g // 4, (g % 4) * P:(g % 4 + 1) * P], vtok[:, t, g * P:(g + 1) * P], wsT[:, g, :])
                        last.then_inc(S["sg_mm"], 1)

            for pos in range(16):
                n = U_GMI + pos // 2
                if pos % 2 == 0:
                    arrived(n)
                if pos >= 2:
                    pe.wait_ge(S["z_sb1"], pos - 1)
                for c in range(DT):
                    last = mm(psum[:, pos % 2, 0:T], mix_view(n)[:, c, (pos % 2) * P:(pos % 2 + 1) * P], hT[:, c, :], c == 0, c == DT - 1)
                last.then_inc(S["z_mm1"], 1)
                beside_u(pos)
            pe.wait_ge(S["vs_sb"], 1)
            output_product(1, U_GMO, z)
            pe.wait_ge(S["out_sb"], 12)
            sum_squares(5)
            sum_squares(6)
            moe(1)
            sum_squares(7)
            for n in range(6):
                half, t = n // 3, n % 3
                pe.wait_ge(S["y_done"], 3 * DT + 4 * (half + 1))
                if n >= 2:
                    pe.wait_ge(S["fin_sb"], n - 1)
                for c in range(4):
                    last = tr(psum[0:TR, n % 2, c * P:(c + 1) * P], xT[:, half * 4 + c, t * TR:(t + 1) * TR])
                last.then_inc(S["fin_tr"], 1)

        @block.scalar
        def _(act):
            def f(out, in_, func, **kw):
                return nc.scalar.activation(out, in_, func, **kw)

            def root(k):
                act.wait_ge(S["ss_mm"], k + 1)
                f(rstd[:, :], psum[:, 7, 0:T], ACT.Sqrt, bias=eps[:, 0:1]).then_inc(S["sd_ready"], 1)

            def pre(k):
                for c in range(DT):
                    act.wait_ge(S["y_done"], DT * (k // 2 - 1) + c + 1)
                    f(hT[:, c, :], xT[:, c, :], ACT.Square, scale=D ** -0.5).then_inc(S["sq_act"], 1)
                root(k)
                sh, sc = mod[:, k // 4, 3 * (k // 2 % 2)], mod[:, k // 4, 3 * (k // 2 % 2) + 1]
                act.wait_ge(S["norm_half"], k // 2)
                for c in range(4):
                    last = f(hT[:, c, 0:NPR], hT[:, c, 0:NPR], ACT.Identity, bias=sh[:, c, 0:1], scale=sc[:, c, 0:1])
                last.then_inc(S["h_act"], 1)

            act.wait_ge(S["c_in"], 32)
            f(ctok2[0:NSEQ, :], ctok[0:NSEQ, :], ACT.Silu).then_inc(S["silu_c"], 1)

            def mod_rows(k):
                act.wait_ge(S["mod_mm"], 2 * (k + 1))
                if k >= 2:
                    act.wait_ge(S["mod_tr"], k // 2)
                f(mrow[:, k % 2 * 512:(k % 2 + 1) * 512], psum[:, 6, :], ACT.Copy).then_inc(S["mod_row"], 1)

            mod_rows(0)
            mod_rows(1)
            root(0)
            mod_rows(2)
            mod_rows(3)
            def beside_projection(pos):
                if pos == 15:
                    act.wait_ge(S["small_in"], 16 * NSMALL)
                    act.wait_ge(S["mixed"], 1)
                    f(xm[0:64, 12, :], xm[0:64, 12, :], ACT.Tanh).then_inc(S["lora_in"], 1)
                    f(xm[:, 13, :], xm[:, 13, :], ACT.Sigmoid).then_inc(S["lora_in"], 1)
                elif pos == 16:
                    act.wait_ge(S["lora_mm"], 1)
                    for q in range(QT):
                        last = f(ld[:, q, :], psum[:, 2 + q, 0:T], ACT.Sigmoid, bias=w0[:, q:q + 1])
                    last.then_inc(S["lora_sb"], 1)
                elif pos == 17:
                    act.wait_ge(S["lora_mm"], 2)
                    for q in range(QT):
                        last = f(a_sig[:, q, :], psum[:, 2 + q, 0:T], ACT.Sigmoid, bias=a0[:, q:q + 1])
                    last.then_inc(S["lora_sb"], 1)
                elif pos == 18:
                    act.wait_ge(S["lora_mm"], 3)
                    f(g_t, psum[:, 2:6, 0:T], ACT.Copy).then_inc(S["lora_sb"], 1)
                elif pos == 20:
                    act.wait_ge(S["kkss_mm"], 1)
                    f(tmp, psum[:, 2:6, 0:T], ACT.Sqrt).then_inc(S["kknorm"], 1)
                elif pos == 21:
                    act.wait_ge(S["cs_ready"], 1)
                    f(px, px, ACT.Exp).then_inc(S["exp_step"], 1)
                    f(ld, cs, ACT.Exp, scale=-1.0).then_inc(S["exp_step"], 1)
                    act.wait_ge(S["exp_step"], 2)
                    f(cs, cs, ACT.Exp).then_inc(S["exp_ready"], 1)

            for pos in range(PROJT):
                m = PROJ_TILE[pos]
                if m == 0:
                    act.wait_ge(S["st_sb"], 2)
                    act.wait_ge(S["conv_out"], 16)
                act.wait_ge(S["proj_mm"], pos + 1)
                f(conv_in[:, m, :] if m < 12 else proj[:, m, :], psum[:, pos % 2, 0:T], ACT.Copy).then_inc(S["proj_sb"], 1)
                if pos % 2:
                    for k in MOD_PROJ[pos // 2]:
                        mod_rows(k)
                beside_projection(pos)
            act.wait_ge(S["svec_tr"], 1)
            for v, n, buf in svec_tok:
                last = f(buf, psum[0:NSA, v:v + n, :], ACT.Copy)
            last.then_inc(S["svec_sb"], 1)
            mod_rows(17)
            act.wait_ge(S["shift_out"], 32)
            act.wait_ge(S["tok_tr"], 1)
            for t in range(2):
                f(Btok[:, t, :], psum[:, 3 * t + 1, :], ACT.Copy)
                last = f(Ktok[:, t, :], psum[:, 3 * t + 2, :], ACT.Copy)
            last.then_inc(S["tok_sb"], 1)
            for k in range(18, 24):
                mod_rows(k)
            act.wait_ge(S["wkv_tr"], 1)
            f(wkv_o[0:64], psum[0:64, 0, :].rearrange("p (h j) -> p h j", h=H), ACT.Copy).then_inc(S["wkv_sb"], 1)
            act.wait_ge(S["gn_mm"], 2)
            f(tmp, psum[:, 0:4, 0:T], ACT.Sqrt, bias=eps[:, 1:2]).then_inc(S["gn_sd"], 1)

            def outputs(l, y):
                for m in range(DT):
                    act.wait_ge(S["out_mm"], 8 * l + m + 1)
                    f(y[:, m, :], psum[:, (m + 4) % 8, 0:T], ACT.Copy).then_inc(S["out_sb"], 1)

            def moe(l):
                act.wait_ge(S["logit_mm"], l + 1)
                if l == 0:
                    act.wait_ge(S["rwkv_free"], 1)
                else:
                    act.wait_ge(S["vs_stored"], 1)
                act.wait_ge(S["y_done"], DT * (2 * l + 1))
                f(score[0:TR], psum[0:TR, 0, 0:3 * NE].rearrange("p (t e) -> p t e", t=3), ACT.Sigmoid).then_inc(S["score_ready"], 1)
                for n in range(6):
                    act.wait_ge(S["htr_mm"], 6 * l + n + 1)
                    f(htok[0:TR, n // 2, (n % 2) * 512:(n % 2 + 1) * 512], psum[0:TR, 2 + n % 2, :], ACT.Copy).then_inc(S["htr_sb"], 1)
                act.wait_ge(S["sh_mm"], 2 * l + 1)
                f(ssil, psum[:, 4:6, 0:T], ACT.Silu).then_inc(S["sh_act"], 1)
                for m in range(DT):
                    act.wait_ge(S["shd_mm"], 8 * l + m + 1)
                    f(yacc[:, m, :], psum[:, 2 + m % 2, 0:T], ACT.Copy).then_inc(S["shd_sb"], 1)
                act.wait_ge(S["round_set"], l + 1)
                first = act.value_load(nrounds[0:1, 0:1], min_val=1, max_val=MAXR) if l else 0
                end = act.value_load(nrounds[0:1, l:l + 1], min_val=1, max_val=(l + 1) * MAXR)
                with act.Fori(first, end) as r:
                    for half in range(2):
                        act.wait_ge(S["xt_mm"], r * XT_R + (half + 1))
                        if half == 0:
                            act.wait_ge(S["unit_used"], r * RU + ONE)
                        f(xgT[0][:, half * 4:half * 4 + 4, :], psum[:, 5, :].rearrange("p (c s) -> p c s", c=4), ACT.Copy).then_inc(S["xt_sb"], 1)
                    with act.Fori(0, NTURN) as i:
                        for b in range(EBODY):
                            done1 = r * NPAIR + i * EBODY + (b + 1)
                            used0 = r * RU + i * (EBODY * PU) + b * PU
                            nb = (b + 1) % 2
                            for half in range(2):
                                act.wait_ge(S["xt_mm"], r * XT_R + i * 8 + (2 * b + 3 + half))
                                if half == 0:
                                    act.wait_ge(S["unit_used"], used0 + ONE)
                                f(xgT[nb][:, half * 4:half * 4 + 4, :], psum[:, 5, :].rearrange("p (c s) -> p c s", c=4), ACT.Copy).then_inc(S["xt_sb"], 1)
                                if half == 0:
                                    act.wait_ge(S["unit_used"], used0 + 2 + ONE)
                                    act.wait_ge(S["ghid"], done1 - 1 + ONE)
                                    f(gsil, psum[:, 0, 0:DE], ACT.Silu).then_inc(S["gsil"], 1)
                            act.wait_ge(S["ht_mm"], done1 + ONE)
                            act.wait_ge(S["unit_used"], used0 + ONE)
                            f(ghT, psum[:, 5, 0:2 * P].rearrange("p (j s) -> p j s", j=2), ACT.Copy).then_inc(S["ht_sb"], 1)
                            act.wait_ge(S["unit_used"], used0 + 6 + ONE)
                            f(gout[:, 0:512], psum[:, 2, :], ACT.Copy).then_inc(S["os_a"], 1)

            outputs(0, yacc)
            root(1)
            pre(2)
            moe(0)
            root(3)
            pre(4)
            for pos in range(16):
                m = (pos + 8) % 16
                act.wait_ge(S["z_mm1"], pos + 1)
                if pos == 0:
                    act.wait_ge(S["y_done"], 2 * DT)
                f(z[:, m, :], psum[:, pos % 2, 0:T], ACT.Gelu_apprx_tanh, bias=gb_in[:, m:m + 1]).then_inc(S["z_sb1"], 1)
                if pos == 10:
                    act.wait_ge(S["vvar_mm"], 1)
                    f(rstd[:, :], psum[:, 7, 0:T], ACT.Sqrt, bias=eps[:, 0:1]).then_inc(S["ln_sd"], 1)
                elif pos == 13:
                    for t in range(2):
                        act.wait_ge(S["vt_tr"], t + 1)
                        f(vtok[:, t, :].rearrange("p (a n) -> p a n", a=2), psum[:, 2 + 2 * t:4 + 2 * t, :], ACT.Copy).then_inc(S["vt_sb"], 1)
                    act.wait_ge(S["vt_tr"], 3)
                    f(vs_out[0:NSA, :].rearrange("p (a n) -> p a n", a=2), psum[0:NSA, 6:8, :], ACT.Copy).then_inc(S["vs_sb"], 1)
            outputs(1, gt1)
            root(5)
            pre(6)
            moe(1)
            root(7)
            for n in range(6):
                act.wait_ge(S["fin_tr"], n + 1)
                half, t = n // 3, n % 3
                out = xo[0:TR, t, :].rearrange("p (d c) -> p c d", c=DT)[:, half * 4:half * 4 + 4, :]
                f(out, psum[0:TR, n % 2, :].rearrange("p (c d) -> p c d", c=4), ACT.Copy).then_inc(S["fin_sb"], 1)

        @block.vector
        def _(dve):
            V = nc.vector
            done = [0]

            def v(i):
                done[0] += 1
                i.then_inc(S["vec"], 1)
                dve.wait_ge(S["vec"], done[0])

            def over(col, n):
                return col.unsqueeze(len(col.shape)).broadcast_to([*col.shape, n])

            def inverse_root(k):
                dve.wait_ge(S["ss_mm"], k + 1)
                dve.wait_ge(S["sd_ready"], k + 1)
                v(V.reciprocal(rstd[:, :], rstd[:, :]))

            def rms(k, src, tile_ready=None):
                for c in range(DT):
                    if tile_ready:
                        dve.wait_ge(S[tile_ready[0]], tile_ready[1] + c + 1)
                    V.scalar_tensor_tensor(squares(k)[:, c, :], src[:, c, :], 1.0 / D, src[:, c, :], ALU.mult, ALU.mult).then_inc(S["sq_ready"], 1)
                inverse_root(k)

            wide = lambda n=DT: rstd[:, :].unsqueeze(1).broadcast_to([P, n, T])

            def shift_samples(l, half):
                sh, sc = mod[:, l, 3 * half], mod[:, l, 3 * half + 1]
                v(V.tensor_tensor(hT[:, :, NPR:T], hT[:, :, NPR:T], sc[:, :, 1:NSEQ], ALU.mult))
                V.tensor_tensor(hT[:, :, NPR:T], hT[:, :, NPR:T], sh[:, :, 1:NSEQ], ALU.add)

            def shift_prompt(l, half, tiles):
                sh, sc = mod[:, l, 3 * half], mod[:, l, 3 * half + 1]
                for c in tiles:
                    last = V.tensor_scalar(hT[:, c, 0:NPR], hT[:, c, 0:NPR], sc[:, c, 0:1], sh[:, c, 0:1], ALU.mult, ALU.add)
                last.then_inc(S["h_ready"], 1)

            def pre(k, l, half):
                inverse_root(k)
                V.tensor_tensor(hT[:, 0:4, :], xT[:, 0:4, :], wide(4), ALU.mult).then_inc(S["norm_half"], 1)
                v(V.tensor_tensor(hT[:, 4:8, :], xT[:, 4:8, :], wide(4), ALU.mult))
                dve.wait_ge(S["norm_half"], k // 2)
                shift_samples(l, half)
                shift_prompt(l, half, range(4, DT))

            def post(k, l, half, y, tile_ready=None):
                rms(k, y, tile_ready)
                v(V.tensor_tensor(y, y, wide(), ALU.mult))
                g = mod[:, l, 3 * half + 2]
                v(V.tensor_tensor(y[:, :, NPR:T], y[:, :, NPR:T], g[:, :, 1:NSEQ], ALU.mult))
                V.tensor_tensor(xT[:, :, NPR:T], xT[:, :, NPR:T], y[:, :, NPR:T], ALU.add)
                for c in range(DT):
                    V.scalar_tensor_tensor(xT[:, c, 0:NPR], y[:, c, 0:NPR], g[:, c, 0:1], xT[:, c, 0:NPR], ALU.mult, ALU.add).then_inc(S["y_done"], 1)
                dve.wait_ge(S["y_done"], DT * (2 * l + half + 1))

            V.memset(eps[:, 0:1], EPS)
            V.memset(eps[:, 1:2], GN_EPS)
            v(V.memset(cT[:, :, :], 0.0))
            dve.wait_ge(S["c_tr"], 1)
            V.tensor_copy(cT[:, :, 0:NSEQ], psum[:, 5, 0:DT * NSEQ].rearrange("p (c s) -> p c s", c=DT)).then_inc(S["c_sb"], 1)
            for t in range(2):
                dve.wait_ge(S["x_tr"], t + 1)
                V.tensor_copy(xT[:, :, t * P:(t + 1) * P].rearrange("p (a c) n -> p a c n", a=2),
                              psum[:, 2 * t:2 * t + 2, :].rearrange("p a (c n) -> p a c n", c=4)).then_inc(S["x_sb"], 1)
            dve.wait_ge(S["x_tr"], 3)
            V.tensor_copy(xT[:, :, NPR:T], psum[:, 4, 0:DT * NSA].rearrange("p (c s) -> p c s", c=DT)).then_inc(S["x_sb"], 1)
            dve.wait_ge(S["x_sb"], 3)
            rms(0, xT[:, :, :])
            v(V.tensor_tensor(hT[:, :, :], xT[:, :, :], wide(), ALU.mult))

            def mod_part(g):
                l, part = g // 6, g % 6
                dve.wait_ge(S["mod_tr"], g + 1)
                m = mod[:, l, part]
                V.tensor_tensor(m, psum[:, 7, 0:DT * NSEQ].rearrange("p (c s) -> p c s", c=DT),
                                over(b_modT[:, l, part], NSEQ), ALU.add).then_inc(S["mod_set"], 1)
                dve.wait_ge(S["mod_set"], g + 1)
                if part in (1, 4):
                    v(V.tensor_scalar(m, m, 1.0, None, ALU.add))
                    v(V.tensor_tensor(m, m, over(ngT[:, l, part // 3 * 2], NSEQ), ALU.mult))
                if part in (2, 5):
                    v(V.tensor_tensor(m, m, over(ngT[:, l, part // 3 * 2 + 1], NSEQ), ALU.mult))

            dve.wait_ge(S["modp_in"], 32)
            mod_part(0)
            mod_part(1)
            shift_samples(0, 0)
            shift_prompt(0, 0, range(DT))
            mod_part(2)
            dve.wait_ge(S["st_tr"], 1)
            V.tensor_copy(st_shift, psum[:, 4, 0:PBT * NSA].rearrange("p (q s) -> p q s", q=PBT)).then_inc(S["st_sb"], 1)
            V.tensor_copy(st_conv, psum[:, 4, PBT * NSA:PBT * NSA + 64].rearrange("p (w q s) -> p w q s", w=2, q=QT)).then_inc(S["st_sb"], 1)
            mod_part(3)
            dve.wait_ge(S["st_sb"], 2)
            dve.wait_ge(S["const2_in"], 32)
            dve.wait_ge(S["small_in"], 16 * NSMALL)
            dve.wait_ge(S["proj_sb"], PBT)
            V.tensor_tensor(xm[:, :, 1:NPR], pb[:, :, 0:NPR - 1], pb[:, :, 1:NPR], ALU.subtract)
            V.tensor_scalar(xm[:, :, 0:1], pb[:, :, 0:1], -1.0, None, ALU.mult)
            v(V.tensor_tensor(xm[:, :, NPR:T], st_shift, pb[:, :, NPR:T], ALU.subtract))
            for q in reversed(range(PBT)):
                last = V.scalar_tensor_tensor(xm[:, q, :], xm[:, q, :], mu[:, q:q + 1], pb[:, q, :], ALU.mult, ALU.add)
            last.then_inc(S["mixed"], 1)
            dve.wait_ge(S["mixed"], 1)
            dve.wait_ge(S["tail_tr"], 1)
            V.tensor_copy(sh_out, psum[0:NSEQ, 2:6, :].rearrange("p a b -> p (a b)")[:, 0:PB]).then_inc(S["tail_sb"], 1)
            V.memset(Uz, 0.0)
            V.memset(rhs_s, 0.0)
            mod_part(4)

            dve.wait_ge(S["lora_sb"], 1)
            v(V.tensor_scalar(ld, ld, -EMH, None, ALU.mult))
            for q in range(QT):
                for c in range(NCH):
                    s = slice(c * CH, (c + 1) * CH)
                    V.tensor_tensor_scan(cs[:, q, s], ones[:, 0:CH], ld[:, q, s], 0.0, ALU.mult, ALU.add)
            v(V.tensor_copy(cs[:, :, NPR:T], ld[:, :, NPR:T]))
            V.tensor_tensor(px, cs, ld, ALU.subtract).then_inc(S["cs_ready"], 1)
            mod_part(5)
            v(V.tensor_tensor(kk, k_, over(k_k, T), ALU.mult))
            V.tensor_tensor(tmp, kk, kk, ALU.mult).then_inc(S["kksq_ready"], 1)
            dve.wait_ge(S["lora_sb"], 2)
            v(V.tensor_scalar(kh, a_sig, -1.0, None, ALU.add))
            v(V.tensor_tensor(kh, kh, over(k_a, T), ALU.mult))
            v(V.scalar_tensor_tensor(kh, kh, 1.0, k_, ALU.add, ALU.mult))
            v(V.tensor_tensor(bonus, r_, over(r_k, T), ALU.mult))
            V.tensor_tensor(bonus, bonus, kh, ALU.mult).then_inc(S["rk_ready"], 1)
            mod_part(6)
            dve.wait_ge(S["kknorm"], 1)
            v(V.tensor_scalar(tmp, tmp, 1e-12, None, ALU.max))
            v(V.reciprocal(tmp, tmp))
            v(V.tensor_tensor(kk, kk, tmp, ALU.mult))
            v(V.tensor_tensor(bb, kk, a_sig, ALU.mult))
            dve.wait_ge(S["rk_mm"], 1)
            V.tensor_tensor(bonus, psum[:, 2:6, 0:T], v_, ALU.mult).then_inc(S["pad_ready"], 1)
            dve.wait_ge(S["pad_ready"], 1)
            dve.wait_ge(S["proj_sb"], PROJT - 4)
            gated = conv_in[:, 8:12, :]
            V.tensor_tensor(gated, gated, conv_in[:, 0:4, :], ALU.mult).then_inc(S["tail_ready"], 1)
            dve.wait_ge(S["tail_ready"], 1)
            for q in range(QT):
                y, gq = conv_t[:, q, :], gated[:, q, :]
                wq = [conv_w[:, w, q:q + 1] for w in range(3)]
                v(V.tensor_scalar(y, gq, wq[2], None, ALU.mult))
                v(V.scalar_tensor_tensor(y[:, 1:NPR], gq[:, 0:NPR - 1], wq[1], y[:, 1:NPR], ALU.mult, ALU.add))
                v(V.scalar_tensor_tensor(y[:, 2:NPR], gq[:, 0:NPR - 2], wq[0], y[:, 2:NPR], ALU.mult, ALU.add))
                v(V.scalar_tensor_tensor(y[:, NPR:T], st_conv[:, 1, q], wq[1], y[:, NPR:T], ALU.mult, ALU.add))
                v(V.scalar_tensor_tensor(y[:, NPR:T], st_conv[:, 0, q], wq[0], y[:, NPR:T], ALU.mult, ALU.add))
            dve.wait_ge(S["proj_sb"], PROJT)
            V.tensor_tensor(y_a, conv_t, conv_in[:, 4:8, :], ALU.mult).then_inc(S["conv_done"], 1)
            dve.wait_ge(S["conv_done"], 1)
            mod_part(7)
            dve.wait_ge(S["exp_ready"], 1)
            pr = slice(0, NPR)
            dve.wait_ge(S["svec_tr"], 1)
            V.tensor_tensor(bb[:, :, pr], bb[:, :, pr], ld[:, :, pr], ALU.mult)
            V.tensor_tensor(kh[:, :, pr], kh[:, :, pr], ld[:, :, pr], ALU.mult).then_inc(S["pad_ready"], 1)
            dve.wait_ge(S["tail_tr"], 2)
            V.tensor_copy(cv_out, psum[0:10, 7, :]).then_inc(S["tail_sb"], 1)
            for o in range(2):
                own = slice(64 * o, 64 * o + 64)
                V.tensor_tensor(Az[own, o::2, :], px[own, :, pr], kk[own, :, pr], ALU.mult)
                V.tensor_tensor(Rz[own, o::2, :], cs[own, :, pr], r_[own, :, pr], ALU.mult)
            for c in range(NCH):
                last = V.tensor_copy(PC[:, c, :], cs[:, :, c * CH + CH - 1])
            last.then_inc(S["ops_ready"], 1)
            dve.wait_ge(S["ops_ready"], 1)
            dve.wait_ge(S["shift_out"], 32)
            dve.wait_ge(S["tok_tr"], 1)
            for t in range(2):
                V.tensor_copy(Vz[0:64, 0, t, :], psum[0:64, 3 * t, :])
                last = V.tensor_copy(Vz[64:128, 1, t, :], psum[64:128, 3 * t, :])
            last.then_inc(S["tok_sb"], 1)
            mod_part(8)

            def wide4(col):
                return K[:, col:col + P].unsqueeze(1).broadcast_to([P, 4, P])

            quad = lambda b: psum[:, b, :].rearrange("p (h t) -> p h t", h=4)
            gram = ((L1, C_LOS), None, (L2T, C_UPS), (R1T, C_UPI), (R2T, C_UPI))

            def gram_masks(t, m):
                dst, mask_ = gram[m]
                for hh in range(2):
                    g = t * 10 + m * 2 + hh
                    dve.wait_ge(S["gram_mm"], g + 1)
                    V.tensor_tensor(dst[:, 4 * hh:4 * hh + 4, :], quad(gram_bank(g)), wide4(mask_), ALU.mult).then_inc(S["gram_sb"], 1)

            def start_inverse(t):
                for hh in range(2):
                    hs = slice(4 * hh, 4 * hh + 4)
                    g = t * 10 + 2 + hh
                    dve.wait_ge(S["gram_mm"], g + 1)
                    V.tensor_tensor(Y[t][:, hs], quad(gram_bank(g)), wide4(C_LV), ALU.mult).then_inc(S["gram_sb"], 1)
                wide8 = lambda col: K[:, col:col + P].unsqueeze(1).broadcast_to([P, H, P])
                dve.wait_ge(S["gram_sb"], t * 10 + 4)
                v(V.tensor_tensor(X, L1, wide8(C_LV0T), ALU.mult))
                V.tensor_tensor(X, wide8(C_ID), X, ALU.subtract)
                for hh in range(2):
                    hs = slice(4 * hh, 4 * hh + 4)
                    V.tensor_tensor(Y[t][:, hs], wide4(C_ID), Y[t][:, hs], ALU.subtract).then_inc(S["xy0"], 1)
                dve.wait_ge(S["xy0"], 2 * t + 2)

            def level_z(t, k):
                for hh in range(2):
                    hs = slice(4 * hh, 4 * hh + 4)
                    dve.wait_ge(S["z_mm"], t * 10 + (k - 1) * 2 + hh + 1)
                    V.tensor_tensor(Z[:, hs], quad(2 * hh), wide4(C_LV + k * P), ALU.mult).then_inc(S["z_sb"], 1)

            def level_xy(t, k):
                for hh in range(2):
                    hs = slice(4 * hh, 4 * hh + 4)
                    n = t * 10 + (k - 1) * 2 + hh
                    dve.wait_ge(S["d_mm"], n + 1)
                    last = V.tensor_tensor(Y[t][:, hs], Y[t][:, hs], quad(2 * hh), ALU.subtract)
                    if k < 5:
                        last = V.tensor_tensor(X[:, hs], X[:, hs], quad(2 * hh + 1), ALU.subtract)
                    last.then_inc(S["xy"], 1)
                    dve.wait_ge(S["xy"], n + 1)

            def chunk_rhs(c):
                ps = slice(64 * (c % 2), 64 * (c % 2) + 64)
                dve.wait_ge(S["rhs_mm"], c + 1)
                V.tensor_copy(rhs_s[ps, :], psum[ps, 6, :]).then_inc(S["rhs_sb"], 1)

            def chunk_u(c):
                ps = slice(64 * (c % 2), 64 * (c % 2) + 64)
                dve.wait_ge(S["u_mm"], c + 1)
                V.tensor_scalar(Uz[ps, c % 2, :], psum[ps, 7, :], -1.0, None, ALU.mult).then_inc(S["u_sb"], 1)

            def chunk_out(c):
                dve.wait_ge(S["o_mm"], c + 1)
                V.tensor_copy(outT[:, :, c * CH:(c + 1) * CH], psum[:, 4, 0:256].rearrange("p (q t) -> p q t", q=QT)).then_inc(S["o_sb"], 1)
                dve.wait_ge(S["s_mm"], c + 1)
                s_ps = psum[:, 5, 0:256].rearrange("p (q i) -> p q i", q=QT)
                if c == 0:
                    v(V.tensor_copy(S0T, s_ps))
                else:
                    v(V.tensor_tensor(S0T, S0T, s_ps, ALU.add))
                V.tensor_tensor(S0T, S0T, over(PC[:, c, :], HD), ALU.mult).then_inc(S["s_sb"], 1)
                dve.wait_ge(S["s_sb"], c + 1)

            dve.wait_ge(S["svec_out"], 64)
            gram_masks(0, 0)
            start_inverse(0)
            mod_part(9)
            for k in range(1, 6):
                level_z(0, k)
                if k <= 3:
                    gram_masks(0, k + 1)
                level_xy(0, k)
                if k == 4:
                    mod_part(10)
            gram_masks(1, 0)
            start_inverse(1)
            mod_part(11)
            level_z(1, 1)
            chunk_rhs(0)
            level_xy(1, 1)
            chunk_u(0)
            level_z(1, 2)
            chunk_out(0)
            level_xy(1, 2)
            chunk_rhs(1)
            level_z(1, 3)
            chunk_u(1)
            level_xy(1, 3)
            chunk_out(1)
            level_z(1, 4)
            gram_masks(1, 2)
            level_xy(1, 4)
            gram_masks(1, 3)
            level_z(1, 5)
            gram_masks(1, 4)
            level_xy(1, 5)
            for c in (2, 3):
                chunk_rhs(c)
                chunk_u(c)
                if c == 2:
                    for q in range(QT):
                        last = V.scalar_tensor_tensor(bonus[:, q], bonus[:, q], gn_b[:, q:q + 1], g_t[:, q], ALU.add, ALU.mult)
                    v(last)
                    v(V.tensor_tensor(g_t, g_t, over(gn_g, T), ALU.mult))
                chunk_out(c)
            dve.wait_ge(S["samp_tr"], 1)
            V.tensor_copy(outT[:, :, NPR:T], psum[:, 1, 0:QT * NSA].rearrange("p (q s) -> p q s", q=QT)).then_inc(S["samp_sb"], 1)
            dve.wait_ge(S["samp_sb"], 1)
            dve.wait_ge(S["o_sb"], NCH)
            dve.wait_ge(S["gn_mm"], 1)
            v(V.scalar_tensor_tensor(outT, psum[:, 0:4, 0:T], -1.0 / HD, outT, ALU.mult, ALU.add))
            V.scalar_tensor_tensor(tmp, outT, 1.0 / HD, outT, ALU.mult, ALU.mult).then_inc(S["gn_c"], 1)
            v(V.tensor_tensor(outT, outT, g_t, ALU.mult))
            dve.wait_ge(S["gn_mm"], 2)
            dve.wait_ge(S["gn_sd"], 1)
            for q in (slice(0, 2), slice(2, 4)):
                v(V.reciprocal(tmp[:, q], tmp[:, q]))
                v(V.tensor_tensor(outT[:, q], outT[:, q], tmp[:, q], ALU.mult))
                V.tensor_tensor(outT[:, q], outT[:, q], bonus[:, q], ALU.add).then_inc(S["yab_ready"], 1)

            def moe(l):
                if l == 0:
                    dve.wait_ge(S["rwkv_free"], 1)
                g3 = lambda a: a[0:TR]
                dve.wait_ge(S["score_ready"], l + 1)
                v(V.tensor_tensor(g3(sel), g3(score), brout[:, l].unsqueeze(1).broadcast_to([TR, 3, NE]), ALU.add))
                for t in range(3):
                    for g in range(NG):
                        last = V.max(out=gt8[0:TR, t, g, :], in_=sel[0:TR, t, g * 8:(g + 1) * 8])
                v(last)
                v(V.tensor_tensor(g3(grp), gt8[0:TR, :, :, 0], gt8[0:TR, :, :, 1], ALU.add))
                for t in range(3):
                    a = grp[0:TR, t].unsqueeze(1).broadcast_to([TR, NG, NG])
                    b = grp[0:TR, t].unsqueeze(2).broadcast_to([TR, NG, NG])
                    c1, c2 = (c[0:TR, t].rearrange("p (g h) -> p g h", g=NG) for c in (cmp1, cmp2))
                    V.tensor_tensor(c1, a, b, ALU.is_gt)
                    v(V.tensor_tensor(c2, a, b, ALU.is_equal))
                v(V.tensor_tensor(g3(cmp2), g3(cmp2), K[0:TR, C_TRI:C_TRI + 64].unsqueeze(1).broadcast_to([TR, 3, 64]), ALU.mult))
                v(V.tensor_tensor(g3(cmp1), g3(cmp1), g3(cmp2), ALU.add))
                v(V.tensor_reduce(g3(rank), g3(cmp1).rearrange("p t (g h) -> p t g h", g=NG), AX.X, ALU.add))
                v(V.tensor_scalar(g3(gm), g3(rank), float(TOPG), None, ALU.is_lt))
                eg = lambda a: a[0:TR].rearrange("p t (g e) -> p t g e", g=NG)
                v(V.tensor_tensor(eg(selm), eg(sel), over(g3(gm), 8), ALU.mult))
                v(V.tensor_scalar(g3(gm), g3(gm), -1.0, BIG, ALU.add, ALU.mult))
                v(V.tensor_tensor(eg(selm), eg(selm), over(g3(gm), 8), ALU.add))
                for t in range(3):
                    v(V.max(out=top8[0:TR, t, :], in_=selm[0:TR, t, :]))
                    v(V.match_replace(out=rep[0:TR, t, :], in_to_replace=top8[0:TR, t, :], in_values=selm[0:TR, t, :], imm_value=-2 * BIG))
                V.tensor_tensor(g3(mask), g3(rep), g3(selm), ALU.is_lt).then_inc(S["mask_ready"], 1)
                dve.wait_ge(S["mask_ready"], l + 1)
                v(V.tensor_tensor(g3(score), g3(score), g3(mask), ALU.mult))
                v(V.tensor_reduce(csum[0:TR], g3(score), AX.X, ALU.add))
                v(V.reciprocal(csum[0:TR], csum[0:TR]))
                v(V.tensor_scalar(csum[0:TR], csum[0:TR], ROUTE_SCALE, None, ALU.mult))
                V.memset(comb[0:TR, :, NE:NE + 4], 0.0)
                V.memset(posm[0:TR, :, NE:NE + 4], -1.0)
                v(V.tensor_tensor(comb[0:TR, :, 0:NE], g3(score), over(csum[0:TR], NE), ALU.mult))
                dve.wait_ge(S["rank_mm"], l + 1)
                pm = posm[0:TR, :, 0:NE]
                v(V.scalar_tensor_tensor(pm, psum[0:TR, 1, 0:3 * NE].rearrange("p (t e) -> p t e", t=3), 1.0, g3(mask), ALU.add, ALU.mult))
                v(V.tensor_scalar(pm, pm, -1.0, None, ALU.add))
                v(V.tensor_reduce(cmax[0:TR], psum[0:TR, 1, 3 * NE:4 * NE], AX.X, ALU.max))
                for n in range(1, MAXR):
                    v(V.tensor_scalar(cthr[0:TR, n - 1:n], cmax[0:TR], float(CAP * n), None, ALU.is_gt))
                v(V.tensor_reduce(cmax[0:TR], cthr[0:TR, 0:MAXR - 1], AX.X, ALU.add))
                v(V.tensor_scalar(rounds[0:TR, l:l + 1], cmax[0:TR], 1.0, None, ALU.add))
                if l:
                    v(V.tensor_tensor(rounds[0:TR, 1:2], rounds[0:TR, 0:1], rounds[0:TR, 1:2], ALU.add))
                V.memset(gout, 0.0)
                V.memset(selT[3], 0.0)
                V.tensor_copy(nrounds[0:TR, l:l + 1], rounds[0:TR, l:l + 1]).then_inc(S["round_set"], 1)
                dve.wait_ge(S["round_set"], l + 1)
                first = dve.value_load(nrounds[0:1, 0:1], min_val=1, max_val=MAXR) if l else 0
                end = dve.value_load(nrounds[0:1, l:l + 1], min_val=1, max_val=(l + 1) * MAXR)

                def choose(j2):
                    iota = K[0:TR, C_IOTA:C_IOTA + CAP].unsqueeze(1).broadcast_to([TR, 2, CAP])
                    for t in range(3):
                        p = posm[0:TR, t, bass.ds(j2, 2)] if not isinstance(j2, int) else posm[0:TR, t, j2:j2 + 2]
                        last = V.tensor_tensor(slotsel[0:TR, t], iota, over(p, CAP), ALU.is_equal)
                    last.then_inc(S["sel"], 1)

                def take_slots(jj, count):
                    dve.wait_ge(S["slot_mm"], count)
                    V.tensor_copy(idxf[:, jj:jj + 1], psum[:, 4, 0:1])
                    V.tensor_copy(wt[0:64, jj:jj + 1], psum[0:64, 4, 2:3])
                    V.tensor_copy(wt[64:128, jj:jj + 1], psum[64:128, 4, 3:4]).then_inc(S["idxf"], 1)
                    dve.wait_ge(S["idxf"], count)
                    V.tensor_copy(slot_idx[:, jj:jj + 1], idxf[:, jj:jj + 1])
                    V.tensor_scalar(selT[jj], K[:, C_IOTA:C_IOTA + T], idxf[:, jj:jj + 1], None, ALU.is_equal).then_inc(S["idx"], 1)

                def add_back(base, tiles=range(DT)):
                    for c in tiles:
                        dve.wait_ge(S["cb_mm"], base + (c + 1))
                        V.tensor_tensor(yacc[:, c, :], yacc[:, c, :], psum[:, 6 + c % 2, 0:T], ALU.add).then_inc(S["cb_add"], 1)

                choose(0)
                dve.wait_ge(S["sh_act"], l + 1)
                dve.wait_ge(S["sh_mm"], 2 * l + 2)
                V.tensor_tensor(shid, ssil, psum[:, 6:8, 0:T], ALU.mult).then_inc(S["sh_hid"], 1)
                take_slots(0, first * SEL_R + 1)
                choose(2)
                take_slots(1, first * SEL_R + 2)
                dve.wait_ge(S["shd_sb"], 8 * l + 8)
                with dve.Fori(first, end) as r:
                    with dve.Fori(0, NTURN) as i:
                        for b in range(EBODY):
                            done1 = r * NPAIR + i * EBODY + (b + 1)
                            used0 = r * RU + i * (EBODY * PU) + b * PU
                            choose(i * 8 + (2 * b + 4))
                            take_slots((b + 2) % 4, r * SEL_R + i * EBODY + (b + 3))
                            dve.wait_ge(S["cb_add"], r * CB_R + i * 32 + 8 * b + ONE)
                            add_back(r * CB_R + i * 32 + 8 * b, range(3))
                            dve.wait_ge(S["gsil"], done1 + ONE)
                            dve.wait_ge(S["unit_used"], used0 + 4 + ONE)
                            dve.wait_ge(S["ht_mm"], done1 - 1 + ONE)
                            V.scalar_tensor_tensor(ghid, gsil, wt[:, b:b + 1], psum[:, 1, 0:DE], ALU.mult, ALU.mult).then_inc(S["ghid"], 1)
                            add_back(r * CB_R + i * 32 + 8 * b, range(3, DT))
                            dve.wait_ge(S["unit_used"], used0 + 6 + ONE)
                            V.tensor_copy(gout[:, 512:D], psum[:, 3, :]).then_inc(S["os_b"], 1)
                    dve.wait_ge(S["cb_add"], r * CB_R + DT * NPAIR + ONE)
                    add_back(r * CB_R + DT * NPAIR)
                    dve.wait_ge(S["cb_add"], r * CB_R + CB_R + ONE)
                    V.memset(selT[3], 0.0)
                    V.tensor_scalar(posm[0:TR, :, :], posm[0:TR, :, :], -float(CAP), None, ALU.add).then_inc(S["next"], 1)
                    with dve.If(r + 1 < end):
                        dve.wait_ge(S["next"], r + 1)
                        for j in range(2):
                            choose(2 * j)
                            take_slots(j, (r + 1) * SEL_R + (j + 1))

            post(1, 0, 0, yacc, ("out_sb", 0))
            pre(2, 0, 1)
            moe(0)
            post(3, 0, 1, yacc)
            pre(4, 1, 0)
            vz, uz = z[:, 8:16, :], z[:, 0:8, :]
            dve.wait_ge(S["ws_tr"], 1)
            V.tensor_tensor(wsT.rearrange("p (a g) n -> p a g n", a=2), psum[:, 4:6, :].rearrange("p a (g n) -> p a g n", g=4),
                            upi_full.unsqueeze(1).unsqueeze(1).broadcast_to([P, 2, 4, P]), ALU.mult).then_inc(S["ws_sb"], 1)
            dve.wait_ge(S["z_sb1"], 8)
            dve.wait_ge(S["vmu_mm"], 1)
            v(V.tensor_scalar(mu_b, psum[:, 6, 0:T], 1.0 / D, None, ALU.mult))
            v(V.tensor_tensor(vz, vz, mu_b.unsqueeze(1).broadcast_to([P, 8, T]), ALU.subtract))
            for g in range(DT):
                V.scalar_tensor_tensor(gt1[:, g], vz[:, g], 1.0 / D, vz[:, g], ALU.mult, ALU.mult).then_inc(S["vc_ready"], 1)
            dve.wait_ge(S["vvar_mm"], 1)
            dve.wait_ge(S["ln_sd"], 1)
            v(V.reciprocal(rstd[:, :], rstd[:, :]))
            v(V.tensor_tensor(vz, vz, wide(), ALU.mult))
            for g in range(8):
                last = V.tensor_scalar(vz[:, g], vz[:, g], ln_g[:, g:g + 1], ln_b[:, g:g + 1], ALU.mult, ALU.add)
            last.then_inc(S["v_ready"], 1)
            dve.wait_ge(S["v_ready"], 1)
            dve.wait_ge(S["gmisc_in"], 32)
            for g in range(8):
                last = V.tensor_scalar(gt2[:, g, NPR:T], vz[:, g, NPR:T], ws00[:, g:g + 1], bsb[:, g, 0:1], ALU.mult, ALU.add)
            v(last)
            for t in range(2):
                dve.wait_ge(S["sg_mm"], t + 1)
                for a in range(2):
                    v(V.tensor_tensor(gt2[:, 4 * a:4 * a + 4, t * P:(t + 1) * P],
                                      psum[:, 2 + 2 * t + a, :].rearrange("p (g n) -> p g n", g=4), bsb[:, 4 * a:4 * a + 4, :], ALU.add))
            for g in range(DT):
                dve.wait_ge(S["z_sb1"], 8 + g + 1)
                V.tensor_tensor(uz[:, g], uz[:, g], gt2[:, g], ALU.mult).then_inc(S["sg_ready"], 1)
            post(5, 1, 0, gt1, ("out_sb", 8))
            pre(6, 1, 1)
            moe(1)
            post(7, 1, 1, yacc)


_INS = ['x_prompt', 'x_sample', 'c_prompt', 'c_sample', 'state_conv', 'state_shift', 'state_wkv', 'w_mod', 'b_mod', 'norm_g',
        'ab_w_in', 'ab_conv_w', 'ab_mu', 'ab_w0', 'ab_w_decay_up', 'ab_a0', 'ab_a_up', 'ab_g_up', 'ab_k_k', 'ab_k_a', 'ab_r_k',
        'ab_gn_g', 'ab_gn_b', 'ab_w_out', 'gm_w_in', 'gm_b_in', 'gm_ln_g', 'gm_ln_b', 'gm_w_s', 'gm_b_s', 'gm_w_out',
        'moe_w_router', 'moe_b_router', 'moe_w_gate', 'moe_w_up', 'moe_w_down', 'moe_ws_gate', 'moe_ws_up', 'moe_ws_down']
_OUTS = [(1, NPR, D), (NSA, 1, D), (1, 1, 2, DA), (1, NSA, 2, DA), (1, 1, PB), (1, NSA, PB), (1, 1, H, HD, HD), (1, NSA, H, HD, HD), (1, NSA, 1, D)]


def kernel(**inputs):
    import concourse.bacc as _bacc
    from concourse.bass_utils import run_bass_kernel_spmd as _run

    nc = _bacc.Bacc("TRN2", target_bir_lowering=False, num_devices=1)
    arrays, ins, outs = {}, [], []
    for name in _INS:
        a = np.ascontiguousarray(inputs[name])
        arrays[f"in_{name}"] = a
        ins.append(nc.dram_tensor(f"in_{name}", a.shape, F32, kind="ExternalInput").ap())
    arrays["shape_constants"] = shape_constants()
    ins.append(nc.dram_tensor("shape_constants", (P, NCONST), F32, kind="ExternalInput").ap())
    for i, shape in enumerate(_OUTS):
        outs.append(nc.dram_tensor(f"out_{i}_dram", shape, F32, kind="ExternalOutput").ap())
    build(nc, ins, outs)
    r = _run(nc, [arrays], core_ids=[0])
    return tuple(r.results[0][f"out_{i}_dram"] for i in range(len(_OUTS)))
```
